# Optimizing a Trainium2 kernel written in Bass

```python
import jax, jax.numpy as jnp
from jax import lax
import numpy as np
import math

D_MODEL = 1024
BATCH = 1
SEQ = 512
DEPTH = 1

POOL_WIDTH = D_MODEL // 2
POOL_WINDOWS = (2, 4, 8, 16)
N_POOL_GROUPS = len(POOL_WINDOWS)
POOL_GROUP = POOL_WIDTH // N_POOL_GROUPS
N_HEADS = 8
HEAD_DIM = 64
ATTN_WIDTH = N_HEADS * HEAD_DIM
MOBA_BLOCK = 256
MOBA_TOPK = 3
Q_CHUNK = 32
D_FF = 4 * D_MODEL
N_BRANCHES = 2
IN_WIDTH = POOL_WIDTH + 3 * ATTN_WIDTH + N_BRANCHES * D_MODEL
EPS = 1e-6
NEG = -1e30


def rmsnorm(x, g):
    xf = x.astype(jnp.float32)
    y = xf * lax.rsqrt(jnp.mean(xf * xf, axis=-1, keepdims=True) + EPS) * g.astype(jnp.float32)
    return y.astype(x.dtype)

def alibi_slopes(n_heads):
    return jnp.asarray(2.0 ** (-8.0 * np.arange(1, n_heads + 1) / n_heads), dtype=jnp.float32)

def pool_mixer(p, pool_w, pool_scale):
    pf = p.astype(jnp.float32)
    B, S, _ = pf.shape
    cs = jnp.concatenate([jnp.zeros_like(pf[:, :1]), jnp.cumsum(pf, axis=1)], axis=1)
    t = jnp.arange(S)
    outs = []
    for g, w in enumerate(POOL_WINDOWS):
        sl = slice(g * POOL_GROUP, (g + 1) * POOL_GROUP)
        lo = jnp.maximum(t + 1 - w, 0)
        win_sum = cs[:, 1:, sl] - cs[:, lo, sl]
        count = jnp.minimum(t + 1, w).astype(jnp.float32)[None, :, None]
        outs.append(win_sum / count - pf[:, :, sl])
    y = jnp.stack(outs, axis=2)
    y = jnp.einsum('bsgc,gcd->bsgd', y, pool_w.astype(jnp.float32))
    y = y.reshape(B, S, POOL_WIDTH) * pool_scale.astype(jnp.float32)
    return y.astype(p.dtype)

def moba_attention(q, k, v):
    B, S, H, Dh = q.shape
    nb = -(-S // MOBA_BLOCK)
    s_pad = nb * MOBA_BLOCK
    qf = q.transpose(0, 2, 1, 3).astype(jnp.float32) * (HEAD_DIM ** -0.5)
    pad = ((0, 0), (0, 0), (0, s_pad - S), (0, 0))
    kf = jnp.pad(k.transpose(0, 2, 1, 3).astype(jnp.float32), pad)
    vf = jnp.pad(v.transpose(0, 2, 1, 3).astype(jnp.float32), pad)
    kb = kf.reshape(B, H, nb, MOBA_BLOCK, Dh)
    vb = vf.reshape(B, H, nb, MOBA_BLOCK, Dh)
    slope = alibi_slopes(H)[None, :, None, None]
    t = jnp.arange(S)
    qblk = t // MOBA_BLOCK
    k_sel = min(MOBA_TOPK, nb - 1)
    if k_sel > 0:
        kmean = jnp.mean(kb, axis=3)
        gate = jnp.einsum('bhsd,bhnd->bhsn', qf, kmean)
        past = jnp.arange(nb)[None, :] < qblk[:, None]
        gate = jnp.where(past[None, None], gate, NEG)
        _, sel = lax.top_k(gate, k_sel)
    else:
        sel = jnp.zeros((B, H, S, 0), dtype=jnp.int32)
    n_chunks = S // Q_CHUNK
    q_c = qf.reshape(B, H, n_chunks, Q_CHUNK, Dh).transpose(2, 0, 1, 3, 4)
    sel_c = sel.reshape(B, H, n_chunks, Q_CHUNK, k_sel).transpose(2, 0, 1, 3, 4)
    bi = jnp.arange(B)[:, None, None]
    hi = jnp.arange(H)[None, :, None]
    kpos_in = jnp.arange(MOBA_BLOCK)

    def chunk_attn(args):
        c, qc, selc = args
        tq = c * Q_CHUNK + jnp.arange(Q_CHUNK)
        own = (c * Q_CHUNK) // MOBA_BLOCK
        k_own = lax.dynamic_slice_in_dim(kf, own * MOBA_BLOCK, MOBA_BLOCK, axis=2)
        v_own = lax.dynamic_slice_in_dim(vf, own * MOBA_BLOCK, MOBA_BLOCK, axis=2)
        ks = own * MOBA_BLOCK + kpos_in
        dist = (tq[:, None] - ks[None, :]).astype(jnp.float32)
        s_own = jnp.einsum('bhqd,bhkd->bhqk', qc, k_own) - slope * dist[None, None]
        s_own = jnp.where((ks[None, :] <= tq[:, None])[None, None], s_own, NEG)
        scores = [s_own]
        idxs = []
        for j in range(k_sel):
            idx = selc[..., j]
            kg = kb[bi, hi, idx]
            kpos = idx[..., None] * MOBA_BLOCK + kpos_in
            d = (tq[None, None, :, None] - kpos).astype(jnp.float32)
            s = jnp.einsum('bhqd,bhqkd->bhqk', qc, kg) - slope * d
            s = jnp.where((idx < own)[..., None], s, NEG)
            scores.append(s)
            idxs.append(idx)
        p = jax.nn.softmax(jnp.concatenate(scores, axis=-1), axis=-1)
        out = jnp.einsum('bhqk,bhkd->bhqd', p[..., :MOBA_BLOCK], v_own)
        for j, idx in enumerate(idxs):
            vg = vb[bi, hi, idx]
            pj = p[..., (j + 1) * MOBA_BLOCK:(j + 2) * MOBA_BLOCK]
            out = out + jnp.einsum('bhqk,bhqkd->bhqd', pj, vg)
        return out

    out = lax.map(chunk_attn, (jnp.arange(n_chunks), q_c, sel_c))
    out = out.transpose(1, 0, 3, 2, 4).reshape(B, S, H * Dh)
    return out.astype(q.dtype)

def first_inputs(seed: int = 0) -> dict:
    key = jax.random.key(seed)
    ks = jax.random.split(key, 16)
    f32 = jnp.float32

    def nrm(k, shape, fan_in):
        return jax.random.normal(k, shape, f32) * (fan_in ** -0.5)

    def gain(k, shape):
        return 1.0 + 0.02 * jax.random.normal(k, shape, f32)

    L = DEPTH
    return {
        "x": jax.random.normal(ks[0], (BATCH, SEQ, D_MODEL), f32),
        "norm_mix_pre": gain(ks[1], (L, D_MODEL)),
        "w_in": nrm(ks[2], (L, D_MODEL, IN_WIDTH), D_MODEL),
        "b_gate": 0.01 * jax.random.normal(ks[3], (L, N_BRANCHES * D_MODEL), f32),
        "pool_w": nrm(ks[4], (L, N_POOL_GROUPS, POOL_GROUP, POOL_GROUP), POOL_GROUP),
        "pool_scale": gain(ks[5], (L, POOL_WIDTH)),
        "w_branch_pool": nrm(ks[6], (L, POOL_WIDTH, D_MODEL), POOL_WIDTH),
        "w_branch_attn": nrm(ks[7], (L, ATTN_WIDTH, D_MODEL), ATTN_WIDTH),
        "w_out": nrm(ks[8], (L, D_MODEL, D_MODEL), D_MODEL),
        "norm_mix_post": gain(ks[9], (L, D_MODEL)),
        "norm_mlp_pre": gain(ks[10], (L, D_MODEL)),
        "w_up": nrm(ks[11], (L, D_MODEL, D_FF), D_MODEL),
        "w_down": nrm(ks[12], (L, D_FF, D_MODEL), D_FF),
        "norm_mlp_post": gain(ks[13], (L, D_MODEL)),
    }

def first_block(x, norm_mix_pre, w_in, b_gate, pool_w, pool_scale, w_branch_pool, w_branch_attn, w_out,
              norm_mix_post, norm_mlp_pre, w_up, w_down, norm_mlp_post):
    B, S, _ = x.shape
    h = x
    o_q = POOL_WIDTH
    o_k = o_q + ATTN_WIDTH
    o_v = o_k + ATTN_WIDTH
    o_g = o_v + ATTN_WIDTH
    for l in range(DEPTH):
        u = rmsnorm(h, norm_mix_pre[l])
        z = u @ w_in[l]
        p = z[..., :o_q]
        q = z[..., o_q:o_k].reshape(B, S, N_HEADS, HEAD_DIM)
        k = z[..., o_k:o_v].reshape(B, S, N_HEADS, HEAD_DIM)
        v = z[..., o_v:o_g].reshape(B, S, N_HEADS, HEAD_DIM)
        g = z[..., o_g:] + b_gate[l]
        g_pool, g_attn = g[..., :D_MODEL], g[..., D_MODEL:]
        y_pool = pool_mixer(p, pool_w[l], pool_scale[l]) @ w_branch_pool[l]
        y_attn = moba_attention(q, k, v) @ w_branch_attn[l]
        m = jax.nn.sigmoid(g_pool) * y_pool + jax.nn.sigmoid(g_attn) * y_attn
        h = h + rmsnorm(m @ w_out[l], norm_mix_post[l])
        u2 = rmsnorm(h, norm_mlp_pre[l])
        a = jnp.square(jax.nn.relu(u2 @ w_up[l]))
        h = h + rmsnorm(a @ w_down[l], norm_mlp_post[l])
    return h


CHUNK = 64
D_CONV = D_MODEL
CONV_WIDTH = 31
SSM_EXPAND = 2
D_INNER = SSM_EXPAND * D_MODEL
N_SSM_HEADS = D_INNER // HEAD_DIM
D_STATE = 128
N_GROUPS = 4
SSM_CONV_WIDTH = 4
D_XBC = D_INNER + 2 * N_GROUPS * D_STATE
D_FF_2 = ((8 * D_MODEL // 3 + 255) // 256) * 256
IN_COLS = 2 * D_CONV + D_INNER + D_XBC + N_SSM_HEADS + 2 * D_MODEL
NORM_EPS = 1e-6
LN_EPS = 1e-5


def rms_norm(x, w, eps=NORM_EPS):
    xf = x.astype(jnp.float32)
    y = xf * lax.rsqrt(jnp.mean(xf * xf, axis=-1, keepdims=True) + eps)
    return (y * w.astype(jnp.float32)).astype(x.dtype)

def layer_norm(x, w, b, eps=LN_EPS):
    xf = x.astype(jnp.float32)
    mu = jnp.mean(xf, axis=-1, keepdims=True)
    var = jnp.mean(jnp.square(xf - mu), axis=-1, keepdims=True)
    y = (xf - mu) * lax.rsqrt(var + eps)
    return (y * w.astype(jnp.float32) + b.astype(jnp.float32)).astype(x.dtype)

def causal_depthwise_conv(u, w, b):
    k, ch = w.shape
    out = lax.conv_general_dilated(
        u, w[:, None, :].astype(u.dtype), window_strides=(1,), padding=[(k - 1, 0)],
        dimension_numbers=("NWC", "WIO", "NWC"), feature_group_count=ch)
    return out + b.astype(u.dtype)

def adaln(c, w, b):
    mod = jax.nn.silu(c) @ w + b
    shift, scale, gate = jnp.split(mod, 3, axis=-1)
    return shift[:, None, :], scale[:, None, :], gate[:, None, :]

def ssd_chunked_scan(xs, dt, a, bm, cm):
    b, L, H, P = xs.shape
    G, N = bm.shape[2], bm.shape[3]
    J = H // G
    nc = L // CHUNK

    def to_chunks(t):
        return jnp.moveaxis(t.reshape(b, nc, CHUNK, *t.shape[2:]), 1, 0)

    xdt = (xs * dt[..., None]).reshape(b, L, G, J, P)
    da = (dt * a).reshape(b, L, G, J)
    xc, ac, bc, cc = to_chunks(xdt), to_chunks(da), to_chunks(bm), to_chunks(cm)
    causal = jnp.tril(jnp.ones((CHUNK, CHUNK), dtype=bool))[None, :, :, None, None]

    def step(state, inp):
        xk, ak, bk, ck = inp
        acs = jnp.cumsum(ak, axis=1)
        seg = acs[:, :, None] - acs[:, None, :]
        decay = jnp.exp(jnp.where(causal, seg, -jnp.inf))
        cb = jnp.einsum("blgn,bsgn->blsg", ck, bk)
        y_diag = jnp.einsum("blsg,blsgj,bsgjp->blgjp", cb, decay, xk)
        y_off = jnp.einsum("blgn,bgjpn,blgj->blgjp", ck, state, jnp.exp(acs))
        last = acs[:, -1]
        w_in = jnp.exp(last[:, None] - acs)
        new_state = state * jnp.exp(last)[..., None, None] + jnp.einsum(
            "bsgn,bsgj,bsgjp->bgjpn", bk, w_in, xk)
        return new_state, y_diag + y_off

    init = jnp.zeros((b, G, J, P, N), jnp.float32)
    _, ys = lax.scan(step, init, (xc, ac, bc, cc))
    return jnp.moveaxis(ys, 0, 1).reshape(b, L, H, P)

def mixer_sublayer(h, w_in, conv_dw_w, conv_dw_b, conv_ln_w, conv_ln_b, w_conv_out,
                   ssm_conv_w, ssm_conv_b, dt_bias, a_log, d_skip, ssm_norm_w, w_ssm_out, w_out):
    b, L, _ = h.shape
    proj = h @ w_in
    splits = np.cumsum([2 * D_CONV, D_INNER, D_XBC, N_SSM_HEADS, D_MODEL]).tolist()
    conv_in, z, xbc, dt_raw, g_conv, g_ssm = jnp.split(proj, splits, axis=-1)

    a_half, b_half = jnp.split(conv_in, 2, axis=-1)
    u = a_half * jax.nn.sigmoid(b_half)
    u = causal_depthwise_conv(u, conv_dw_w, conv_dw_b)
    u = jax.nn.silu(layer_norm(u, conv_ln_w, conv_ln_b))
    y_conv = u @ w_conv_out

    xbc = jax.nn.silu(causal_depthwise_conv(xbc, ssm_conv_w, ssm_conv_b))
    xs, bm, cm = jnp.split(xbc, [D_INNER, D_INNER + N_GROUPS * D_STATE], axis=-1)
    xs_f = xs.astype(jnp.float32).reshape(b, L, N_SSM_HEADS, HEAD_DIM)
    bm_f = bm.astype(jnp.float32).reshape(b, L, N_GROUPS, D_STATE)
    cm_f = cm.astype(jnp.float32).reshape(b, L, N_GROUPS, D_STATE)
    dt = jax.nn.softplus(dt_raw.astype(jnp.float32) + dt_bias.astype(jnp.float32))
    a = -jnp.exp(a_log.astype(jnp.float32))
    y = ssd_chunked_scan(xs_f, dt, a, bm_f, cm_f) + d_skip.astype(jnp.float32)[:, None] * xs_f
    y = y.reshape(b, L, D_INNER) * jax.nn.silu(z.astype(jnp.float32))
    yg = y.reshape(b, L, N_GROUPS, D_INNER // N_GROUPS)
    yg = yg * lax.rsqrt(jnp.mean(yg * yg, axis=-1, keepdims=True) + NORM_EPS)
    y = (yg.reshape(b, L, D_INNER) * ssm_norm_w.astype(jnp.float32)).astype(h.dtype)
    y_ssm = y @ w_ssm_out

    merged = jax.nn.sigmoid(g_conv) * y_conv + jax.nn.sigmoid(g_ssm) * y_ssm
    return merged @ w_out

def ffn_sublayer(h, w_ffn_in, w_ffn_down):
    gate, up = jnp.split(h @ w_ffn_in, 2, axis=-1)
    return (jax.nn.silu(gate) * up) @ w_ffn_down

def second_inputs(seed: int = 0) -> dict:
    key = jax.random.key(seed)
    ks = jax.random.split(key, 32)
    f32 = jnp.float32
    nrm = lambda k, shape, s: jax.random.normal(k, shape, f32) * s
    gain = lambda k, shape: 1.0 + 0.05 * jax.random.normal(k, shape, f32)
    Ld = DEPTH
    u_dt = jax.random.uniform(ks[13], (Ld, N_SSM_HEADS), f32)
    dt0 = jnp.exp(u_dt * (math.log(0.1) - math.log(0.001)) + math.log(0.001))
    dt_bias = dt0 + jnp.log(-jnp.expm1(-dt0))
    a_log = jnp.log(jax.random.uniform(ks[14], (Ld, N_SSM_HEADS), f32, 1.0, 16.0))
    return {
        "x": jax.random.normal(ks[0], (BATCH, SEQ, D_MODEL), f32),
        "c": jax.random.normal(ks[1], (BATCH, D_MODEL), f32),
        "w_ada_mix": nrm(ks[2], (Ld, D_MODEL, 3 * D_MODEL), D_MODEL ** -0.5),
        "b_ada_mix": nrm(ks[3], (Ld, 3 * D_MODEL), 0.01),
        "norm_mix_w": gain(ks[4], (Ld, D_MODEL)),
        "w_in": nrm(ks[5], (Ld, D_MODEL, IN_COLS), D_MODEL ** -0.5),
        "conv_dw_w": nrm(ks[6], (Ld, CONV_WIDTH, D_CONV), CONV_WIDTH ** -0.5),
        "conv_dw_b": nrm(ks[7], (Ld, D_CONV), 0.01),
        "conv_ln_w": gain(ks[8], (Ld, D_CONV)),
        "conv_ln_b": nrm(ks[9], (Ld, D_CONV), 0.01),
        "w_conv_out": nrm(ks[10], (Ld, D_CONV, D_MODEL), D_CONV ** -0.5),
        "ssm_conv_w": nrm(ks[11], (Ld, SSM_CONV_WIDTH, D_XBC), SSM_CONV_WIDTH ** -0.5),
        "ssm_conv_b": nrm(ks[12], (Ld, D_XBC), 0.01),
        "dt_bias": dt_bias,
        "a_log": a_log,
        "d_skip": gain(ks[15], (Ld, N_SSM_HEADS)),
        "ssm_norm_w": gain(ks[16], (Ld, D_INNER)),
        "w_ssm_out": nrm(ks[17], (Ld, D_INNER, D_MODEL), D_INNER ** -0.5),
        "w_out": nrm(ks[18], (Ld, D_MODEL, D_MODEL), D_MODEL ** -0.5),
        "w_ada_ffn": nrm(ks[19], (Ld, D_MODEL, 3 * D_MODEL), D_MODEL ** -0.5),
        "b_ada_ffn": nrm(ks[20], (Ld, 3 * D_MODEL), 0.01),
        "norm_ffn_w": gain(ks[21], (Ld, D_MODEL)),
        "w_ffn_in": nrm(ks[22], (Ld, D_MODEL, 2 * D_FF_2), D_MODEL ** -0.5),
        "w_ffn_down": nrm(ks[23], (Ld, D_FF_2, D_MODEL), D_FF_2 ** -0.5),
        "final_norm_w": gain(ks[24], (D_MODEL,)),
    }

def second_block(x, c, w_ada_mix, b_ada_mix, norm_mix_w, w_in, conv_dw_w, conv_dw_b, conv_ln_w,
              conv_ln_b, w_conv_out, ssm_conv_w, ssm_conv_b, dt_bias, a_log, d_skip, ssm_norm_w,
              w_ssm_out, w_out, w_ada_ffn, b_ada_ffn, norm_ffn_w, w_ffn_in, w_ffn_down,
              final_norm_w):
    for i in range(DEPTH):
        shift, scale, gate = adaln(c, w_ada_mix[i], b_ada_mix[i])
        h = rms_norm(x, norm_mix_w[i]) * (1.0 + scale) + shift
        x = x + gate * mixer_sublayer(
            h, w_in[i], conv_dw_w[i], conv_dw_b[i], conv_ln_w[i], conv_ln_b[i], w_conv_out[i],
            ssm_conv_w[i], ssm_conv_b[i], dt_bias[i], a_log[i], d_skip[i], ssm_norm_w[i],
            w_ssm_out[i], w_out[i])
        shift, scale, gate = adaln(c, w_ada_ffn[i], b_ada_ffn[i])
        h = rms_norm(x, norm_ffn_w[i]) * (1.0 + scale) + shift
        x = x + gate * ffn_sublayer(h, w_ffn_in[i], w_ffn_down[i])
    return rms_norm(x, final_norm_w)


def setup_inputs(seed=0):
    out = dict(first_inputs(seed))
    for name, value in second_inputs(seed + 1).items():
        if name != "x":
            out[name + "_2"] = value
    return out


def reference(
    x, norm_mix_pre, w_in, b_gate, pool_w, pool_scale, w_branch_pool, w_branch_attn, w_out,
    norm_mix_post, norm_mlp_pre, w_up, w_down, norm_mlp_post, c_2, w_ada_mix_2, b_ada_mix_2,
    norm_mix_w_2, w_in_2, conv_dw_w_2, conv_dw_b_2, conv_ln_w_2, conv_ln_b_2, w_conv_out_2,
    ssm_conv_w_2, ssm_conv_b_2, dt_bias_2, a_log_2, d_skip_2, ssm_norm_w_2, w_ssm_out_2,
    w_out_2, w_ada_ffn_2, b_ada_ffn_2, norm_ffn_w_2, w_ffn_in_2, w_ffn_down_2, final_norm_w_2,
):
    x = first_block(
        x, norm_mix_pre, w_in, b_gate, pool_w, pool_scale, w_branch_pool, w_branch_attn, w_out,
        norm_mix_post, norm_mlp_pre, w_up, w_down, norm_mlp_post,
    )
    return second_block(
        x, c_2, w_ada_mix_2, b_ada_mix_2, norm_mix_w_2, w_in_2, conv_dw_w_2, conv_dw_b_2,
        conv_ln_w_2, conv_ln_b_2, w_conv_out_2, ssm_conv_w_2, ssm_conv_b_2, dt_bias_2, a_log_2,
        d_skip_2, ssm_norm_w_2, w_ssm_out_2, w_out_2, w_ada_ffn_2, b_ada_ffn_2, norm_ffn_w_2,
        w_ffn_in_2, w_ffn_down_2, final_norm_w_2,
    )


_drawn_inputs = setup_inputs


def setup_inputs(seed=0):
    import zlib

    import numpy as np

    out = dict(_drawn_inputs(seed))
    spreads = {}
    factors = {'norm_mix_pre': 2.92,
     'b_gate': 8.0,
     'pool_scale': 3.743,
     'norm_mix_post': 3.606,
     'norm_mlp_pre': 4.129,
     'norm_mlp_post': 12.375,
     'b_ada_mix_2': 8.0,
     'norm_mix_w_2': 3.515,
     'conv_dw_b_2': 42.42,
     'conv_ln_w_2': 24.13,
     'conv_ln_b_2': 200.0,
     'ssm_conv_b_2': 59.146,
     'd_skip_2': 200.0,
     'ssm_norm_w_2': 18.254,
     'b_ada_ffn_2': 24.077,
     'norm_ffn_w_2': 8.0}
    for name, (base, spread) in spreads.items():
        noise = np.random.default_rng([zlib.crc32(name.encode()), seed]).standard_normal(out[name].shape)
        drawn = base * np.exp(spread * noise) if base else spread * noise
        out[name] = __import__('jax').numpy.asarray(drawn.astype(out[name].dtype))
    for name, factor in factors.items():
        out[name] = (out[name] * factor).astype(out[name].dtype)
    return out
```

```python
from contextlib import ExitStack

import numpy as np

import concourse.bass as bass
from concourse import mybir

F32 = mybir.dt.float32
F32R = mybir.dt.float32r
ACT = mybir.ActivationFunctionType
ALU = mybir.AluOpType
AX = mybir.AxisListType

P = 128
S = 512
D = 1024
KC = D // P
EPS = 1e-6
HEAD = 64
HEADS = 8
QT = S // P
PANEL = 16 * P
MASKED = 1e33

GROUPS = 4
GH = 8
SSM_HEADS = GROUPS * GH
CONV_TAPS = 31
SSM_TAPS = 4
FFN_GROUPS = 2
FC = 11
ADA_PIECES = 8
ADA_COLS = 12 * P
LN_EPS = 1e-5

PAIRS = 4
P_PAIR = 0
P_BRANCH = P_PAIR + 4 * PAIRS
P_WOUT = P_BRANCH + 4
P_MLP = P_WOUT + 4
MLP_GROUPS = 4
P_DT = P_MLP + MLP_GROUPS * 8
P_GRP = P_DT + 1
P_CONV = P_GRP + 8 * GROUPS
P_GSSM = P_CONV + 4
P_SSM = P_GSSM + 4
P_WOUT2 = P_SSM + 8
P_FFN = P_WOUT2 + 4
P_END = P_FFN + FFN_GROUPS * (FC + 8)
T_PAIR = 0
T_BRANCH = T_PAIR + 8 * PAIRS
T_WOUT = T_BRANCH + 16
T_MLP = T_WOUT + 8
T_DT = T_MLP + MLP_GROUPS * 16
T_GRP = T_DT + 1
T_CONV = T_GRP + 16 * GROUPS
T_GSSM = T_CONV + 8
T_SSM = T_GSSM + 8
T_WOUT2 = T_SSM + 16
T_FFN = T_WOUT2 + 8
T_END = T_FFN + FFN_GROUPS * (2 * FC + 8)

G_CONV_W, G_CONV_B = 0, 2 * CONV_TAPS
G_SSM_W = G_CONV_B + 2
G_SSM_B = G_SSM_W + 6 * SSM_TAPS
G_D = G_SSM_B + 6
GCOLS = G_D + 4

COLS = {}


def _cols():
    at = 0
    for name, n in [("norm_mix_pre", 8), ("b_gate", 16), ("pool_scale", 4), ("norm_mix_post", 8),
                    ("norm_mlp_pre", 8), ("norm_mlp_post", 8), ("b_ada", 48), ("norm_mix_w", 8),
                    ("norm_ffn_w", 8), ("final_norm_w", 8), ("conv_ln_w", 8), ("conv_ln_b", 8), ("ssm_norm_w", 16),
                    ("c", 8), ("dt_bias", 1), ("a_log", 1), ("group", GCOLS * GROUPS)]:
        COLS[name] = at
        at += n
    return at


NCOL = _cols()


def build(nc, x_in, w_in, cols_in, poolw_in, ada_in, out):
    A_USE_SSM = 4 * KC
    A_USE_FFN = A_USE_SSM + KC
    B_USE_CONV = KC + MLP_GROUPS * KC
    B_USE_SSM = B_USE_CONV + KC
    B_USE_WOUT = B_USE_SSM + KC

    with ExitStack() as ctx:
        def sb(name, shape, dt=F32):
            return ctx.enter_context(nc.sbuf_tensor(name, shape, dt))

        def sem(name):
            return ctx.enter_context(nc.semaphore(name))

        gemm_bank = [ctx.enter_context(nc.psum_tensor(f"gemm_bank{b}", [P, S], F32)) for b in range(4)]
        aux = [ctx.enter_context(nc.psum_tensor(f"aux_bank{b}", [P, S], F32)) for b in range(4)]

        raw = [sb(f"w_raw{s}", [P, PANEL]) for s in range(2)]
        whi = [sb(f"w_hi{s}", [P, PANEL], F32R) for s in range(2)]
        wlo = [sb(f"w_lo{s}", [P, PANEL], F32R) for s in range(2)]
        h = sb("h", [P, KC, S])
        a_hi = sb("a_hi", [P, KC, S], F32R)
        a_lo = sb("a_lo", [P, KC, S], F32R)
        CHUNK = S * 4
        b_at = nc.sbuf_base
        scratch = sb("scratch", [P, 16, S])
        b_hi = nc.alloc_sbuf_tensor_at("b_hi", [P, KC, S], F32R, offset=b_at)
        b_lo = nc.alloc_sbuf_tensor_at("b_lo", [P, KC, S], F32R, offset=b_at + KC * CHUNK)
        arena_at = nc.sbuf_base
        arena = sb("arena", [P, 32, S])
        f_hi = nc.alloc_sbuf_tensor_at("f_hi", [P, FC, S], F32R, offset=arena_at)
        f_lo = nc.alloc_sbuf_tensor_at("f_lo", [P, FC, S], F32R, offset=arena_at + FC * CHUNK)
        ada_w = [arena[:, 20 + 3 * s:23 + 3 * s, :].rearrange("p a n -> p (a n)") for s in range(2)]
        ada_acc = arena[:, 26:29, :].rearrange("p a n -> p (a n)")
        conv_u = arena[:, 0:8, :]
        y_ssm = arena[:, 8:24, :]
        g_conv = arena[:, 24:32, :]
        g_ssm = arena[:, 0:8, :]
        ssm_out = arena[:, 16:24, :]
        ffn_t = [arena[:, 22 + s, :] for s in range(2)]
        ffn_raw = [arena[:, 24 + s, :] for s in range(2)]
        e_row = [scratch[:, 0 + s, :] for s in range(2)]
        x_dt = scratch[:, 2:6, :]
        state = scratch[:, 6:9, :]
        cb = scratch[:, 9, :]
        b_t = scratch[:, 10, :]
        c_t = scratch[:, 11, :]
        b_n = scratch[:, 12, :]
        u_buf = scratch[:, 13:15, :]
        gates = arena[:, 0:16, :]
        y = arena[:, 0:8, :]
        pool_x = arena[:, 16:20, :]
        probs = arena[:, 20:24, :]
        probs_t = arena[:, 24:28, :]
        y_attn = arena[:, 20:28, :]
        q_s = arena[:, 28, :]
        k_s = arena[:, 29, :]
        v_s = arena[:, 30, :]
        v_n = arena[:, 31, :]
        win = [arena[:, 28, :], arena[:, 29, :]]
        relu = [arena[:, 16 + s, :] for s in range(2)]
        act_raw = [arena[:, 18 + s, :] for s in range(2)]
        tmp = sb("tmp", [P, 2, S])
        acc31 = sb("acc31", [P, 2, S])
        seg1 = sb("seg1", [P, S])
        seg = [scratch[:, 15, :], seg1[:, :]]
        x_win = [seg[0], seg[1], state[:, 2, :]]
        dt_x, dt_e, dt_s, dt_q, dt_p = [scratch[0:SSM_HEADS, c, :] for c in range(5)]
        dt_row = scratch[0:SSM_HEADS, 5, :]
        cum = sb("cum", [SSM_HEADS, S])
        cum_t = sb("cum_t", [P, QT * SSM_HEADS])
        dt_t = sb("dt_t", [P, QT * SSM_HEADS])
        win_t = sb("win_t", [P, QT * SSM_HEADS])
        dec_t = sb("dec_t", [P, QT * SSM_HEADS])
        sel_g = sb("sel_g", [SSM_HEADS, GH])
        cum_g, dt_g, win_g, dec_g = [sb(n, [P, QT, GH]) for n in ("cum_g", "dt_g", "win_g", "dec_g")]
        gcol = sb("gcol", [P, GCOLS])
        causal = sb("causal", [P, P])
        c_silu = sb("c_silu", [P, KC])
        mod = sb("mod", [P, 48])
        gain2 = sb("gain2", [P, 2 * KC])
        neg_exp_a = sb("neg_exp_a", [SSM_HEADS, 1])
        neg_mean = sb("neg_mean", [P, QT])
        group_inv = sb("group_inv", [P, GROUPS * QT])
        group_root = sb("group_root", [P, GROUPS * QT])
        sq = sb("sq", [P, 2, S])
        dist = sb("dist", [P, S])
        sq_sum = dist[:, :]
        cols = sb("cols", [P, NCOL])
        poolw = sb("poolw", [P, 4, P])
        ident = sb("ident", [P, P])
        ones = sb("ones", [P, P])
        eps = sb("eps", [P, 2])
        slopes = sb("slopes", [P, HEADS])
        recip_count = sb("recip_count", [P, 16])
        neg_max = sb("neg_max", [P, 2 * QT])
        row_sum = sb("row_sum", [P, 2 * QT])
        row_inv = sb("row_inv", [P, 2 * QT])
        root = sb("root", [P, QT])
        rinv = sb("rinv", [P, QT])

        w_loaded = [sem(f"w_loaded{s}") for s in range(2)]
        w_hi_ready = sem("w_hi_ready")
        w_lo_ready = sem("w_lo_ready")
        pool_turn = sem("pool_turn")
        tile_done = sem("tile_done")
        bank_free = [sem(f"bank_free{b}") for b in range(4)]
        x_loaded = [sem(f"x_loaded{c}") for c in range(4)]
        params_loaded = sem("params_loaded")
        consts = sem("consts")
        const_step = sem("const_step")
        dve_consts = sem("dve_consts")
        sq_ready = sem("sq_ready")
        sum_done = sem("sum_done")
        sq_read = sem("sq_read")
        root_ready = sem("root_ready")
        rinv_ready = sem("rinv_ready")
        r_ready = sem("r_ready")
        pre_raw = sem("pre_raw")
        a_hi_ready = sem("a_hi_ready")
        a_lo_ready = sem("a_lo_ready")
        b_hi_ready = sem("b_hi_ready")
        b_lo_ready = sem("b_lo_ready")
        qkv_ready = sem("qkv_ready")
        p_ready = sem("p_ready")
        s_done = sem("s_done")
        s_read = sem("s_read")
        max_ready = sem("max_ready")
        exp_ready = sem("exp_ready")
        inv_step = sem("inv_step")
        probs_ready = sem("probs_ready")
        t_done = sem("t_done")
        t_read = sem("t_read")
        pv_done = sem("pv_done")
        win_step = sem("win_step")
        win_ready = sem("win_ready")
        einsum_done = sem("einsum_done")
        ya_ready = sem("ya_ready")
        gate_ready = sem("gate_ready")
        m_step = sem("m_step")
        m_ready = sem("m_ready")
        y_ready = sem("y_ready")
        ysq_ready = sem("ysq_ready")
        sq_sum_step = sem("sq_sum_step")
        relu_ready = sem("relu_ready")
        act_step = sem("act_step")
        y_step = sem("y_step")
        post_step = sem("post_step")
        h_ready = sem("h_ready")
        out_done = sem("out_done")

        ada_loaded0 = sem("ada_loaded0")
        ada_loaded1 = sem("ada_loaded1")
        c_ready = sem("c_ready")
        ada_used = sem("ada_used")
        mod_done = sem("mod_done")
        mod_ready = sem("mod_ready")
        gain2_ready = sem("gain2_ready")
        dt_raw_ready = sem("dt_raw_ready")
        exp_dt_ready = sem("exp_dt_ready")
        dt_step = sem("dt_step")
        cum_step = sem("cum_step")
        dtt_done = sem("dtt_done")
        dtt_ready = sem("dtt_ready")
        last_done = sem("last_done")
        last_ready = sem("last_ready")
        win_ready2 = sem("win_ready2")
        gcol_ready = sem("gcol_ready")
        sigb_ready = sem("sigb_ready")
        u_ready = sem("u_ready")
        conv_init = sem("conv_init")
        tap = [sem(f"tap{q}") for q in range(2)]
        uc_ready = sem("uc_ready")
        c4_init = sem("c4_init")
        c4_step = sem("c4_step")
        silu_ready = sem("silu_ready")
        xcopy = sem("xcopy")
        xst_done = sem("xst_done")
        xdt_ready = sem("xdt_ready")
        bt_done = sem("bt_done")
        bn_ready = sem("bn_ready")
        cb_done = sem("cb_done")
        cbm_ready = sem("cbm_ready")
        xw_ready = sem("xw_ready")
        st_done = sem("st_done")
        st_step = sem("st_step")
        st_ready = sem("st_ready")
        row_done = sem("row_done")
        e_ready = sem("e_ready")
        seg_step = sem("seg_step")
        seg_ready = sem("seg_ready")
        segx_ready = sem("segx_ready")
        mt_ready = sem("mt_ready")
        ce_ready = sem("ce_ready")
        y_done = sem("y_done")
        yskip = sem("yskip")
        z_ready = sem("z_ready")
        yz_ready = sem("yz_ready")
        mean_done = sem("mean_done")
        mean_ready = sem("mean_ready")
        mean_spread = sem("mean_spread")
        centered = sem("centered")
        ln_raw = sem("ln_raw")
        ln_silu = sem("ln_silu")
        gsum_done = sem("gsum_done")
        groot_ready = sem("groot_ready")
        ginv_ready = sem("ginv_ready")
        gspread_done = sem("gspread_done")
        yop_raw = sem("yop_raw")
        gc_ready = sem("gc_ready")
        mg_ready = sem("mg_ready")
        gs_ready = sem("gs_ready")
        ssm_step = sem("ssm_step")
        ssm_step2 = sem("ssm_step2")
        merged = sem("merged")
        fs_ready = sem("fs_ready")
        f_raw = sem("f_raw")
        f_hi_ready = sem("f_hi_ready")
        f_lo_ready = sem("f_lo_ready")
        out_raw = sem("out_raw")
        gread = sem("gread")
        g_copy = sem("g_copy")
        ada_loaded = [ada_loaded0, ada_loaded1]

        block = ctx.enter_context(nc.Block())

        def col(name, k):
            c = COLS[name] + k
            return cols[:, c:c + 1] if isinstance(c, int) else cols[:, bass.ds(c, 1)]

        def gc(c):
            return gcol[:, c:c + 1]

        def free_value(t):
            return t // 4 + 2

        def chunk(t, k):
            if isinstance(k, int):
                return t[:, k, :]
            return t[:, bass.ds(k, 1), :].rearrange("p a n -> p (a n)")

        @block.sync
        def _(sp):
            for c in range(4):
                sp.dma_start(h[:, 2 * c:2 * c + 2, :], x_in[:, 2 * c:2 * c + 2, :]).then_inc(x_loaded[c], 16)
                if c == 0:
                    sp.dma_start(cols[:, :], cols_in).then_inc(params_loaded, 16)
                    sp.dma_start(raw[0][:, :], w_in[0]).then_inc(w_loaded[0], 16)
            sp.dma_start(raw[1][:, :], w_in[1]).then_inc(w_loaded[1], 16)
            sp.dma_start(poolw[:, :, :], poolw_in).then_inc(params_loaded, 16)
            with sp.Fori(1, P_END // 2) as i:
                for s in range(2):
                    sp.wait_ge(w_lo_ready, 2 * i + s - 1)
                    sp.dma_start(raw[s][:, :], w_in[bass.ds(2 * i + s, 1)].rearrange("a p n -> (a p) n")) \
                        .then_inc(w_loaded[s], 16)
            if P_END % 2:
                sp.wait_ge(w_lo_ready, P_END - 2)
                sp.dma_start(raw[0][:, :], w_in[P_END - 1]).then_inc(w_loaded[0], 16)
            for k in range(KC):
                sp.wait_ge(out_raw, k + 1)
                sp.dma_start(out[:, k, :], arena[:, k, :]).then_inc(out_done, 16)
            sp.wait_ge(out_done, 16 * KC)

        @block.gpsimd
        def _(pool):
            pool.memset(ones[:, :], 1.0).then_inc(const_step, 1)
            pool.wait_ge(const_step, 1)
            pool.affine_select(out=ident[:, :], in_=ones[:, :], compare_op=ALU.is_equal, fill=0.0, base=0,
                               pattern=[[-1, P]], channel_multiplier=1).then_inc(consts, 1)
            pool.iota(dist[:, :], [[-1, S]], base=S - P, channel_multiplier=1,
                      allow_small_or_imprecise_dtypes=True).then_inc(const_step, 1)
            pool.wait_ge(const_step, 2)
            pool.affine_select(out=dist[:, :], in_=dist[:, :], compare_op=ALU.is_ge, fill=MASKED, base=S - P,
                               pattern=[[-1, S]], channel_multiplier=1).then_inc(consts, 1)
            pool.iota(recip_count[:, :], [[1, 16]], base=1, channel_multiplier=0,
                      allow_small_or_imprecise_dtypes=True).then_inc(consts, 1)
            pool.affine_select(out=causal[:, :], in_=ones[:, :], compare_op=ALU.is_ge, fill=0.0, base=0,
                               pattern=[[1, P]], channel_multiplier=-1).then_inc(consts, 1)

            def low_parts(i, s):
                pool.wait_ge(w_loaded[s], 16 * i + 16)
                pool.wait_ge(w_hi_ready, 2 * i + s + 1)
                pool.tensor_tensor(wlo[s][:, :], raw[s][:, :], whi[s][:, :].bitcast(F32), ALU.subtract) \
                    .then_inc(w_lo_ready, 1)

            with pool.Fori(0, P_END // 2) as i:
                low_parts(i, 0)
                low_parts(i, 1)
            if P_END % 2:
                low_parts(P_END // 2, 0)

        @block.tensor
        def _(pe):
            def high_products(bank, slot, blocks, hi, lo, ready=None):
                for n, (blk, k) in enumerate(blocks):
                    if ready is not None:
                        pe.wait_ge(ready[0], ready[1] + n)
                    w = slice(blk * P, blk * P + P)
                    pe.matmul(gemm_bank[bank][:, :], whi[slot][:, w], hi[:, k, :], start=(n == 0), stop=False)
                    pe.matmul(gemm_bank[bank][:, :], whi[slot][:, w], lo[:, k, :], start=False, stop=False)

            def low_products(bank, slot, blocks, hi):
                last = len(blocks) - 1
                for n, (blk, k) in enumerate(blocks):
                    mm = pe.matmul(gemm_bank[bank][:, :], wlo[slot][:, blk * P:blk * P + P], hi[:, k, :],
                                   start=False, stop=(n == last))
                mm.then_inc(tile_done, 1)

            def tile_high(i, panel, t, p_it, t_it, blocks, hi, lo, ready=None, first=False):
                if first:
                    pe.wait_ge(w_hi_ready, panel + p_it * i + 1)
                pe.wait_ge(bank_free[t % 4], t // 4 + 1 + (t_it // 4) * i)
                high_products(t % 4, panel % 2, blocks, hi, lo, ready)

            def tile_low(i, panel, t, p_it, blocks, hi, first=False):
                if first:
                    pe.wait_ge(w_lo_ready, panel + p_it * i + 1)
                low_products(t % 4, panel % 2, blocks, hi)

            def tile(i, panel, t, p_it, t_it, blocks, hi, lo, ready=None, first=False):
                tile_high(i, panel, t, p_it, t_it, blocks, hi, lo, ready, first)
                tile_low(i, panel, t, p_it, blocks, hi, first)

            def sums(q, n):
                for k in range(KC):
                    pe.wait_ge(sq_ready, KC * q + k + 1)
                    for j in range(QT):
                        mm = pe.matmul(aux[0][:, j:j + 1], sq[:, k % 2, j * P:(j + 1) * P], ones[:, 0:1],
                                       start=(k == 0 and j == 0), stop=(k == KC - 1 and j == QT - 1),
                                       skip_group_check=True)
                    mm.then_inc(sq_read, 1)

            def spread(n):
                pe.wait_ge(rinv_ready, n + 1)
                for j in range(QT):
                    mm = pe.matmul(aux[1][:, j * P:(j + 1) * P], rinv[:, j:j + 1].to_broadcast([P, P]), ident[:, :],
                                   start=True, stop=True)
                mm.then_inc(r_ready, 1)

            pe.wait_ge(consts, 3)
            sums(0, 0)
            spread(0)

            with pe.Fori(0, PAIRS) as i:
                lhs = [[(2 * k + m, k) for k in range(KC)] for m in range(2)]

                def g(j):
                    tile(i, j // 2, j, 4, 8, lhs[j % 2], a_hi, a_lo,
                         ready=(a_lo_ready, 1) if j == 0 else None, first=j % 2 == 0)

                def scores(head, qt):
                    u = 4 * head + qt
                    if u == 0:
                        pe.wait_ge(qkv_ready, 3 * i + 2)
                    if u >= 2:
                        pe.wait_ge(s_read, 8 * i + u - 1)
                    hp = slice(HEAD * head, HEAD * head + HEAD)
                    n = P * (qt + 1)
                    pe.matmul(aux[u % 2][:, 0:n], q_s[hp, qt * P:(qt + 1) * P], k_s[hp, 0:n],
                              start=True, stop=True).then_inc(s_done, 1)

                def transposes(head, j):
                    if head < 0:
                        pe.wait_ge(qkv_ready, 3 * i + 3)
                        for t in range(QT):
                            mm = pe.transpose(aux[2][:, t * P:(t + 1) * P], v_s[:, t * P:(t + 1) * P], ident[:, :])
                    else:
                        if j == 0:
                            pe.wait_ge(probs_ready, 8 * i + 4 * head + 4)
                        pe.wait_ge(t_read, 9 * i + 1 + 4 * head + j)
                        for qt in range(j, QT):
                            mm = pe.transpose(aux[2][:, qt * P:(qt + 1) * P], probs[:, qt, j * P:(j + 1) * P],
                                              ident[:, :])
                    mm.then_inc(t_done, 1)

                def values(head):
                    pe.wait_ge(t_read, 9 * i + 5 + 4 * head)
                    if head == 0:
                        pe.wait_ge(b_lo_ready, i + 1)
                    hp = slice(HEAD * head, HEAD * head + HEAD)
                    for j in range(QT):
                        mm = pe.matmul(aux[3][hp, j * P:S], v_n[:, j * P + HEAD * head:j * P + HEAD * head + HEAD],
                                       probs_t[:, j, j * P:S], start=(j == 0), stop=(j == QT - 1))
                    mm.then_inc(pv_done, 1)

                g(0), g(1), g(2)
                scores(0, 0), scores(0, 1)
                g(3)
                scores(0, 2), scores(0, 3)
                transposes(-1, 0)
                g(4)
                for j in range(QT):
                    transposes(0, j)
                scores(1, 0), scores(1, 1)
                g(5)
                scores(1, 2), scores(1, 3)
                values(0)
                g(6)
                for j in range(QT):
                    transposes(1, j)
                g(7)
                values(1)

            t = T_BRANCH
            for panel in range(2):
                for m in range(4):
                    tile(0, P_BRANCH + panel, t, 0, 0, [(4 * k + m, k) for k in range(4)], b_hi, b_lo,
                         ready=(b_lo_ready, 2) if t == T_BRANCH else None, first=m == 0)
                    t += 1
            for g4 in range(4):
                pe.wait_ge(win_ready, g4 + 1)
                if g4 >= 2:
                    pe.wait_ge(b_lo_ready, 1 + 4 + g4 - 1)
                pe.matmul(aux[g4 % 2][:, :], poolw[:, g4, :], pool_x[:, g4, :], start=True, stop=True) \
                    .then_inc(einsum_done, 1)
            for panel in range(2, 4):
                for m in range(4):
                    tile(0, P_BRANCH + panel, t, 0, 0, [(4 * k + m, 4 + k) for k in range(4)], b_hi, b_lo,
                         ready=(b_lo_ready, 6) if t == T_BRANCH + 8 else None, first=m == 0)
                    t += 1

            with pe.Fori(0, 2) as i:
                for j in range(4):
                    tile(i, P_WOUT + j // 2, T_WOUT + j, 2, 4, [(2 * k + j % 2, k) for k in range(KC)], a_hi, a_lo,
                         ready=(a_lo_ready, KC + 1) if j == 0 else None, first=j % 2 == 0)

            def sums_of_sum(n, steps):
                pe.wait_ge(sq_sum_step, steps)
                for j in range(QT):
                    mm = pe.matmul(aux[0][:, j:j + 1], sq_sum[:, j * P:(j + 1) * P], ones[:, 0:1],
                                   start=(j == 0), stop=(j == QT - 1), skip_group_check=True)
                mm.then_inc(sum_done, 1)

            sums_of_sum(1, 9)
            spread(1)
            sums(1, 2)
            spread(2)

            with pe.Fori(0, MLP_GROUPS) as i:
                for j in range(8):
                    tile(i, P_MLP + j // 2, T_MLP + j, 8, 16, [(2 * k + j % 2, k) for k in range(KC)], a_hi, a_lo,
                         ready=(a_lo_ready, 2 * KC + 1) if j == 0 else None, first=j % 2 == 0)
                for j in range(8):
                    tile(i, P_MLP + 4 + j // 2, T_MLP + 8 + j, 8, 16, [(2 * k + j % 2, k) for k in range(KC)], b_hi, b_lo,
                         ready=(b_lo_ready, 1 + 8 + 8 * i + 1) if j == 0 else None, first=j % 2 == 0)
                    if j == 3:
                        pe.wait_ge(ada_used, ADA_PIECES * i + ADA_PIECES)
                        for m in range(12):
                            mm = pe.matmul(aux[2][:, m:m + 1], ada_acc[:, m * P:(m + 1) * P], ones[:, 0:1],
                                           start=True, stop=True)
                        mm.then_inc(mod_done, 1)
            sums_of_sum(3, 18)
            spread(3)
            sums(2, 4)
            spread(4)

            tile(0, P_DT, T_DT, 0, 0, [(2 * k, k) for k in range(KC)], a_hi, a_lo, ready=(a_lo_ready, 3 * KC + 1), first=True)
            ident_h = ident[0:SSM_HEADS, 0:SSM_HEADS]

            def turn_sums():
                pe.wait_ge(cum_step, QT)
                for c in range(QT):
                    pe.transpose(aux[0][:, c * SSM_HEADS:(c + 1) * SSM_HEADS], cum[:, c * P:(c + 1) * P], ident_h)
                    mm = pe.transpose(aux[0][:, P + c * SSM_HEADS:P + (c + 1) * SSM_HEADS],
                                      dt_row[:, c * P:(c + 1) * P], ident_h)
                mm.then_inc(dtt_done, 1)

            def last_sums():
                pe.wait_ge(dtt_ready, 2)
                pe.matmul(aux[1][:, 0:P], ident[:, P - 1:P].to_broadcast([P, P]), cum_t[:, :], start=True, stop=True) \
                    .then_inc(last_done, 1)

            def ssm_group(i, first):
                def g(j):
                    tile(i, P_GRP + j // 2, T_GRP + j, 8, 16, [(2 * k + j % 2, k) for k in range(KC)], a_hi, a_lo,
                         first=j % 2 == 0)

                def g_part(j, part):
                    blocks = [(2 * k + j % 2, k) for k in range(KC)]
                    if part == 0:
                        tile_high(i, P_GRP + j // 2, T_GRP + j, 8, 16, blocks, a_hi, a_lo, first=j % 2 == 0)
                    else:
                        tile_low(i, P_GRP + j // 2, T_GRP + j, 8, blocks, a_hi, first=j % 2 == 0)

                def turn_x(k):
                    pe.wait_ge(silu_ready, 6 * i + k + 1)
                    if k >= 2:
                        pe.wait_ge(xdt_ready, 4 * i + k - 1)
                    for c in range(QT):
                        mm = pe.transpose(aux[k % 2][:, c * P:(c + 1) * P], e_row[k % 2][:, c * P:(c + 1) * P], ident[:, :])
                    mm.then_inc(xst_done, 1)

                def states(c):
                    pe.wait_ge(xw_ready, 3 * i + c + 1)
                    if c == 2:
                        pe.wait_ge(st_ready, 3 * i + 1)
                    pe.matmul(aux[2 + c % 2][:, :], b_n[:, c * P:(c + 1) * P], x_win[c],
                              start=True, stop=True).then_inc(st_done, 1)

                def row(hh):
                    if hh >= 2:
                        pe.wait_ge(seg_ready, 8 * i + hh - 1)
                    pe.matmul(aux[hh % 2][:, :], sel_g[:, hh:hh + 1].to_broadcast([SSM_HEADS, P]), cum[:, :],
                              start=True, stop=True).then_inc(row_done, 1)

                def outputs(hh):
                    pe.wait_ge(mt_ready, 8 * i + hh + 1)
                    pe.wait_ge(ce_ready, 8 * i + hh + 1)
                    if hh == 4 or hh == 6:
                        pe.wait_ge(yskip, 4 * i + hh // 2 - 1)
                    hp = slice(HEAD * (hh % 2), HEAD * (hh % 2) + HEAD)
                    f = slice(HEAD * hh, HEAD * hh + HEAD)
                    for c in range(QT):
                        t_ = slice(c * P, (c + 1) * P)
                        mm = pe.matmul(aux[2 + hh // 2 % 2][hp, t_], x_dt[:, c, f], seg[hh % 2][:, t_],
                                       start=True, stop=(c == 0))
                        if c:
                            mm = pe.matmul(aux[2 + hh // 2 % 2][hp, t_], state[:, c - 1, f], e_row[hh % 2][:, t_],
                                           start=False, stop=True)
                    mm.then_inc(y_done, 1)

                g(0), g(1), g(2), g(3)
                if first:
                    turn_sums(), last_sums()
                g(4), g(5), g(6)
                turn_x(0)
                g(7)
                turn_x(1)
                g(8)
                turn_x(2)
                g(9)
                turn_x(3)
                g(10)
                pe.wait_ge(silu_ready, 6 * i + 5)
                pe.wait_ge(xdt_ready, 4 * i + 3)
                for c in range(QT):
                    mm = pe.transpose(aux[0][:, c * P:(c + 1) * P], b_t[:, c * P:(c + 1) * P], ident[:, :])
                mm.then_inc(bt_done, 1)
                g(11)
                pe.wait_ge(silu_ready, 6 * i + 6)
                pe.wait_ge(xdt_ready, 4 * i + 4)
                for c in range(QT):
                    mm = pe.matmul(aux[1][:, c * P:(c + 1) * P], b_t[:, c * P:(c + 1) * P], c_t[:, c * P:(c + 1) * P],
                                   start=True, stop=True)
                mm.then_inc(cb_done, 1)
                pe.wait_ge(bn_ready, i + 1)
                pe.wait_ge(gcol_ready, 6 * i + 6)
                row(0)
                states(0)
                states(1)
                g(12)
                pe.wait_ge(cbm_ready, i + 1)
                row(1)
                states(2)
                g_part(13, 0)
                pe.wait_ge(st_ready, 3 * i + 3)
                for hh in range(GH):
                    outputs(hh)
                    if hh + 2 < GH:
                        row(hh + 2)
                    if hh < 5:
                        g_part(13 + (hh + 1) // 2, (hh + 1) % 2)

            ssm_group(0, True)
            with pe.Fori(1, GROUPS) as i:
                ssm_group(i, False)

            for k in range(KC):
                pe.wait_ge(uc_ready, k + 1)
                for j in range(QT):
                    mm = pe.matmul(aux[0][:, j:j + 1], conv_u[:, k, j * P:(j + 1) * P], ones[:, 0:1],
                                   start=(k == 0 and j == 0), stop=(k == KC - 1 and j == QT - 1), skip_group_check=True)
            mm.then_inc(mean_done, 1)
            pe.wait_ge(mean_ready, 1)
            for j in range(QT):
                mm = pe.matmul(aux[1][:, j * P:(j + 1) * P], neg_mean[:, j:j + 1].to_broadcast([P, P]), ident[:, :],
                               start=True, stop=True)
            mm.then_inc(mean_spread, 1)
            sums(3, 5)
            spread(5)

            def full(p, t, hi, lo, ready=None):
                for j in range(2):
                    tile(0, p, t + j, 0, 0, [(2 * k + j, k) for k in range(KC)], hi, lo,
                         ready=ready if j == 0 else None, first=j == 0)

            for m in range(4):
                full(P_CONV + m, T_CONV + 2 * m, b_hi, b_lo, ready=(b_lo_ready, B_USE_CONV + 2) if m == 0 else None)
                for k in range(4 * m, 4 * m + 4):
                    pe.wait_ge(sq_ready, 4 * KC + k + 1)
                    if k == 0:
                        pe.wait_ge(root_ready, 6)
                    for j in range(QT):
                        mm = pe.matmul(aux[0][:, 4 * (k // 4) + j:4 * (k // 4) + j + 1], sq[:, k % 2, j * P:(j + 1) * P],
                                       ones[:, 0:1], start=(k == 0 and j == 0), stop=(k == 15 and j == QT - 1),
                                       skip_group_check=True)
                    mm.then_inc(sq_read, 1)
            for m in range(4):
                full(P_GSSM + m, T_GSSM + 2 * m, a_hi, a_lo)
                if m == 0:
                    pe.wait_ge(ginv_ready, 1)
                    for q in (2, 3):
                        for j in range(QT):
                            mm = pe.matmul(aux[q][:, j * P:(j + 1) * P],
                                           group_inv[:, 4 * q + j:4 * q + j + 1].to_broadcast([P, P]), ident[:, :],
                                           start=True, stop=True)
                        mm.then_inc(gspread_done, 1)
            pe.wait_ge(centered, 8)
            pe.wait_ge(ln_raw, 8)
            for q in (0, 1):
                for j in range(QT):
                    mm = pe.matmul(aux[q][:, j * P:(j + 1) * P],
                                   group_inv[:, 4 * q + j:4 * q + j + 1].to_broadcast([P, P]), ident[:, :],
                                   start=True, stop=True)
                mm.then_inc(gspread_done, 1)
            for m in range(4):
                full(P_SSM + m, T_SSM + 2 * m, b_hi, b_lo, ready=(b_lo_ready, B_USE_SSM + 2) if m == 0 else None)
            for m in range(4):
                full(P_SSM + 4 + m, T_SSM + 8 + 2 * m, a_hi, a_lo, ready=(a_lo_ready, A_USE_SSM + 1) if m == 0 else None)
            for m in range(4):
                full(P_WOUT2 + m, T_WOUT2 + 2 * m, b_hi, b_lo, ready=(b_lo_ready, B_USE_WOUT + 2) if m == 0 else None)
            sums_of_sum(6, 27)
            spread(6)

            for grp in range(FFN_GROUPS):
                p0, t0 = P_FFN + grp * (FC + 8), T_FFN + grp * (2 * FC + 8)

                def up(i, j, ready=None):
                    tile(i, p0 + j // 2, t0 + j, 2, 4, [(2 * k + j % 2, k) for k in range(KC)], a_hi, a_lo,
                         ready=ready, first=j % 2 == 0)

                with pe.Fori(0, FC // 2) as i:
                    for j in range(4):
                        up(i, j, (a_lo_ready, A_USE_FFN + 1) if j == 0 else None)
                up(0, 2 * FC - 2), up(0, 2 * FC - 1)
                with pe.Fori(0, 2) as i:
                    for j in range(4):
                        tile(i, p0 + FC + j, t0 + 2 * FC + j, 4, 4, [(k, k) for k in range(FC)], f_hi, f_lo,
                             ready=(f_lo_ready, FC * grp + 1) if j == 0 else None, first=True)
            sums_of_sum(7, 36)
            spread(7)

        @block.scalar
        def _(act):
            def round_weights(i, panel, p_it, tile_t, t_it):
                act.wait_ge(w_loaded[panel % 2], 16 * (panel // 2 + 1) + 16 * (p_it // 2) * i)
                if tile_t:
                    act.wait_ge(tile_done, tile_t + t_it * i)
                act.activation(whi[panel % 2][:, :], raw[panel % 2][:, :], ACT.Copy).then_inc(w_hi_ready, 1)

            def squares(q):
                for k in range(KC):
                    if q == 0:
                        act.wait_ge(x_loaded[k // 2], 16)
                    else:
                        act.wait_ge(h_ready, KC * (q - 1) + k + 1)
                    if KC * q + k >= 2:
                        act.wait_ge(sq_read, KC * q + k - 1)
                    act.activation(sq[:, k % 2, :], h[:, k, :], ACT.Square).then_inc(sq_ready, 1)

            def roots(n, sem_, value, e=0):
                act.wait_ge(sem_, value)
                act.activation(root[:, :], aux[0][:, 0:QT], ACT.Sqrt, bias=eps[:, e:e + 1], scale=1.0 / D) \
                    .then_inc(root_ready, 1)

            def operand(n):
                for k in range(KC):
                    act.wait_ge(pre_raw, KC * n + k + 1)
                    act.activation(a_hi[:, k, :], tmp[:, k % 2, :], ACT.Copy).then_inc(a_hi_ready, 1)

            def load_ada(piece, slot):
                act.dma_start(ada_w[slot], ada_in[bass.ds(piece, 1)].rearrange("a p n -> (a p) n")) \
                    .then_inc(ada_loaded[slot], 16)

            squares(0)
            act.wait_ge(params_loaded, 32)
            act.activation(c_silu[:, :], cols[:, COLS["c"]:COLS["c"] + KC], ACT.Silu).then_inc(c_ready, 1)
            round_weights(0, 0, 0, 0, 0)
            act.wait_ge(consts, 3)
            act.wait_ge(dve_consts, 2)
            roots(0, sq_read, KC)
            round_weights(0, 1, 0, 0, 0)
            operand(0)

            with act.Fori(0, PAIRS) as i:
                def done(j):
                    act.wait_ge(tile_done, 8 * i + j + 1)
                    return gemm_bank[j % 4][:, :]

                def exps(head, qt):
                    u = 4 * head + qt
                    n = P * (qt + 1)
                    act.wait_ge(max_ready, 8 * i + u + 1)
                    act.activation(probs[:, qt, 0:n], probs[:, qt, 0:n], ACT.Exp, bias=neg_max[:, u:u + 1],
                                   accum_out=row_sum[:, u:u + 1]).then_inc(exp_ready, 1)

                def turned(head, j):
                    act.wait_ge(t_done, 9 * i + (1 if head < 0 else 2 + 4 * head + j))
                    if head < 0:
                        act.activation(v_n, aux[2][:, :], ACT.Copy).then_inc(t_read, 1)
                    else:
                        act.activation(probs_t[:, j, j * P:S], aux[2][:, j * P:S], ACT.Copy).then_inc(t_read, 1)

                def gate(j):
                    src = done(j)
                    k = 4 * i + j - 4
                    act.activation(chunk(gates, k), src, ACT.Identity, bias=col("b_gate", k)) \
                        .then_inc(bank_free[j % 4], 1)

                src = done(0)
                act.activation(q_s, src, ACT.Copy, scale=HEAD ** -0.5).then_inc(bank_free[0], 1)
                src = done(1)
                act.activation(k_s, src, ACT.Copy).then_inc(bank_free[1], 1)
                round_weights(i, P_PAIR + 2, 4, 2, 8)
                act.wait_ge(bank_free[0], 2 * i + 2)
                act.wait_ge(bank_free[1], 2 * i + 2)
                act.sem_inc(qkv_ready, 2)
                src = done(2)
                act.activation(v_s, src, ACT.Copy).then_inc(bank_free[2], 1)
                exps(0, 0)
                act.wait_ge(bank_free[2], 2 * i + 2)
                act.sem_inc(qkv_ready, 1)
                exps(0, 1)
                src = done(3)
                act.activation(chunk(pool_x, i), src, ACT.Copy).then_inc(bank_free[3], 1)
                round_weights(i, P_PAIR + 3, 4, 4, 8)
                exps(0, 2), exps(0, 3)
                turned(-1, 0)
                gate(4)
                for j in range(QT):
                    turned(0, j)
                exps(1, 0), exps(1, 1)
                gate(5)
                round_weights(i, P_PAIR + 4, 4, 6, 8)
                exps(1, 2), exps(1, 3)
                gate(6)
                for j in range(QT):
                    turned(1, j)
                gate(7)
                round_weights(i, P_PAIR + 5, 4, 8, 8)
                act.wait_ge(pv_done, 2 * i + 2)
                act.activation(chunk(b_hi, i), aux[3][:, :], ACT.Copy).then_inc(b_hi_ready, 1)

            act.wait_ge(bank_free[3], 1 + 2 * PAIRS)
            act.sem_inc(p_ready, 1)
            for m in range(KC):
                act.activation(gates[:, 8 + m, :], gates[:, 8 + m, :], ACT.Sigmoid).then_inc(gate_ready, 1)
                act.activation(gates[:, m, :], gates[:, m, :], ACT.Sigmoid).then_inc(gate_ready, 1)
                act.wait_ge(tile_done, T_BRANCH + m + 1)
                act.activation(y_attn[:, m, :], gemm_bank[m % 4][:, :], ACT.Copy).then_inc(bank_free[m % 4], 1)
                if m % 4 == 3:
                    round_weights(0, P_BRANCH + 2 + m // 4, 0, T_BRANCH + m + 1, 0)
            for g4 in range(4):
                act.wait_ge(einsum_done, g4 + 1)
                act.activation(b_hi[:, 4 + g4, :], aux[g4 % 2][:, :], ACT.Identity, scale=col("pool_scale", g4)) \
                    .then_inc(b_hi_ready, 1)
            for m in range(KC):
                act.wait_ge(m_ready, m + 1)
                act.activation(a_hi[:, m, :], tmp[:, m % 2, :], ACT.Copy).then_inc(a_hi_ready, 1)
                if m % 4 == 3:
                    round_weights(0, P_WOUT + m // 4, 0, T_BRANCH + 8 + m + 1, 0)

            with act.Fori(0, 2) as i:
                for j in range(4):
                    act.wait_ge(tile_done, T_WOUT + 4 * i + j + 1)
                    act.wait_ge(sq_sum_step, 4 * i + j) if j >= 1 else act.wait_ge(sq_sum_step, 4 * i + 1 + j)
                    act.activation(sq[:, j % 2, :], gemm_bank[(T_WOUT + j) % 4][:, :], ACT.Square).then_inc(ysq_ready, 1)
                    act.activation(chunk(y, 4 * i + j), gemm_bank[(T_WOUT + j) % 4][:, :], ACT.Copy) \
                        .then_inc(bank_free[(T_WOUT + j) % 4], 1)
                    if j % 2 == 1:
                        round_weights(i, P_WOUT + 2 + j // 2, 2, T_WOUT + j + 1, 4)
            roots(1, sum_done, 1)
            squares(1)
            roots(2, sq_read, 2 * KC)
            operand(1)

            load_ada(0, 0)
            load_ada(1, 1)

            def mlp(i, last):
                for j in range(8):
                    t = T_MLP + j
                    act.wait_ge(tile_done, t + 16 * i + 1)
                    if j >= 1 and not (last and j == 7):
                        act.wait_ge(ada_used, ADA_PIECES * i + j)
                        load_ada(ADA_PIECES * i + j + 1, (j + 1) % 2)
                    if j >= 2:
                        act.wait_ge(b_lo_ready, 9 + 8 * i + j - 1)
                    act.activation(relu[j % 2], gemm_bank[t % 4][:, :], ACT.Relu).then_inc(relu_ready, 1)
                    act.wait_ge(relu_ready, 8 * i + j + 1)
                    act.sem_inc(bank_free[t % 4], 1)
                    act.activation(b_hi[:, j, :], relu[j % 2], ACT.Square).then_inc(b_hi_ready, 1)
                    if j % 2 == 1:
                        round_weights(i, P_MLP + 2 + j // 2, 8, t + 1, 16)
                if not last:
                    act.wait_ge(ada_used, ADA_PIECES * i + ADA_PIECES)
                    load_ada(ADA_PIECES * i + ADA_PIECES + 1, 1)
                for j in range(8):
                    t = T_MLP + 8 + j
                    if last:
                        act.wait_ge(y_step, 8 * i + j + 1)
                        act.wait_ge(sq_sum_step, 10 + max(j - 1, 0))
                        act.activation(sq[:, j % 2, :], y[:, j, :], ACT.Square).then_inc(ysq_ready, 1)
                    if j % 2 == 1:
                        round_weights(i, P_MLP + 6 + j // 2, 8, t + 1, 16)

            with act.Fori(0, MLP_GROUPS - 1) as i:
                mlp(i, False)
            mlp(MLP_GROUPS - 1, True)
            roots(3, sum_done, 2)
            squares(2)
            roots(4, sq_read, 3 * KC)

            def operand_shifted(n, shift):
                for k in range(KC):
                    act.wait_ge(pre_raw, KC * n + k + 1)
                    act.activation(a_hi[:, k, :], tmp[:, k % 2, :], ACT.Identity, bias=mod[:, shift + k:shift + k + 1]) \
                        .then_inc(a_hi_ready, 1)

            act.wait_ge(mod_ready, MLP_GROUPS)
            operand_shifted(2, 0)

            act.wait_ge(tile_done, T_DT + 1)
            act.activation(dt_x, gemm_bank[T_DT % 4][0:SSM_HEADS, :], ACT.Identity,
                           bias=cols[0:SSM_HEADS, COLS["dt_bias"]:COLS["dt_bias"] + 1]).then_inc(bank_free[T_DT % 4], 1)
            act.wait_ge(bank_free[T_DT % 4], free_value(T_DT))
            act.activation(dt_e, dt_x, ACT.Abs).then_inc(dt_raw_ready, 1)
            act.wait_ge(dt_raw_ready, 1)
            act.activation(dt_e, dt_e, ACT.Exp, scale=-1.0).then_inc(exp_dt_ready, 1)
            act.activation(neg_exp_a[:, :], cols[0:SSM_HEADS, COLS["a_log"]:COLS["a_log"] + 1], ACT.Exp) \
                .then_inc(exp_dt_ready, 1)
            round_weights(0, P_DT + 2, 0, T_DT + 1, 0)

            def window_exps():
                act.wait_ge(last_ready, 1)
                act.activation(dec_t[:, :], aux[1][:, 0:P], ACT.Exp).then_inc(win_ready2, 1)
                act.activation(win_t[:, :], win_t[:, :], ACT.Exp).then_inc(win_ready2, 1)

            def ssm_group(i, first):
                def grp_round(j):
                    round_weights(i, P_GRP + j // 2 + 2, 8, T_GRP + j + 1, 16)

                def bank_of(j):
                    act.wait_ge(tile_done, T_GRP + 16 * i + j + 1)
                    return gemm_bank[(T_GRP + j) % 4][:, :]

                def freed(j):
                    return bank_free[(T_GRP + j) % 4]

                def conv_start(q):
                    act.wait_ge(u_ready, 2 * i + q + 1)
                    act.activation(acc31[:, q, :], u_buf[:, q, :], ACT.Identity, bias=gc(G_CONV_B + q),
                                   scale=gc(G_CONV_W + CONV_TAPS * q + CONV_TAPS - 1)).then_inc(conv_init, 1)

                for q in range(2):
                    src = bank_of(2 * q + 1)
                    act.activation(u_buf[:, q, :], src, ACT.Sigmoid).then_inc(freed(2 * q + 1), 1)
                    grp_round(2 * q + 1)
                    if q == 0:
                        if not first:
                            act.wait_ge(gcol_ready, 6 * i + 6)
                            conv_start(0)
                    elif first:
                        window_exps()
                        act.wait_ge(gcol_ready, 6 * i + 6)
                        conv_start(0)
                conv_start(1)

                def c4_start(n):
                    j = 4 + n
                    src = bank_of(j)
                    if n >= 2:
                        act.wait_ge(silu_ready, 6 * i + n - 1)
                    act.activation(sq[:, n % 2, :], src, ACT.Identity, bias=gc(G_SSM_B + n),
                                   scale=gc(G_SSM_W + SSM_TAPS * n + SSM_TAPS - 1)).then_inc(c4_init, 1)

                def c4_end(n):
                    j = 4 + n
                    act.wait_ge(freed(j), free_value(T_GRP + j) + 4 * i)
                    if n < 4:
                        if n >= 2:
                            act.wait_ge(xst_done, 4 * i + n - 1)
                            act.wait_ge(xcopy, 4 * i + n - 1)
                        act.activation(e_row[n % 2], sq[:, n % 2, :], ACT.Silu).then_inc(silu_ready, 1)
                        act.wait_ge(silu_ready, 6 * i + n + 1)
                        act.activation(chunk(y_ssm, 4 * i + n), e_row[n % 2], ACT.Copy).then_inc(xcopy, 1)
                    else:
                        act.activation([b_t, c_t][n - 4], sq[:, n % 2, :], ACT.Silu).then_inc(silu_ready, 1)

                for n in range(6):
                    c4_start(n)
                    if n % 2 == 1:
                        grp_round(4 + n)
                    if n >= 1:
                        c4_end(n - 1)
                c4_end(5)
                src = bank_of(10)
                act.activation(chunk(g_conv, 2 * i), src, ACT.Copy).then_inc(freed(10), 1)
                act.wait_ge(bt_done, i + 1)
                act.activation(b_n, aux[0][:, :], ACT.Copy).then_inc(bn_ready, 1)
                src = bank_of(11)
                act.activation(chunk(g_conv, 2 * i + 1), src, ACT.Copy).then_inc(freed(11), 1)
                grp_round(11)

                def exp_row(hh):
                    act.wait_ge(row_done, 8 * i + hh + 1)
                    if hh >= 2:
                        act.wait_ge(y_done, 8 * i + hh - 1)
                    else:
                        act.wait_ge(xcopy, 4 * i + 4)
                    act.activation(e_row[hh % 2], aux[hh % 2][:, :], ACT.Exp).then_inc(e_ready, 1)

                def exp_seg(hh):
                    act.wait_ge(seg_ready, 8 * i + hh + 1)
                    act.activation(seg[hh % 2], seg[hh % 2], ACT.Exp).then_inc(segx_ready, 1)

                zbuf = [tmp[:, 0, :], tmp[:, 1, :], sq[:, 0, :], sq[:, 1, :]]

                def z_copy(q):
                    src = bank_of(12 + q)
                    act.activation(zbuf[q], src, ACT.Copy).then_inc(freed(12 + q), 1)
                    if q % 2 == 1:
                        grp_round(12 + q)

                for hh in range(GH):
                    exp_row(hh)
                    exp_seg(hh)
                    if hh in (0, 2, 4, 6):
                        z_copy(hh // 2)
                for q in range(4):
                    act.wait_ge(freed(12 + q), free_value(T_GRP + 12 + q) + 4 * i)
                    act.activation(zbuf[q], zbuf[q], ACT.Silu).then_inc(z_ready, 1)
                for q in range(2):
                    act.wait_ge(tap[q], (CONV_TAPS - 1) * (i + 1))
                    act.activation(chunk(conv_u, 2 * i + q), acc31[:, q, :], ACT.Copy).then_inc(uc_ready, 1)

            ssm_group(0, True)
            with act.Fori(1, GROUPS) as i:
                ssm_group(i, False)

            for k in range(KC):
                act.wait_ge(centered, k + 1)
                act.wait_ge(sq_read, 3 * KC + k - 1) if k >= 2 else act.wait_ge(yz_ready, 4 * GROUPS)
                act.activation(sq[:, k % 2, :], conv_u[:, k, :], ACT.Square).then_inc(sq_ready, 1)
            roots(5, sq_read, 4 * KC, e=1)
            for q in range(2):
                act.wait_ge(tap[q], (CONV_TAPS - 1) * GROUPS)
            for k in range(KC):
                act.wait_ge(ln_raw, k + 1)
                if k >= 2:
                    act.wait_ge(b_lo_ready, B_USE_CONV + k)
                act.activation(acc31[:, k % 2, :], tmp[:, k % 2, :], ACT.Silu, bias=col("conv_ln_b", k)).then_inc(ln_silu, 1)
                act.wait_ge(ln_silu, k + 1)
                act.activation(b_hi[:, k, :], acc31[:, k % 2, :], ACT.Copy).then_inc(b_hi_ready, 1)
            for k in range(KC):
                act.activation(g_conv[:, k, :], g_conv[:, k, :], ACT.Sigmoid).then_inc(gc_ready, 1)

            def after(p, t):
                round_weights(0, p + 2, 0, t + 2, 0)

            for m in range(4):
                for k in range(4 * m, 4 * m + 4):
                    act.wait_ge(sq_read, 4 * KC + k - 1)
                    act.activation(sq[:, k % 2, :], y_ssm[:, k, :], ACT.Square).then_inc(sq_ready, 1)
                after(P_CONV + m, T_CONV + 2 * m)
            act.wait_ge(sq_read, 6 * KC)
            act.activation(group_root[:, :], aux[0][:, 0:GROUPS * QT], ACT.Sqrt, bias=eps[:, 0:1],
                           scale=1.0 / (4 * P)).then_inc(groot_ready, 1)

            def y_operand(hi, hi_sem, n0):
                for k in range(KC):
                    act.wait_ge(yop_raw, n0 + k + 1)
                    act.activation(hi[:, k, :], tmp[:, k % 2, :], ACT.Copy).then_inc(hi_sem, 1)

            for m in range(4):
                for j in range(2):
                    act.wait_ge(tile_done, T_GSSM + 2 * m + j + 1)
                    act.activation(g_ssm[:, 2 * m + j, :], gemm_bank[(T_GSSM + 2 * m + j) % 4][:, :], ACT.Sigmoid) \
                        .then_inc(bank_free[(T_GSSM + 2 * m + j) % 4], 1)
                after(P_GSSM + m, T_GSSM + 2 * m)
                for k in range(2 * m, 2 * m + 2):
                    act.wait_ge(yop_raw, k + 1)
                    act.activation(b_hi[:, k, :], tmp[:, k % 2, :], ACT.Copy).then_inc(b_hi_ready, 1)
            y_operand(a_hi, a_hi_ready, KC)
            for m in range(4):
                for j in range(2):
                    t = T_SSM + 2 * m + j
                    act.wait_ge(tile_done, t + 1)
                    act.activation(ssm_out[:, 2 * m + j, :], gemm_bank[t % 4][:, :], ACT.Copy).then_inc(bank_free[t % 4], 1)
                after(P_SSM + m, T_SSM + 2 * m)
            for m in range(4):
                for k in range(2 * m, 2 * m + 2):
                    act.wait_ge(merged, k + 1)
                    act.activation(b_hi[:, k, :], tmp[:, k % 2, :], ACT.Copy).then_inc(b_hi_ready, 1)
                after(P_SSM + 4 + m, T_SSM + 8 + 2 * m)
            for k in range(KC):
                act.wait_ge(h_ready, 2 * KC + k + 1)
                act.wait_ge(sq_sum_step, 19 + max(k - 1, 0))
                act.activation(sq[:, k % 2, :], h[:, k, :], ACT.Square).then_inc(ysq_ready, 1)
                if k % 2 == 1:
                    after(P_WOUT2 + k // 2, T_WOUT2 + k - 1)
            roots(6, sum_done, 3)
            operand_shifted(3, 24)

            def ffn_up(grp, i, j, p_it, t_it, n_it):
                p, t = P_FFN + grp * (FC + 8) + j, T_FFN + grp * (2 * FC + 8) + 2 * j
                n = FC * grp + j + n_it * i
                act.wait_ge(tile_done, t + t_it * i + 1)
                if grp or j >= 2:
                    act.wait_ge(f_lo_ready, n - 1)
                act.activation(ffn_t[(FC * grp + j) % 2], gemm_bank[t % 4][:, :], ACT.Silu).then_inc(bank_free[t % 4], 1)
                act.wait_ge(f_raw, n + 1)
                kk = j + n_it * i
                act.activation(chunk(f_hi, kk), ffn_raw[(FC * grp + j) % 2], ACT.Copy).then_inc(f_hi_ready, 1)
                round_weights(i, p + 2, p_it, t + 2, t_it)

            for grp in range(FFN_GROUPS):
                ffn_up(grp, 0, 0, 0, 0, 0), ffn_up(grp, 0, 1, 0, 0, 0)
                with act.Fori(0, FC // 2 - 1) as i:
                    ffn_up(grp, i, 2, 2, 4, 2), ffn_up(grp, i, 3, 2, 4, 2)
                ffn_up(grp, 0, FC - 1, 0, 0, 0)
                p0, t0 = P_FFN + grp * (FC + 8) + FC, T_FFN + grp * (2 * FC + 8) + 2 * FC
                for k in range(KC):
                    if grp == FFN_GROUPS - 1:
                        act.wait_ge(h_ready, 4 * KC + k + 1)
                        act.wait_ge(sq_sum_step, 28 + max(k - 1, 0))
                        act.activation(sq[:, k % 2, :], h[:, k, :], ACT.Square).then_inc(ysq_ready, 1)
                    if p0 + k + 2 < P_END:
                        round_weights(0, p0 + k + 2, 0, t0 + k + 1, 0)
            roots(7, sum_done, 4)

        @block.vector
        def _(dve):
            def inverse(n):
                dve.wait_ge(root_ready, n + 1)
                if n:
                    dve.wait_ge(rinv_ready, n)
                dve.reciprocal(rinv[:, :], root[:, :]).then_inc(rinv_ready, 1)

            def normed_shifted(n, q, base, part):
                inverse(n)
                dve.wait_ge(r_ready, n + 1)
                for k in range(KC + 1):
                    if k < KC:
                        dve.wait_ge(a_lo_ready, base + max(k - 1, 0))
                        dve.scalar_tensor_tensor(tmp[:, k % 2, :], h[:, k, :], gain2[:, KC * part + k:KC * part + k + 1],
                                                 aux[1][:, :], ALU.mult, ALU.mult).then_inc(pre_raw, 1)
                    if k >= 1:
                        dve.wait_ge(a_hi_ready, base + k)
                        dve.scalar_tensor_tensor(a_lo[:, k - 1, :], tmp[:, (k - 1) % 2, :],
                                                 mod[:, 24 * part + k - 1:24 * part + k],
                                                 a_hi[:, k - 1, :].bitcast(F32), ALU.add, ALU.subtract) \
                            .then_inc(a_lo_ready, 1)

            def normed(n, q, gain):
                inverse(n)
                dve.wait_ge(r_ready, n + 1)
                if q:
                    dve.wait_ge(h_ready, KC * q)
                for k in range(KC + 1):
                    if k < KC:
                        if k >= 2:
                            dve.wait_ge(a_lo_ready, A_USE[q] + k - 1)
                        dve.scalar_tensor_tensor(tmp[:, k % 2, :], h[:, k, :], col(gain, k), aux[1][:, :],
                                                 ALU.mult, ALU.mult).then_inc(pre_raw, 1)
                    if k >= 1:
                        low_part(q, k - 1)

            def low_part(q, k):
                dve.wait_ge(a_hi_ready, A_USE[q] + k + 1)
                dve.tensor_tensor(a_lo[:, k, :], tmp[:, k % 2, :], a_hi[:, k, :].bitcast(F32), ALU.subtract) \
                    .then_inc(a_lo_ready, 1)

            A_USE = [0, 16]

            def residual(n, gain, base, a_used):
                inverse(n)
                dve.wait_ge(r_ready, n + 1)
                dve.wait_ge(a_lo_ready, a_used)
                for k in range(KC):
                    if k >= 2:
                        dve.wait_ge(h_ready, base + k - 1)
                    dve.scalar_tensor_tensor(tmp[:, k % 2, :], y[:, k, :], col(gain, k), aux[1][:, :],
                                             ALU.mult, ALU.mult).then_inc(post_step, 1)
                    dve.wait_ge(post_step, base + k + 1)
                    dve.tensor_tensor(h[:, k, :], h[:, k, :], tmp[:, k % 2, :], ALU.add).then_inc(h_ready, 1)

            for b in range(4):
                dve.sem_inc(bank_free[b], 1)
            dve.sem_inc(b_lo_ready, 1)
            dve.memset(eps[:, 0:1], EPS).then_inc(dve_consts, 1)
            dve.memset(eps[:, 1:2], LN_EPS).then_inc(dve_consts, 1)
            for k in range(HEADS):
                dve.memset(slopes[:, k:k + 1], -(2.0 ** (-8.0 * (k + 1) / HEADS))).then_inc(dve_consts, 1)
            dve.wait_ge(consts, 3)
            dve.reciprocal(recip_count[:, :], recip_count[:, :]).then_inc(dve_consts, 1)
            dve.wait_ge(dve_consts, HEADS + 3)
            dve.wait_ge(params_loaded, 32)
            normed(0, 0, "norm_mix_pre")

            with dve.Fori(0, PAIRS) as i:
                for head in range(2):
                    for qt in range(QT + 1):
                        if qt < QT:
                            u = 4 * head + qt
                            n = P * (qt + 1)
                            dve.wait_ge(s_done, 8 * i + u + 1)
                            if head == 1:
                                dve.wait_ge(t_done, 9 * i + 5)
                            dve.scalar_tensor_tensor(probs[:, qt, 0:n], dist[:, S - n:S], slopes[:, bass.ds(2 * i + head, 1)],
                                                     aux[u % 2][:, 0:n], ALU.mult, ALU.add).then_inc(s_read, 1)
                            dve.wait_ge(s_read, 8 * i + u + 1)
                            dve.tensor_reduce(neg_max[:, u:u + 1], probs[:, qt, 0:n], AX.X, ALU.max, negate=True) \
                                .then_inc(max_ready, 1)
                        if qt >= 1:
                            u = 4 * head + qt - 1
                            n = P * qt
                            dve.wait_ge(exp_ready, 8 * i + u + 1)
                            dve.reciprocal(row_inv[:, u:u + 1], row_sum[:, u:u + 1]).then_inc(inv_step, 1)
                            dve.wait_ge(inv_step, 8 * i + u + 1)
                            dve.tensor_scalar(probs[:, qt - 1, 0:n], probs[:, qt - 1, 0:n], row_inv[:, u:u + 1], None,
                                              ALU.mult).then_inc(probs_ready, 1)
                dve.wait_ge(b_hi_ready, i + 1)
                dve.tensor_tensor(chunk(b_lo, i), aux[3][:, :], chunk(b_hi, i).bitcast(F32), ALU.subtract) \
                    .then_inc(b_lo_ready, 1)

            steps = 0
            dve.wait_ge(p_ready, 1)
            for g in range(4):
                src = pool_x[:, g, :]
                if g:
                    dve.wait_ge(win_ready, g)
                for lvl in range(g + 1):
                    d = 1 << lvl
                    dst = win[lvl % 2]
                    dve.tensor_copy(dst[:, 0:d], src[:, 0:d]).then_inc(win_step, 1)
                    dve.tensor_tensor(dst[:, d:S], src[:, d:S], src[:, 0:S - d], ALU.add).then_inc(win_step, 1)
                    steps += 2
                    dve.wait_ge(win_step, steps)
                    src = dst
                w = 2 << g
                head_w = win[(g + 1) % 2]
                dve.tensor_tensor(head_w[:, 0:w - 1], src[:, 0:w - 1], recip_count[:, 0:w - 1], ALU.mult) \
                    .then_inc(win_step, 1)
                steps += 1
                dve.wait_ge(win_step, steps)
                dve.tensor_tensor(pool_x[:, g, 0:w - 1], head_w[:, 0:w - 1], pool_x[:, g, 0:w - 1], ALU.subtract) \
                    .then_inc(win_step, 1)
                steps += 1
                dve.wait_ge(win_step, steps)
                dve.scalar_tensor_tensor(pool_x[:, g, w - 1:S], src[:, w - 1:S], 1.0 / w, pool_x[:, g, w - 1:S],
                                         ALU.mult, ALU.subtract).then_inc(win_ready, 1)
            for g in range(4):
                dve.wait_ge(b_hi_ready, 4 + g + 1)
                dve.scalar_tensor_tensor(b_lo[:, 4 + g, :], aux[g % 2][:, :], col("pool_scale", g),
                                         b_hi[:, 4 + g, :].bitcast(F32), ALU.mult, ALU.subtract).then_inc(b_lo_ready, 1)
            dve.wait_ge(gate_ready, 2 * KC)
            for m in range(KC):
                if m == 0:
                    for b in range(4):
                        dve.wait_ge(bank_free[b], 1 + (T_BRANCH + 8) // 4)
                dve.tensor_tensor(gates[:, 8 + m, :], gates[:, 8 + m, :], y_attn[:, m, :], ALU.mult).then_inc(m_step, 1)
                dve.wait_ge(tile_done, T_BRANCH + 8 + m + 1)
                dve.tensor_tensor(gates[:, m, :], gates[:, m, :], gemm_bank[m % 4][:, :], ALU.mult).then_inc(bank_free[m % 4], 1)
                dve.wait_ge(m_step, m + 1)
                dve.wait_ge(bank_free[m % 4], 1 + (T_BRANCH + 8 + m) // 4 + 1)
                dve.wait_ge(a_lo_ready, KC + max(m - 1, 0))
                dve.tensor_tensor(tmp[:, m % 2, :], gates[:, 8 + m, :], gates[:, m, :], ALU.add).then_inc(m_ready, 1)
                dve.wait_ge(a_hi_ready, KC + m + 1)
                dve.tensor_tensor(a_lo[:, m, :], tmp[:, m % 2, :], a_hi[:, m, :].bitcast(F32), ALU.subtract) \
                    .then_inc(a_lo_ready, 1)

            dve.memset(sq_sum, 0.0).then_inc(sq_sum_step, 1)
            with dve.Fori(0, 2) as i:
                for j in range(4):
                    dve.wait_ge(ysq_ready, 4 * i + j + 1)
                    dve.wait_ge(sq_sum_step, 4 * i + j + 1)
                    dve.tensor_tensor(sq_sum, sq_sum, sq[:, j % 2, :], ALU.add).then_inc(sq_sum_step, 1)
            for b in range(4):
                dve.wait_ge(bank_free[b], 1 + (T_WOUT + 8) // 4)
            residual(1, "norm_mix_post", 0, 16)
            normed(2, 1, "norm_mlp_pre")

            def mlp(i, first, last):
                for j in range(8):
                    dve.wait_ge(relu_ready, 8 * i + j + 1)
                    dve.tensor_tensor(act_raw[j % 2], relu[j % 2], relu[j % 2], ALU.mult).then_inc(act_step, 1)
                    dve.wait_ge(act_step, 8 * i + j + 1)
                    dve.wait_ge(b_hi_ready, 8 + 8 * i + j + 1)
                    dve.tensor_tensor(b_lo[:, j, :], act_raw[j % 2], b_hi[:, j, :].bitcast(F32), ALU.subtract) \
                        .then_inc(b_lo_ready, 1)
                    dve.wait_ge(ada_loaded[j % 2], 16 * (4 * i + j // 2 + 1))
                    if j == 0:
                        dve.tensor_scalar(ada_acc, ada_w[0], c_silu[:, 0:1], None, ALU.mult).then_inc(ada_used, 1)
                    else:
                        dve.wait_ge(ada_used, ADA_PIECES * i + j)
                        dve.scalar_tensor_tensor(ada_acc, ada_w[j % 2], c_silu[:, j:j + 1], ada_acc,
                                                 ALU.mult, ALU.add).then_inc(ada_used, 1)
                for j in range(8):
                    t = T_MLP + 8 + j
                    bank = gemm_bank[t % 4][:, :]
                    dve.wait_ge(tile_done, t + 16 * i + 1)
                    if first:
                        dve.tensor_copy(y[:, j, :], bank).then_inc(y_step, 1)
                    else:
                        dve.tensor_tensor(y[:, j, :], y[:, j, :], bank, ALU.add).then_inc(y_step, 1)
                    dve.wait_ge(y_step, 8 * i + j + 1)
                    dve.sem_inc(bank_free[t % 4], 1)
                    if j == 5:
                        dve.wait_ge(mod_done, i + 1)
                        dve.tensor_tensor(mod[:, bass.ds(12 * i, 12)], aux[2][:, 0:12],
                                          cols[:, bass.ds(COLS["b_ada"] + 12 * i, 12)], ALU.add).then_inc(mod_ready, 1)
                    if last:
                        dve.wait_ge(ysq_ready, 8 + j + 1)
                        dve.wait_ge(sq_sum_step, 10 + j)
                        dve.tensor_tensor(sq_sum, sq_sum, sq[:, j % 2, :], ALU.add).then_inc(sq_sum_step, 1)

            dve.wait_ge(c_ready, 1)
            mlp(0, True, False)
            with dve.Fori(1, MLP_GROUPS - 1) as i:
                mlp(i, False, False)
            dve.memset(sq_sum, 0.0).then_inc(sq_sum_step, 1)
            mlp(MLP_GROUPS - 1, False, True)
            residual(3, "norm_mlp_post", 8, 24)
            dve.wait_ge(mod_ready, MLP_GROUPS)
            for part, name in enumerate(("norm_mix_w", "norm_ffn_w")):
                dve.scalar_tensor_tensor(gain2[:, KC * part:KC * part + KC], mod[:, 24 * part + KC:24 * part + 2 * KC], 1.0,
                                         cols[:, COLS[name]:COLS[name] + KC], ALU.add, ALU.mult).then_inc(gain2_ready, 1)
            dve.wait_ge(gain2_ready, 2)
            dve.wait_ge(h_ready, 2 * KC)
            normed_shifted(4, 2, 3 * KC, 0)

            n = 0

            def step(ins):
                nonlocal n
                ins.then_inc(dt_step, 1)
                n += 1
                dve.wait_ge(dt_step, n)

            dve.wait_ge(exp_dt_ready, 2)
            step(dve.tensor_scalar(dt_s, dt_e, 2.0, None, ALU.add))
            step(dve.reciprocal(dt_s, dt_s))
            step(dve.tensor_tensor(dt_s, dt_s, dt_e, ALU.mult))
            step(dve.tensor_tensor(dt_q, dt_s, dt_s, ALU.mult))
            step(dve.tensor_scalar(dt_p, dt_q, 1.0 / 17, None, ALU.mult))
            for odd in range(15, 1, -2):
                step(dve.scalar_tensor_tensor(dt_p, dt_p, 1.0 / odd, dt_q, ALU.add, ALU.mult))
            step(dve.scalar_tensor_tensor(dt_p, dt_p, 1.0, dt_s, ALU.add, ALU.mult))
            step(dve.tensor_scalar(dt_x, dt_x, 0.0, None, ALU.max))
            step(dve.scalar_tensor_tensor(dt_row, dt_p, 2.0, dt_x, ALU.mult, ALU.add))
            step(dve.tensor_scalar(dt_p, dt_row, neg_exp_a[:, 0:1], -1.0, ALU.mult, ALU.mult))
            for c in range(QT):
                dve.tensor_tensor_scan(cum[:, c * P:(c + 1) * P], ones[0:SSM_HEADS, :], dt_p[:, c * P:(c + 1) * P],
                                       0.0, ALU.mult, ALU.add).then_inc(cum_step, 1)
            dve.wait_ge(dtt_done, 1)
            dve.tensor_copy(cum_t[:, :], aux[0][:, 0:P]).then_inc(dtt_ready, 1)
            dve.tensor_copy(dt_t[:, :], aux[0][:, P:2 * P]).then_inc(dtt_ready, 1)
            dve.wait_ge(dtt_ready, 2)
            dve.wait_ge(last_done, 1)
            dve.tensor_tensor(win_t[:, :], aux[1][:, 0:P], cum_t[:, :], ALU.subtract).then_inc(last_ready, 1)
            dve.wait_ge(win_ready2, 2)

            def ssm_group(i):
                def done(j):
                    dve.wait_ge(tile_done, T_GRP + 16 * i + j + 1)
                    return gemm_bank[(T_GRP + j) % 4][:, :]

                def freed(j):
                    return bank_free[(T_GRP + j) % 4]

                def taps(a, b, chunks=(0, 1)):
                    for d in range(a, b + 1):
                        for q in chunks:
                            if d == 1:
                                dve.wait_ge(conv_init, 2 * i + q + 1)
                            else:
                                dve.wait_ge(tap[q], (CONV_TAPS - 1) * i + d - 1)
                            dve.scalar_tensor_tensor(acc31[:, q, d:S], u_buf[:, q, 0:S - d],
                                                     gc(G_CONV_W + CONV_TAPS * q + CONV_TAPS - 1 - d), acc31[:, q, d:S],
                                                     ALU.mult, ALU.add).then_inc(tap[q], 1)

                dve.tensor_copy(gcol[:, :], cols[:, bass.ds(COLS["group"] + GCOLS * i, GCOLS)]).then_inc(gcol_ready, 1)
                for dst, src in ((cum_g, cum_t), (dt_g, dt_t), (win_g, win_t), (dec_g, dec_t)):
                    dve.tensor_copy(dst[:, :, :], src[:, :].rearrange("p (c h) -> p c h", c=QT)[:, :, bass.ds(GH * i, GH)]) \
                        .then_inc(gcol_ready, 1)
                dve.tensor_copy(sel_g[:, :], ident[0:SSM_HEADS, bass.ds(GH * i, GH)]).then_inc(gcol_ready, 1)
                dve.wait_ge(gcol_ready, 6 * i + 6)
                for q in range(2):
                    src = done(2 * q + 1)
                    dve.wait_ge(freed(2 * q + 1), free_value(T_GRP + 2 * q + 1) + 4 * i)
                    src = done(2 * q)
                    dve.tensor_tensor(u_buf[:, q, :], u_buf[:, q, :], src, ALU.mult).then_inc(u_ready, 1)
                    dve.wait_ge(u_ready, 2 * i + q + 1)
                    dve.sem_inc(freed(2 * q), 1)
                    taps(1, 8, (q,))

                def conv4(n):
                    j = 4 + n
                    acc = sq[:, n % 2, :]
                    bank = gemm_bank[(T_GRP + j) % 4][:, :]
                    dve.wait_ge(c4_init, 6 * i + n + 1)
                    for d in range(1, SSM_TAPS):
                        ins = dve.scalar_tensor_tensor(acc[:, d:S], bank[:, 0:S - d],
                                                       gc(G_SSM_W + SSM_TAPS * n + SSM_TAPS - 1 - d), acc[:, d:S],
                                                       ALU.mult, ALU.add)
                        if d < SSM_TAPS - 1:
                            ins.then_inc(c4_step, 1)
                            dve.wait_ge(c4_step, 12 * i + 2 * n + d)
                        else:
                            ins.then_inc(freed(j), 1)

                def x_times_dt(k):
                    dve.wait_ge(xst_done, 4 * i + k + 1)
                    heads = lambda ap: ap.rearrange("p c (h f) -> p c h f", h=2)
                    dve.tensor_tensor(heads(x_dt[:, :, k * P:(k + 1) * P]),
                                      heads(aux[k % 2][:, :].rearrange("p (c f) -> p c f", c=QT)),
                                      dt_g[:, :, 2 * k:2 * k + 2].unsqueeze(3).to_broadcast([P, QT, 2, HEAD]),
                                      ALU.mult).then_inc(xdt_ready, 1)

                def per_head(ap, vals):
                    return ap.rearrange("p (h f) -> p h f", h=GH), vals.unsqueeze(2).to_broadcast([P, GH, HEAD])

                def x_window(c):
                    a, b = per_head(x_dt[:, c, :], win_g[:, c, :])
                    dst = x_win[c]
                    if c == 0:
                        dve.wait_ge(xdt_ready, 4 * i + 4)
                    dve.tensor_tensor(dst.rearrange("p (h f) -> p h f", h=GH), a, b, ALU.mult).then_inc(xw_ready, 1)

                def next_state(c):
                    dve.wait_ge(st_done, 3 * i + c + 1)
                    bank = aux[2 + c % 2][:, :]
                    if c == 0:
                        dve.tensor_copy(state[:, 0, :], bank).then_inc(st_ready, 1)
                        return
                    dve.wait_ge(st_ready, 3 * i + c)
                    a, b = per_head(state[:, c - 1, :], dec_g[:, c, :])
                    dve.tensor_tensor(state[:, c, :].rearrange("p (h f) -> p h f", h=GH), a, b, ALU.mult) \
                        .then_inc(st_step, 1)
                    dve.wait_ge(st_step, 2 * i + c)
                    dve.tensor_tensor(state[:, c, :], state[:, c, :], bank, ALU.add).then_inc(st_ready, 1)

                def segments(hh):
                    dve.wait_ge(e_ready, 8 * i + hh + 1)
                    if hh >= 2:
                        dve.wait_ge(y_done, 8 * i + hh - 1)
                    if hh < 2:
                        dve.wait_ge(st_done, 3 * i + hh + 1)
                    for c in range(QT):
                        t_ = slice(c * P, (c + 1) * P)
                        ins = dve.tensor_scalar(seg[hh % 2][:, t_], aux[hh % 2][:, t_], cum_g[:, c, hh:hh + 1], 0.0,
                                                ALU.subtract, ALU.min)
                        if c < QT - 1:
                            ins.then_inc(seg_step, 1)
                        else:
                            ins.then_inc(seg_ready, 1)

                def weigh(hh):
                    dve.wait_ge(segx_ready, 8 * i + hh + 1)
                    dve.tensor_tensor(seg[hh % 2], seg[hh % 2], cb, ALU.mult).then_inc(mt_ready, 1)
                    dve.tensor_tensor(e_row[hh % 2], e_row[hh % 2], c_t, ALU.mult).then_inc(ce_ready, 1)

                def skip(k):
                    dve.wait_ge(y_done, 8 * i + 2 * k + 2)
                    dve.wait_ge(xcopy, 4 * i + k + 1)
                    yk = chunk(y_ssm, 4 * i + k)
                    dve.scalar_tensor_tensor(yk, yk, gc(G_D + k), aux[2 + k % 2][:, :], ALU.mult, ALU.add) \
                        .then_inc(yskip, 1)

                for n in range(6):
                    conv4(n)
                    taps(9 + 2 * n, 10 + 2 * n)
                    if n >= 2:
                        x_times_dt(n - 2)
                for c in range(3):
                    x_window(c)
                taps(21, 23)
                dve.wait_ge(cb_done, i + 1)
                dve.tensor_tensor(cb.rearrange("p (c l) -> p c l", c=QT), aux[1][:, :].rearrange("p (c l) -> p c l", c=QT),
                                  causal[:, :].unsqueeze(1).to_broadcast([P, QT, P]), ALU.mult).then_inc(cbm_ready, 1)
                dve.wait_ge(cbm_ready, i + 1)
                segments(0)
                next_state(0)
                next_state(1)
                weigh(0)
                segments(1)
                next_state(2)
                weigh(1)
                for hh in range(2, GH):
                    segments(hh)
                    taps(22 + hh, 22 + hh)
                    weigh(hh)
                    if hh % 2 == 1:
                        skip((hh - 3) // 2)
                taps(30, 30)
                skip(3)
                for q in range(4):
                    dve.wait_ge(z_ready, 4 * i + q + 1)
                    dve.wait_ge(yskip, 4 * i + q + 1)
                    yk = chunk(y_ssm, 4 * i + q)
                    dve.tensor_tensor(yk, yk, [tmp[:, 0, :], tmp[:, 1, :], sq[:, 0, :], sq[:, 1, :]][q], ALU.mult) \
                        .then_inc(yz_ready, 1)

            ssm_group(0)
            with dve.Fori(1, GROUPS) as i:
                ssm_group(i)

            dve.wait_ge(mean_done, 1)
            dve.tensor_scalar(neg_mean[:, :], aux[0][:, 0:QT], -1.0 / D, None, ALU.mult).then_inc(mean_ready, 1)
            dve.wait_ge(mean_spread, 1)
            for k in range(KC):
                dve.tensor_tensor(conv_u[:, k, :], conv_u[:, k, :], aux[1][:, :], ALU.add).then_inc(centered, 1)
            inverse(5)
            dve.wait_ge(r_ready, 6)
            dve.wait_ge(centered, KC)
            dve.wait_ge(yz_ready, 4 * GROUPS)
            for k in range(KC + 1):
                if k < KC:
                    if k >= 2:
                        dve.wait_ge(ln_silu, k - 1)
                    dve.scalar_tensor_tensor(tmp[:, k % 2, :], conv_u[:, k, :], col("conv_ln_w", k), aux[1][:, :],
                                             ALU.mult, ALU.mult).then_inc(ln_raw, 1)
                if k >= 1:
                    dve.wait_ge(b_hi_ready, B_USE_CONV + k)
                    dve.tensor_tensor(b_lo[:, k - 1, :], acc31[:, (k - 1) % 2, :], b_hi[:, k - 1, :].bitcast(F32),
                                      ALU.subtract).then_inc(b_lo_ready, 1)
            for k in range(KC):
                t = T_CONV + k
                dve.wait_ge(gc_ready, k + 1)
                dve.wait_ge(tile_done, t + 1)
                dve.tensor_tensor(g_conv[:, k, :], g_conv[:, k, :], gemm_bank[t % 4][:, :], ALU.mult) \
                    .then_inc(bank_free[t % 4], 1)
            dve.wait_ge(groot_ready, 1)
            dve.reciprocal(group_inv[:, :], group_root[:, :]).then_inc(ginv_ready, 1)

            def y_operand(first, hi, hi_sem, hi_base, lo, lo_sem, lo_base, n0, spreads):
                dve.wait_ge(gspread_done, spreads)
                for k in range(KC + 1):
                    if k < KC:
                        f = first + k
                        if k >= 2:
                            dve.wait_ge(lo_sem, lo_base + k - 1)
                        dve.scalar_tensor_tensor(tmp[:, k % 2, :], y_ssm[:, f, :], col("ssm_norm_w", f),
                                                 aux[f // 4][:, :], ALU.mult, ALU.mult).then_inc(yop_raw, 1)
                    if k >= 1:
                        dve.wait_ge(hi_sem, hi_base + k)
                        dve.tensor_tensor(lo[:, k - 1, :], tmp[:, (k - 1) % 2, :], hi[:, k - 1, :].bitcast(F32),
                                          ALU.subtract).then_inc(lo_sem, 1)

            dve.wait_ge(ln_silu, KC)
            dve.wait_ge(tile_done, T_GSSM)
            y_operand(8, b_hi, b_hi_ready, B_USE_SSM, b_lo, b_lo_ready, B_USE_SSM + 1, 0, 2)
            dve.wait_ge(tile_done, T_SSM)
            dve.wait_ge(b_lo_ready, B_USE_SSM + 1 + KC)
            y_operand(0, a_hi, a_hi_ready, A_USE_SSM, a_lo, a_lo_ready, A_USE_SSM, KC, 4)
            for k in range(KC + 1):
                if k < KC:
                    t = T_SSM + 8 + k
                    t1 = T_SSM + k
                    dve.wait_ge(tile_done, t + 1)
                    dve.wait_ge(bank_free[t1 % 4], free_value(t1))
                    dve.tensor_tensor(ssm_out[:, k, :], ssm_out[:, k, :], gemm_bank[t % 4][:, :], ALU.add) \
                        .then_inc(bank_free[t % 4], 1)
                    dve.wait_ge(bank_free[t % 4], free_value(t))
                    dve.tensor_tensor(ssm_out[:, k, :], ssm_out[:, k, :], g_ssm[:, k, :], ALU.mult).then_inc(ssm_step, 1)
                    dve.wait_ge(ssm_step, k + 1)
                    dve.wait_ge(b_lo_ready, B_USE_WOUT + k) if k >= 2 else dve.wait_ge(a_lo_ready, A_USE_SSM + KC)
                    dve.tensor_tensor(tmp[:, k % 2, :], ssm_out[:, k, :], g_conv[:, k, :], ALU.add).then_inc(merged, 1)
                if k >= 1:
                    dve.wait_ge(b_hi_ready, B_USE_WOUT + k)
                    dve.tensor_tensor(b_lo[:, k - 1, :], tmp[:, (k - 1) % 2, :], b_hi[:, k - 1, :].bitcast(F32),
                                      ALU.subtract).then_inc(b_lo_ready, 1)

            def add_gated(k, t, part, n, done_count):
                dve.wait_ge(tile_done, done_count)
                dve.wait_ge(h_ready, n - KC + 1)
                hk = chunk(h, k)
                c = 24 * part + 16 + k
                g_ = mod[:, c:c + 1] if isinstance(c, int) else mod[:, bass.ds(c, 1)]
                dve.scalar_tensor_tensor(hk, gemm_bank[t % 4][:, :], g_, hk, ALU.mult, ALU.add).then_inc(h_ready, 1)
                dve.wait_ge(h_ready, n + 1)
                dve.sem_inc(bank_free[t % 4], 1)

            def add_square(k, first, n):
                dve.wait_ge(ysq_ready, n + k + 1)
                dve.wait_ge(sq_sum_step, first + k)
                dve.tensor_tensor(sq_sum, sq_sum, sq[:, k % 2, :], ALU.add).then_inc(sq_sum_step, 1)

            dve.memset(sq_sum, 0.0).then_inc(sq_sum_step, 1)
            for k in range(KC):
                add_gated(k, T_WOUT2 + k, 0, 2 * KC + k, T_WOUT2 + k + 1)
                if k >= 1:
                    add_square(k - 1, 19, 16)
            add_square(KC - 1, 19, 16)
            dve.wait_ge(b_lo_ready, B_USE_WOUT + 1 + KC)
            dve.wait_ge(h_ready, 3 * KC)
            normed_shifted(6, 3, A_USE_FFN, 1)

            def ffn_up(grp, i, j, t_it, n_it):
                t = T_FFN + grp * (2 * FC + 8) + 2 * j
                n = FC * grp + j + n_it * i
                s = (FC * grp + j) % 2
                dve.wait_ge(tile_done, t + t_it * i + 2)
                dve.wait_ge(bank_free[t % 4], free_value(t) + (t_it // 4) * i)
                if grp or j >= 2:
                    dve.wait_ge(f_lo_ready, n - 1)
                dve.tensor_tensor(ffn_raw[s], ffn_t[s], gemm_bank[(t + 1) % 4][:, :], ALU.mult).then_inc(f_raw, 1)
                dve.wait_ge(f_raw, n + 1)
                dve.sem_inc(bank_free[(t + 1) % 4], 1)
                dve.wait_ge(f_hi_ready, n + 1)
                kk = j + n_it * i
                dve.tensor_tensor(chunk(f_lo, kk), ffn_raw[s], chunk(f_hi, kk).bitcast(F32), ALU.subtract) \
                    .then_inc(f_lo_ready, 1)

            for grp in range(FFN_GROUPS):
                ffn_up(grp, 0, 0, 0, 0), ffn_up(grp, 0, 1, 0, 0)
                with dve.Fori(0, FC // 2 - 1) as i:
                    ffn_up(grp, i, 2, 4, 2), ffn_up(grp, i, 3, 4, 2)
                ffn_up(grp, 0, FC - 1, 0, 0)
                if grp == FFN_GROUPS - 1:
                    dve.memset(sq_sum, 0.0).then_inc(sq_sum_step, 1)
                t0 = T_FFN + grp * (2 * FC + 8) + 2 * FC
                for k in range(KC):
                    add_gated(k, t0 + k, 1, (3 + grp) * KC + k, t0 + k + 1)
                    if grp == FFN_GROUPS - 1 and k >= 1:
                        add_square(k - 1, 28, 24)
            add_square(KC - 1, 28, 24)
            inverse(7)
            dve.wait_ge(r_ready, 8)
            dve.wait_ge(h_ready, 5 * KC)
            dve.wait_ge(f_lo_ready, FFN_GROUPS * FC)
            for k in range(KC):
                dve.scalar_tensor_tensor(arena[:, k, :], h[:, k, :], col("final_norm_w", k), aux[1][:, :],
                                         ALU.mult, ALU.mult).then_inc(out_raw, 1)


def panels(w, kc, mc):
    n = w.shape[1] // (mc * P)
    return w.reshape(kc, P, n, mc * P).transpose(2, 1, 0, 3).reshape(n, P, kc * mc * P)


INPUTS = """x norm_mix_pre w_in b_gate pool_w pool_scale w_branch_pool w_branch_attn w_out norm_mix_post
norm_mlp_pre w_up w_down norm_mlp_post c_2 w_ada_mix_2 b_ada_mix_2 norm_mix_w_2 w_in_2 conv_dw_w_2 conv_dw_b_2
conv_ln_w_2 conv_ln_b_2 w_conv_out_2 ssm_conv_w_2 ssm_conv_b_2 dt_bias_2 a_log_2 d_skip_2 ssm_norm_w_2 w_ssm_out_2
w_out_2 w_ada_ffn_2 b_ada_ffn_2 norm_ffn_w_2 w_ffn_in_2 w_ffn_down_2 final_norm_w_2""".split()


def weight_stream(v):
    def pick(w, chunks):
        return np.concatenate([w[:, c * P:(c + 1) * P] for c in chunks], axis=1)

    w_in, up, down = v["w_in"], v["w_up"], v["w_down"]
    stream = [panels(pick(w_in, [4 + i, 8 + i, 12 + i, i] + [16 + 4 * i + j for j in range(4)]), KC, 2)
              for i in range(PAIRS)]
    stream += [panels(v["w_branch_attn"], 4, 4), panels(v["w_branch_pool"], 4, 4), panels(v["w_out"], KC, 2)]
    for g in range(MLP_GROUPS):
        stream += [panels(up[:, g * D:(g + 1) * D], KC, 2), panels(down[g * D:(g + 1) * D, :], KC, 2)]
    w = v["w_in_2"]
    z0, x0 = 16, 32
    dt0 = (x0 + 24) * P
    dt = np.zeros((D, 2 * P), np.float32)
    dt[:, 0:SSM_HEADS] = w[:, dt0:dt0 + SSM_HEADS]
    stream.append(panels(dt, KC, 2))
    gates = w[:, dt0 + SSM_HEADS:]
    for g in range(GROUPS):
        stream.append(panels(pick(w, [2 * g, 8 + 2 * g, 2 * g + 1, 8 + 2 * g + 1]
                                  + [x0 + 4 * g + j for j in range(4)] + [x0 + 16 + g, x0 + 20 + g]), KC, 2))
        stream.append(panels(pick(gates, [2 * g, 2 * g + 1]), KC, 2))
        stream.append(panels(pick(w, [z0 + 4 * g + j for j in range(4)]), KC, 2))
    stream += [panels(v["w_conv_out_2"], KC, 2), panels(pick(gates, range(8, 16)), KC, 2),
               panels(v["w_ssm_out_2"][D:], KC, 2), panels(v["w_ssm_out_2"][:D], KC, 2), panels(v["w_out_2"], KC, 2)]
    ffn, ffn_down = v["w_ffn_in_2"], v["w_ffn_down_2"]
    for g in range(FFN_GROUPS):
        chunks = range(FC * g, FC * g + FC)
        stream.append(panels(pick(ffn, [c + half for c in chunks for half in (0, FFN_GROUPS * FC)]), KC, 2))
        rows = np.zeros((16 * P, D), np.float32)
        rows[:FC * P] = ffn_down[FC * P * g:FC * P * (g + 1)]
        stream.append(panels(rows, 16, 1))
    return np.ascontiguousarray(np.concatenate(stream, axis=0))


def columns(v):
    def cols(a):
        return a.reshape(-1, P).T

    def heads(a):
        out = np.zeros((P, 1), np.float32)
        out[:SSM_HEADS, 0] = a
        return out

    parts = [cols(v[n]) for n in ("norm_mix_pre", "b_gate", "pool_scale", "norm_mix_post", "norm_mlp_pre",
                                  "norm_mlp_post", "b_ada_mix_2", "b_ada_ffn_2", "norm_mix_w_2", "norm_ffn_w_2",
                                  "final_norm_w_2", "conv_ln_w_2", "conv_ln_b_2", "ssm_norm_w_2", "c_2")]
    parts += [heads(v["dt_bias_2"]), heads(v["a_log_2"])]
    wide = v["conv_dw_w_2"].reshape(CONV_TAPS, KC, P).transpose(2, 1, 0)
    short = v["ssm_conv_w_2"].reshape(SSM_TAPS, 24, P).transpose(2, 1, 0)
    wide_b, short_b = cols(v["conv_dw_b_2"]), cols(v["ssm_conv_b_2"])
    d = cols(np.repeat(v["d_skip_2"], HEAD))
    for g in range(GROUPS):
        own = [4 * g + j for j in range(4)] + [16 + g, 20 + g]
        parts += [wide[:, 2 * g:2 * g + 2].reshape(P, -1), wide_b[:, 2 * g:2 * g + 2], short[:, own].reshape(P, -1),
                  short_b[:, own], d[:, 4 * g:4 * g + 4]]
    return np.ascontiguousarray(np.concatenate(parts, axis=1))


def kernel(**inputs):
    import concourse.bacc as bacc
    from concourse.bass_utils import run_bass_kernel_spmd

    v = {n: np.asarray(inputs[n]) for n in INPUTS}
    v = {n: a if n == "final_norm_w_2" else a[0] for n, a in v.items()}
    ada = [v[n].reshape(KC, P, 2, ADA_COLS).transpose(2, 0, 1, 3) for n in ("w_ada_mix_2", "w_ada_ffn_2")]
    arrays = {
        "x_t": np.ascontiguousarray(v["x"].T.reshape(KC, P, S).transpose(1, 0, 2)),
        "weights": weight_stream(v),
        "cols": columns(v),
        "pool_w": np.ascontiguousarray(v["pool_w"].transpose(1, 0, 2)),
        "ada": np.ascontiguousarray(np.concatenate(ada).reshape(4 * ADA_PIECES, P, ADA_COLS)),
    }
    assert arrays["weights"].shape == (P_END, P, PANEL) and arrays["cols"].shape == (P, NCOL)
    nc = bacc.Bacc("TRN2", target_bir_lowering=False, num_devices=1, dynamic_dma_scratch_size=2048)
    aps = [nc.dram_tensor(n + "_dram", a.shape, F32, kind="ExternalInput").ap() for n, a in arrays.items()]
    out = nc.dram_tensor("out_t_dram", (P, KC, S), F32, kind="ExternalOutput").ap()
    build(nc, *aps, out)
    r = run_bass_kernel_spmd(nc, [{n + "_dram": a for n, a in arrays.items()}], core_ids=[0])
    return r.results[0]["out_t_dram"].transpose(1, 0, 2).reshape(D, S).T[None]
```

```python
from contextlib import ExitStack

import numpy as np

import concourse.bass as bass
from concourse import mybir

F32 = mybir.dt.float32
F32R = mybir.dt.float32r
ACT = mybir.ActivationFunctionType
ALU = mybir.AluOpType
AX = mybir.AxisListType

P = 128
S = 512
D = 1024
KC = D // P
EPS = 1e-6
HEAD = 64
HEADS = 8
QT = S // P
PANEL = 16 * P
MASKED = 1e33

GROUPS = 4
GH = 8
SSM_HEADS = GROUPS * GH
CONV_TAPS = 31
SSM_TAPS = 4
FFN_GROUPS = 2
FC = 11
ADA_PIECES = 8
ADA_COLS = 12 * P
LN_EPS = 1e-5

PAIRS = 4
P_PAIR = 0
P_BRANCH = P_PAIR + 4 * PAIRS
P_WOUT = P_BRANCH + 4
P_MLP = P_WOUT + 4
MLP_GROUPS = 4
P_DT = P_MLP + MLP_GROUPS * 8
P_GRP = P_DT + 1
P_GATE = P_GRP + 8 * GROUPS
P_CONV = P_GATE + 2
P_GATE2 = P_CONV + 4
P_SSM = P_GATE2 + 2
P_WOUT2 = P_SSM + 8
P_FFN = P_WOUT2 + 4
P_END = P_FFN + FFN_GROUPS * (FC + 8)
T_PAIR = 0
T_BRANCH = T_PAIR + 8 * PAIRS
T_WOUT = T_BRANCH + 16
T_MLP = T_WOUT + 8
T_DT = T_MLP + MLP_GROUPS * 16
T_GRP = T_DT + 1
T_GATE = T_GRP + 16 * GROUPS
T_CONV = T_GATE + 4
T_GATE2 = T_CONV + 8
T_SSM = T_GATE2 + 4
T_WOUT2 = T_SSM + 16
T_FFN = T_WOUT2 + 8
T_END = T_FFN + FFN_GROUPS * (2 * FC + 8)

G_CONV_W, G_CONV_B = 0, 2 * CONV_TAPS
G_SSM_W = G_CONV_B + 2
G_SSM_B = G_SSM_W + 6 * SSM_TAPS
G_D = G_SSM_B + 6
GCOLS = G_D + 4

COLS = {}


def _cols():
    at = 0
    for name, n in [("norm_mix_pre", 8), ("b_gate", 16), ("pool_scale", 4), ("norm_mix_post", 8),
                    ("norm_mlp_pre", 8), ("norm_mlp_post", 8), ("b_ada", 48), ("norm_mix_w", 8),
                    ("norm_ffn_w", 8), ("final_norm_w", 8), ("conv_ln_w", 8), ("conv_ln_b", 8), ("ssm_norm_w", 16),
                    ("c", 8), ("dt_bias", 1), ("a_log", 1), ("group", GCOLS * GROUPS)]:
        COLS[name] = at
        at += n
    return at


NCOL = _cols()


def build(nc, x_in, w_in, cols_in, poolw_in, ada_in, out):
    A_USE_SSM = 4 * KC
    A_USE_FFN = A_USE_SSM + KC
    B_USE_CONV = KC + MLP_GROUPS * KC
    B_USE_SSM = B_USE_CONV + KC
    B_USE_WOUT = B_USE_SSM + KC

    with ExitStack() as ctx:
        def sb(name, shape, dt=F32):
            return ctx.enter_context(nc.sbuf_tensor(name, shape, dt))

        def sem(name):
            return ctx.enter_context(nc.semaphore(name))

        gemm_bank = [ctx.enter_context(nc.psum_tensor(f"gemm_bank{b}", [P, S], F32)) for b in range(4)]
        aux = [ctx.enter_context(nc.psum_tensor(f"aux_bank{b}", [P, S], F32)) for b in range(4)]

        raw = [sb(f"w_raw{s}", [P, PANEL]) for s in range(2)]
        whi = [sb(f"w_hi{s}", [P, PANEL], F32R) for s in range(2)]
        wlo = [sb(f"w_lo{s}", [P, PANEL], F32R) for s in range(2)]
        h = sb("h", [P, KC, S])
        a_hi = sb("a_hi", [P, KC, S], F32R)
        a_raw = sb("a_raw", [P, KC, S])
        a_lo = nc.alloc_sbuf_tensor_at("a_lo", [P, KC, S], F32R, offset=nc.sbuf_base - KC * S * 4)
        CHUNK = S * 4
        b_at = nc.sbuf_base
        scratch = sb("scratch", [P, 16, S])
        b_hi = nc.alloc_sbuf_tensor_at("b_hi", [P, KC, S], F32R, offset=b_at)
        b_lo = nc.alloc_sbuf_tensor_at("b_lo", [P, KC, S], F32R, offset=b_at + KC * CHUNK)
        b_raw = scratch[:, KC:2 * KC, :]
        arena_at = nc.sbuf_base
        arena = sb("arena", [P, 32, S])
        f_hi = nc.alloc_sbuf_tensor_at("f_hi", [P, FC, S], F32R, offset=arena_at)
        f_lo = nc.alloc_sbuf_tensor_at("f_lo", [P, FC, S], F32R, offset=arena_at + FC * CHUNK)
        ada_w = [arena[:, 20 + 3 * s:23 + 3 * s, :].rearrange("p a n -> p (a n)") for s in range(2)]
        ada_acc = arena[:, 26:29, :].rearrange("p a n -> p (a n)")
        conv_u = arena[:, 0:8, :]
        y_ssm = arena[:, 8:24, :]
        g_conv = arena[:, 24:32, :]
        g_ssm = arena[:, 0:8, :]
        ssm_out = arena[:, 16:24, :]
        ffn_t = [arena[:, 22 + s, :] for s in range(2)]
        ffn_raw = [arena[:, 24 + s, :] for s in range(2)]
        e_row = [scratch[:, 0 + s, :] for s in range(2)]
        x_dt = scratch[:, 2:6, :]
        state = scratch[:, 6:9, :]
        cb = scratch[:, 9, :]
        b_t = scratch[:, 10, :]
        c_t = scratch[:, 11, :]
        b_n = scratch[:, 12, :]
        ln_sq = scratch[:, 0:8, :]
        u_buf = scratch[:, 13:15, :]
        gates = arena[:, 0:16, :]
        y = arena[:, 0:8, :]
        pool_x = arena[:, 16:20, :]
        probs = arena[:, 20:24, :]
        probs_t = arena[:, 24:28, :]
        y_attn = arena[:, 20:28, :]
        q_s = arena[:, 28, :]
        k_s = arena[:, 29, :]
        v_s = arena[:, 30, :]
        v_n = arena[:, 31, :]
        win = [arena[:, 28, :], arena[:, 29, :]]
        relu = [arena[:, 16 + s, :] for s in range(2)]
        act_raw = [arena[:, 18 + s, :] for s in range(2)]
        tmp = sb("tmp", [P, 2, S])
        acc31 = sb("acc31", [P, 2, S])
        sq_acc = acc31[:, 0, :]
        seg1 = sb("seg1", [P, S])
        seg = [scratch[:, 15, :], seg1[:, :]]
        ln_sum = seg1[:, :]
        x_win = [seg[0], seg[1], state[:, 2, :]]
        dt_x, dt_e, dt_s, dt_q, dt_p = [scratch[0:SSM_HEADS, c, :] for c in range(5)]
        dt_row = scratch[0:SSM_HEADS, 5, :]
        cum = sb("cum", [SSM_HEADS, S])
        cum_t = sb("cum_t", [P, QT * SSM_HEADS])
        dt_t = sb("dt_t", [P, QT * SSM_HEADS])
        win_t = sb("win_t", [P, QT * SSM_HEADS])
        dec_t = sb("dec_t", [P, QT * SSM_HEADS])
        sel_g = sb("sel_g", [SSM_HEADS, GH], F32R)
        cum_lo = sb("cum_lo", [SSM_HEADS, S], F32R)
        cum_g, dt_g, win_g, dec_g = [sb(n, [P, QT, GH]) for n in ("cum_g", "dt_g", "win_g", "dec_g")]
        gcol = sb("gcol", [P, GCOLS])
        causal = sb("causal", [P, P])
        c_silu = sb("c_silu", [P, KC])
        mod = sb("mod", [P, 48])
        gain2 = sb("gain2", [P, 2 * KC])
        neg_exp_a = sb("neg_exp_a", [SSM_HEADS, 1])
        neg_mean = sb("neg_mean", [P, QT])
        group_inv = sb("group_inv", [P, GROUPS * QT])
        group_root = sb("group_root", [P, GROUPS * QT])
        sq = sb("sq", [P, 2, S])
        dist_at = nc.sbuf_base
        dist = sb("dist", [P, S])
        cum_hi = nc.alloc_sbuf_tensor_at("cum_hi", [SSM_HEADS, S], F32R, offset=dist_at)
        sq_sum = dist[:, :]
        y_sq = [sq[:, 0, :], sq[:, 1, :], tmp[:, 0, :], tmp[:, 1, :]]
        r_row = acc31[:, 1, :]
        cols = sb("cols", [P, NCOL])
        poolw = sb("poolw", [P, 4, P])
        u_sum = poolw[:, :, :].rearrange("p g n -> p (g n)")
        ident = sb("ident", [P, P])
        ones = sb("ones", [P, P])
        eps = sb("eps", [P, 2])
        table_out = sb("table_out", [P, 8])
        slopes = sb("slopes", [P, HEADS])
        recip_count = sb("recip_count", [P, 16])
        neg_max = sb("neg_max", [P, 2 * QT])
        row_sum = sb("row_sum", [P, 2 * QT])
        row_inv = sb("row_inv", [P, 2 * QT])
        root = sb("root", [P, QT])
        rinv = sb("rinv", [P, QT])

        w_loaded = [sem(f"w_loaded{s}") for s in range(2)]
        w_hi_ready = sem("w_hi_ready")
        w_lo_ready = sem("w_lo_ready")
        tile_done = sem("tile_done")
        bank_free = [sem(f"bank_free{b}") for b in range(4)]
        x_loaded = [sem(f"x_loaded{c}") for c in range(4)]
        params_loaded = sem("params_loaded")
        poolw_loaded = sem("poolw_loaded")
        consts = sem("consts")
        const_step = sem("const_step")
        dve_consts = sem("dve_consts")
        sq_ready = sem("sq_ready")
        sum_done = sem("sum_done")
        sq_read = sem("sq_read")
        added = [sem("added_dve"), sem("added_pool")]
        root_ready = sem("root_ready")
        rinv_ready = sem("rinv_ready")
        r_ready = sem("r_ready")
        r_row_ready = sem("r_row_ready")
        pre_raw = sem("pre_raw")
        a_hi_ready = sem("a_hi_ready")
        a_lo_ready = sem("a_lo_ready")
        b_hi_ready = sem("b_hi_ready")
        b_lo_ready = sem("b_lo_ready")
        s_done = sem("s_done")
        s_read = sem("s_read")
        max_ready = sem("max_ready")
        exp_ready = sem("exp_ready")
        inv_step = sem("inv_step")
        probs_ready = sem("probs_ready")
        t_done = sem("t_done")
        t_read = sem("t_read")
        pv_done = sem("pv_done")
        win_step = sem("win_step")
        win_ready = sem("win_ready")
        einsum_done = sem("einsum_done")
        gate_ready = sem("gate_ready")
        m_step = sem("m_step")
        m_ready = sem("m_ready")
        ysq_ready = sem("ysq_ready")
        sq_sum_step = sem("sq_sum_step")
        relu_ready = sem("relu_ready")
        act_step = sem("act_step")
        y_step = sem("y_step")
        post_step = sem("post_step")
        h_ready = sem("h_ready")
        out_done = sem("out_done")

        ada_loaded0 = sem("ada_loaded0")
        ada_loaded1 = sem("ada_loaded1")
        c_ready = sem("c_ready")
        ada_used = sem("ada_used")
        mod_done = sem("mod_done")
        mod_ready = sem("mod_ready")
        gain2_ready = sem("gain2_ready")
        dt_raw_ready = sem("dt_raw_ready")
        exp_dt_ready = sem("exp_dt_ready")
        dt_step = sem("dt_step")
        cum_step = sem("cum_step")
        cum_split = sem("cum_split")
        dtt_done = sem("dtt_done")
        dtt_ready = sem("dtt_ready")
        last_done = sem("last_done")
        last_ready = sem("last_ready")
        win_ready2 = sem("win_ready2")
        gcol_ready = sem("gcol_ready")
        u_ready = sem("u_ready")
        conv_init = sem("conv_init")
        tap = [sem(f"tap{q}") for q in range(2)]
        uc_ready = sem("uc_ready")
        c4_init = sem("c4_init")
        c4_step = sem("c4_step")
        silu_ready = sem("silu_ready")
        xcopy = sem("xcopy")
        xst_done = sem("xst_done")
        xdt_ready = sem("xdt_ready")
        bt_done = sem("bt_done")
        bn_ready = sem("bn_ready")
        cb_done = sem("cb_done")
        cbm_ready = sem("cbm_ready")
        xw_ready = sem("xw_ready")
        st_done = sem("st_done")
        st_step = sem("st_step")
        st_ready = sem("st_ready")
        row_done = sem("row_done")
        e_ready = sem("e_ready")
        seg_step = sem("seg_step")
        seg_ready = sem("seg_ready")
        segx_ready = sem("segx_ready")
        mt_ready = sem("mt_ready")
        ce_ready = sem("ce_ready")
        y_done = sem("y_done")
        yskip = sem("yskip")
        z_ready = sem("z_ready")
        yz_ready = sem("yz_ready")
        u_sum_step = sem("u_sum_step")
        ln_sum_step = sem("ln_sum_step")
        group_step = sem("group_step")
        mean_done = sem("mean_done")
        mean_ready = sem("mean_ready")
        mean_spread = sem("mean_spread")
        centered = sem("centered")
        ln_raw = sem("ln_raw")
        ln_silu = sem("ln_silu")
        groot_ready = sem("groot_ready")
        ginv_ready = sem("ginv_ready")
        gspread_done = sem("gspread_done")
        yop_raw = sem("yop_raw")
        gc_ready = sem("gc_ready")
        gs_ready = sem("gs_ready")
        ssm_step = sem("ssm_step")
        merged = sem("merged")
        f_raw = sem("f_raw")
        f_hi_ready = sem("f_hi_ready")
        f_lo_ready = sem("f_lo_ready")
        out_raw = sem("out_raw")
        ada_loaded = [ada_loaded0, ada_loaded1]

        block = ctx.enter_context(nc.Block())

        def col(name, k):
            c = COLS[name] + k
            return cols[:, c:c + 1] if isinstance(c, int) else cols[:, bass.ds(c, 1)]

        def gc(c):
            return gcol[:, c:c + 1]

        def free_value(t):
            return t // 4 + 2

        def chunk(t, k):
            if isinstance(k, int):
                return t[:, k, :]
            return t[:, bass.ds(k, 1), :].rearrange("p a n -> p (a n)")

        def add_squares(engine, q, chunks=range(1, KC - 1)):
            signal, base = added[q > 0], 6 * max(q - 1, 0)
            for k in chunks:
                engine.wait_ge(sq_ready, KC * q + k + 1)
                if k >= 2:
                    engine.wait_ge(signal, base + k - 1)
                engine.tensor_tensor(sq_acc, sq_acc, sq[:, k % 2, :], ALU.add).then_inc(signal, 1)

        @block.sync
        def _(sp):
            sp.dma_start(cols[:, :], cols_in).then_inc(params_loaded, 16)
            sp.dma_start(raw[0][:, :], w_in[0]).then_inc(w_loaded[0], 16)
            for c in range(4):
                sp.dma_start(h[:, 2 * c:2 * c + 2, :], x_in[:, 2 * c:2 * c + 2, :]).then_inc(x_loaded[c], 16)
            sp.dma_start(raw[1][:, :], w_in[1]).then_inc(w_loaded[1], 16)
            sp.dma_start(poolw[:, :, :], poolw_in).then_inc(poolw_loaded, 16)
            with sp.Fori(1, P_END // 2) as i:
                for s in range(2):
                    sp.wait_ge(w_lo_ready, 2 * i + s - 1)
                    sp.dma_start(raw[s][:, :], w_in[bass.ds(2 * i + s, 1)].rearrange("a p n -> (a p) n")) \
                        .then_inc(w_loaded[s], 16)
            if P_END % 2:
                sp.wait_ge(w_lo_ready, P_END - 2)
                sp.dma_start(raw[0][:, :], w_in[P_END - 1]).then_inc(w_loaded[0], 16)
            for k in range(KC):
                sp.wait_ge(out_raw, k + 1)
                sp.dma_start(out[:, k, :], arena[:, k, :]).then_inc(out_done, 16)
            sp.wait_ge(out_done, 16 * KC)

        @block.gpsimd
        def _(pool):
            pool.memset(ones[:, :], 1.0).then_inc(const_step, 1)
            pool.wait_ge(const_step, 1)
            pool.affine_select(out=ident[:, :], in_=ones[:, :], compare_op=ALU.is_equal, fill=0.0, base=0,
                               pattern=[[-1, P]], channel_multiplier=1).then_inc(consts, 1)
            pool.iota(dist[:, :], [[-1, S]], base=S - P, channel_multiplier=1,
                      allow_small_or_imprecise_dtypes=True).then_inc(const_step, 1)
            pool.wait_ge(const_step, 2)
            pool.affine_select(out=dist[:, :], in_=dist[:, :], compare_op=ALU.is_ge, fill=MASKED, base=S - P,
                               pattern=[[-1, S]], channel_multiplier=1).then_inc(consts, 1)
            pool.iota(recip_count[:, :], [[1, 16]], base=1, channel_multiplier=0,
                      allow_small_or_imprecise_dtypes=True).then_inc(consts, 1)
            pool.affine_select(out=causal[:, :], in_=ones[:, :], compare_op=ALU.is_ge, fill=0.0, base=0,
                               pattern=[[1, P]], channel_multiplier=-1).then_inc(consts, 1)

            def low_parts(i, s):
                pool.wait_ge(w_loaded[s], 16 * i + 16)
                pool.wait_ge(w_hi_ready, 2 * i + s + 1)
                pool.tensor_tensor(wlo[s][:, :], raw[s][:, :], whi[s][:, :].bitcast(F32), ALU.subtract) \
                    .then_inc(w_lo_ready, 1)

            at = 0
            for q, until in ((1, P_MLP // 2 + 1), (2, P_DT // 2 + 1), (None, P_END // 2)):
                with pool.Fori(at, until) as i:
                    low_parts(i, 0)
                    low_parts(i, 1)
                at = until
                if q is not None:
                    add_squares(pool, q)
            if P_END % 2:
                low_parts(P_END // 2, 0)

        @block.tensor
        def _(pe):
            def high_products(bank, slot, blocks, hi, lo, ready=None, of=slice(None)):
                for n, (blk, k) in list(enumerate(blocks))[of]:
                    if ready is not None:
                        pe.wait_ge(ready[0], ready[1] + n)
                    w = slice(blk * P, blk * P + P)
                    pe.matmul(gemm_bank[bank][:, :], whi[slot][:, w], hi[:, k, :], start=(n == 0), stop=False)
                    pe.matmul(gemm_bank[bank][:, :], whi[slot][:, w], lo[:, k, :], start=False, stop=False)

            def low_products(bank, slot, blocks, hi):
                last = len(blocks) - 1
                for n, (blk, k) in enumerate(blocks):
                    mm = pe.matmul(gemm_bank[bank][:, :], wlo[slot][:, blk * P:blk * P + P], hi[:, k, :],
                                   start=False, stop=(n == last))
                mm.then_inc(tile_done, 1)

            def tile_high(i, panel, t, p_it, t_it, blocks, hi, lo, ready=None, first=False, of=slice(None)):
                if first:
                    pe.wait_ge(w_hi_ready, panel + p_it * i + 1)
                pe.wait_ge(bank_free[t % 4], t // 4 + 1 + (t_it // 4) * i)
                high_products(t % 4, panel % 2, blocks, hi, lo, ready, of)

            def tile_low(i, panel, t, p_it, blocks, hi, first=False):
                if first:
                    pe.wait_ge(w_lo_ready, panel + p_it * i + 1)
                low_products(t % 4, panel % 2, blocks, hi)

            def tile(i, panel, t, p_it, t_it, blocks, hi, lo, ready=None, first=False):
                tile_high(i, panel, t, p_it, t_it, blocks, hi, lo, ready, first)
                tile_low(i, panel, t, p_it, blocks, hi, first)

            def tile_pair(tiles, hi, lo, hi_ready, lo_ready, low_weights_first):
                for n in range(len(tiles[0][5])):
                    pe.wait_ge(hi_ready[0], hi_ready[1] + n)
                    for i, panel, t, p_it, t_it, blocks in tiles:
                        blk, k = blocks[n]
                        w = slice(blk * P, blk * P + P)
                        if n == 0:
                            pe.wait_ge(w_hi_ready, panel + p_it * i + 1)
                            pe.wait_ge(bank_free[t % 4], t // 4 + 1 + (t_it // 4) * i)
                        pe.matmul(gemm_bank[t % 4][:, :], whi[panel % 2][:, w], hi[:, k, :], start=(n == 0), stop=False)
                        if low_weights_first:
                            if n == 0:
                                pe.wait_ge(w_lo_ready, panel + p_it * i + 1)
                            pe.matmul(gemm_bank[t % 4][:, :], wlo[panel % 2][:, w], hi[:, k, :], start=False, stop=False)
                if not low_weights_first:
                    for i, panel, t, p_it, t_it, blocks in tiles:
                        pe.wait_ge(w_lo_ready, panel + p_it * i + 1)
                        for blk, k in blocks:
                            pe.matmul(gemm_bank[t % 4][:, :], wlo[panel % 2][:, blk * P:blk * P + P], hi[:, k, :],
                                      start=False, stop=False)
                last = len(tiles[0][5]) - 1
                for n in range(last + 1):
                    pe.wait_ge(lo_ready[0], lo_ready[1] + n)
                    for i, panel, t, p_it, t_it, blocks in tiles:
                        blk, k = blocks[n]
                        mm = pe.matmul(gemm_bank[t % 4][:, :], whi[panel % 2][:, blk * P:blk * P + P], lo[:, k, :],
                                       start=False, stop=(n == last))
                        if n == last:
                            mm.then_inc(tile_done, 1)

            def wide(j):
                return [(2 * k + j % 2, k) for k in range(KC)]

            def sums(q):
                pe.wait_ge(sq_ready, KC * q + KC)
                pe.wait_ge(added[q > 0], 6 * max(q, 1))
                for part, of in enumerate((sq[:, 1, :], sq_acc)):
                    for j in range(QT):
                        mm = pe.matmul(aux[0][:, j:j + 1], of[:, j * P:(j + 1) * P], ones[:, 0:1],
                                       start=(part == 0 and j == 0), stop=(part == 1 and j == QT - 1),
                                       skip_group_check=True)
                mm.then_inc(sum_done, 1)

            def spread(n):
                pe.wait_ge(rinv_ready, n + 1)
                for j in range(QT):
                    mm = pe.matmul(aux[1][:, j * P:(j + 1) * P], rinv[:, j:j + 1].to_broadcast([P, P]), ident[:, :],
                                   start=True, stop=True)
                mm.then_inc(r_ready, 1)

            pe.wait_ge(consts, 3)

            def pair_of_heads(i, first):
                def g(j):
                    tile(i, j // 2, j, 4, 8, wide(j), a_hi, a_lo, first=j % 2 == 0)

                def scores(head, qt):
                    u = 4 * head + qt
                    if u == 0:
                        pe.wait_ge(bank_free[0], 2 * i + 2)
                        pe.wait_ge(bank_free[1], 2 * i + 2)
                    if u >= 2:
                        pe.wait_ge(s_read, 8 * i + u - 1)
                    hp = slice(HEAD * head, HEAD * head + HEAD)
                    n = P * (qt + 1)
                    pe.matmul(aux[u % 2][:, 0:n], q_s[hp, qt * P:(qt + 1) * P], k_s[hp, 0:n],
                              start=True, stop=True).then_inc(s_done, 1)

                def transposes(head, j):
                    if head < 0:
                        pe.wait_ge(bank_free[2], 2 * i + 2)
                        for t in range(QT):
                            mm = pe.transpose(aux[2][:, t * P:(t + 1) * P], v_s[:, t * P:(t + 1) * P], ident[:, :])
                    else:
                        if j == 0:
                            pe.wait_ge(probs_ready, 8 * i + 4 * head + 4)
                        pe.wait_ge(t_read, 9 * i + 1 + 4 * head + j)
                        for qt in range(j, QT):
                            mm = pe.transpose(aux[2][:, qt * P:(qt + 1) * P], probs[:, qt, j * P:(j + 1) * P],
                                              ident[:, :])
                    mm.then_inc(t_done, 1)

                def values(head):
                    pe.wait_ge(t_read, 9 * i + 5 + 4 * head)
                    if head == 0:
                        pe.wait_ge(b_lo_ready, i + 1)
                    hp = slice(HEAD * head, HEAD * head + HEAD)
                    for j in range(QT):
                        mm = pe.matmul(aux[3][hp, j * P:S], v_n[:, j * P + HEAD * head:j * P + HEAD * head + HEAD],
                                       probs_t[:, j, j * P:S], start=(j == 0), stop=(j == QT - 1))
                    mm.then_inc(pv_done, 1)

                tile_pair([(i, 0, j, 4, 8, wide(j)) for j in range(2)], a_hi, a_lo,
                          (a_hi_ready, 1), (a_lo_ready, 1), False)
                if first:
                    sums(0)
                tile_high(i, 1, 2, 4, 8, wide(2), a_hi, a_lo, first=True)
                if first:
                    spread(0)
                tile_low(i, 1, 2, 4, wide(2), a_hi, first=True)
                scores(0, 0), scores(0, 1)
                g(3)
                scores(0, 2), scores(0, 3)
                transposes(-1, 0)
                g(4)
                for head in range(2):
                    j = 5 + 2 * head
                    transposes(head, 0)
                    tile_high(i, j // 2, j, 4, 8, wide(j), a_hi, a_lo, of=slice(0, KC // 2))
                    transposes(head, 1)
                    high_products(j % 4, (j // 2) % 2, wide(j), a_hi, a_lo, of=slice(KC // 2, KC))
                    transposes(head, 2)
                    tile_low(i, j // 2, j, 4, wide(j), a_hi)
                    transposes(head, 3)
                    if head == 0:
                        for qt in range(QT):
                            scores(1, qt)
                        g(6)
                        values(0)
                values(1)

            pair_of_heads(0, True)
            with pe.Fori(1, PAIRS) as i:
                pair_of_heads(i, False)

            def branch_tiles(panel, t, k0):
                blocks = [[(4 * k + m, k0 + k) for k in range(4)] for m in range(4)]
                tile_pair([(0, P_BRANCH + panel, t + m, 0, 0, blocks[m]) for m in range(2)], b_hi, b_lo,
                          (b_hi_ready, k0 + 1), (b_lo_ready, k0 + 2), False)
                for m in range(2, 4):
                    tile(0, P_BRANCH + panel, t + m, 0, 0, blocks[m], b_hi, b_lo)

            t = T_BRANCH
            for panel in range(2):
                branch_tiles(panel, t, 0)
                t += 4
            pe.wait_ge(poolw_loaded, 16)
            for g4 in range(4):
                pe.wait_ge(win_ready, g4 + 1)
                pe.matmul(aux[g4][:, :], poolw[:, g4, :], pool_x[:, g4, :], start=True, stop=True) \
                    .then_inc(einsum_done, 1)
            for panel in range(2, 4):
                branch_tiles(panel, t, 4)
                t += 4

            with pe.Fori(0, 2) as i:
                tile_pair([(i, P_WOUT, T_WOUT + j, 2, 4, wide(j)) for j in range(2)], a_hi, a_lo,
                          (a_hi_ready, KC + 1), (a_lo_ready, KC + 1), False)
                for j in range(2, 4):
                    tile(i, P_WOUT + j // 2, T_WOUT + j, 2, 4, wide(j), a_hi, a_lo, first=j % 2 == 0)

            def sums_of_sum(steps, squares_made=None):
                pe.wait_ge(sq_sum_step, steps)
                parts = [sq_sum]
                if squares_made is not None:
                    pe.wait_ge(ysq_ready, squares_made)
                    parts.append(sq[:, 1, :])
                for n, of in enumerate(parts):
                    for j in range(QT):
                        mm = pe.matmul(aux[0][:, j:j + 1], of[:, j * P:(j + 1) * P], ones[:, 0:1],
                                       start=(n == 0 and j == 0), stop=(n == len(parts) - 1 and j == QT - 1),
                                       skip_group_check=True)
                mm.then_inc(sum_done, 1)

            sums_of_sum(9)
            spread(1)
            def mlp(i, first):
                tile_pair([(i, P_MLP, T_MLP + j, 8, 16, wide(j)) for j in range(2)], a_hi, a_lo,
                          (a_hi_ready, 2 * KC + 1), (a_lo_ready, 2 * KC + 1), True)
                if first:
                    sums(1)
                tile_high(i, P_MLP + 1, T_MLP + 2, 8, 16, wide(2), a_hi, a_lo, first=True)
                if first:
                    spread(2)
                tile_low(i, P_MLP + 1, T_MLP + 2, 8, wide(2), a_hi, first=True)
                for j in range(3, 8):
                    tile(i, P_MLP + j // 2, T_MLP + j, 8, 16, wide(j), a_hi, a_lo, first=j % 2 == 0)
                tile_pair([(i, P_MLP + 4, T_MLP + 8 + j, 8, 16, wide(j)) for j in range(2)], b_hi, b_lo,
                          (b_hi_ready, KC + KC * i + 1), (b_lo_ready, 1 + KC + KC * i + 1), False)
                for j in range(2, 8):
                    tile(i, P_MLP + 4 + j // 2, T_MLP + 8 + j, 8, 16, wide(j), b_hi, b_lo, first=j % 2 == 0)
                    if j == 3:
                        pe.wait_ge(ada_used, ADA_PIECES * i + ADA_PIECES)
                        for m in range(12):
                            mm = pe.matmul(aux[2][:, m:m + 1], ada_acc[:, m * P:(m + 1) * P], ones[:, 0:1],
                                           start=True, stop=True)
                        mm.then_inc(mod_done, 1)

            mlp(0, True)
            with pe.Fori(1, MLP_GROUPS) as i:
                mlp(i, False)
            sums_of_sum(17, 16)
            spread(3)
            sums(2)
            spread(4)

            tile_pair([(0, P_DT, T_DT, 0, 0, wide(0)), (0, P_GRP, T_GRP, 0, 0, wide(0))], a_hi, a_lo,
                      (a_hi_ready, 3 * KC + 1), (a_lo_ready, 3 * KC + 1), True)
            ident_h = ident[0:SSM_HEADS, 0:SSM_HEADS]

            def turn_sums():
                pe.wait_ge(cum_step, QT)
                for c in range(QT):
                    pe.transpose(aux[0][:, c * SSM_HEADS:(c + 1) * SSM_HEADS], cum[:, c * P:(c + 1) * P], ident_h)
                    mm = pe.transpose(aux[0][:, P + c * SSM_HEADS:P + (c + 1) * SSM_HEADS],
                                      dt_row[:, c * P:(c + 1) * P], ident_h)
                mm.then_inc(dtt_done, 1)

            def last_sums():
                pe.wait_ge(dtt_ready, 2)
                pe.matmul(aux[1][:, 0:P], ident[:, P - 1:P].to_broadcast([P, P]), cum_t[:, :], start=True, stop=True) \
                    .then_inc(last_done, 1)

            def ssm_group(i, first):
                def g(j):
                    tile(i, P_GRP + j // 2, T_GRP + j, 8, 16, [(2 * k + j % 2, k) for k in range(KC)], a_hi, a_lo,
                         first=j % 2 == 0)

                def third(n):
                    j, part = 13 + n // 3, n % 3
                    blocks = [(2 * k + j % 2, k) for k in range(KC)]
                    if part == 0:
                        tile_high(i, P_GRP + j // 2, T_GRP + j, 8, 16, blocks, a_hi, a_lo, first=j % 2 == 0,
                                  of=slice(0, KC // 2))
                    elif part == 1:
                        high_products((T_GRP + j) % 4, (P_GRP + j // 2) % 2, blocks, a_hi, a_lo, of=slice(KC // 2, KC))
                    else:
                        tile_low(i, P_GRP + j // 2, T_GRP + j, 8, blocks, a_hi, first=j % 2 == 0)

                def turn_x(k):
                    pe.wait_ge(silu_ready, 6 * i + k + 1)
                    if k >= 2:
                        pe.wait_ge(xdt_ready, 4 * i + k - 1)
                    for c in range(QT):
                        mm = pe.transpose(aux[k % 2][:, c * P:(c + 1) * P], e_row[k % 2][:, c * P:(c + 1) * P], ident[:, :])
                    mm.then_inc(xst_done, 1)

                def states(c):
                    pe.wait_ge(xw_ready, 3 * i + c + 1)
                    if c == 2:
                        pe.wait_ge(st_ready, 3 * i + 1)
                    pe.matmul(aux[2 + c % 2][:, :], b_n[:, c * P:(c + 1) * P], x_win[c],
                              start=True, stop=True).then_inc(st_done, 1)

                def row(hh):
                    if hh == 0:
                        pe.wait_ge(cum_split, 2)
                    if hh >= 2:
                        pe.wait_ge(seg_ready, 8 * i + hh - 1)
                    sel = sel_g[:, hh:hh + 1].to_broadcast([SSM_HEADS, P])
                    pe.matmul(aux[hh % 2][:, :], sel, cum_hi[:, :], start=True, stop=False)
                    pe.matmul(aux[hh % 2][:, :], sel, cum_lo[:, :], start=False, stop=True).then_inc(row_done, 1)

                def outputs(hh):
                    pe.wait_ge(mt_ready, 8 * i + hh + 1)
                    pe.wait_ge(ce_ready, 8 * i + hh + 1)
                    if hh == 4 or hh == 6:
                        pe.wait_ge(yskip, 4 * i + hh // 2 - 1)
                    hp = slice(HEAD * (hh % 2), HEAD * (hh % 2) + HEAD)
                    f = slice(HEAD * hh, HEAD * hh + HEAD)
                    for c in range(QT):
                        t_ = slice(c * P, (c + 1) * P)
                        mm = pe.matmul(aux[2 + hh // 2 % 2][hp, t_], x_dt[:, c, f], seg[hh % 2][:, t_],
                                       start=True, stop=(c == 0))
                        if c:
                            mm = pe.matmul(aux[2 + hh // 2 % 2][hp, t_], state[:, c - 1, f], e_row[hh % 2][:, t_],
                                           start=False, stop=True)
                    mm.then_inc(y_done, 1)

                if not first:
                    g(0)
                g(1), g(2), g(3)
                if first:
                    turn_sums(), last_sums()
                g(4), g(5), g(6)
                turn_x(0)
                g(7)
                turn_x(1)
                g(8)
                turn_x(2)
                g(9)
                turn_x(3)
                g(10)
                pe.wait_ge(silu_ready, 6 * i + 5)
                pe.wait_ge(xdt_ready, 4 * i + 3)
                for c in range(QT):
                    mm = pe.transpose(aux[0][:, c * P:(c + 1) * P], b_t[:, c * P:(c + 1) * P], ident[:, :])
                mm.then_inc(bt_done, 1)
                g(11)
                pe.wait_ge(silu_ready, 6 * i + 6)
                pe.wait_ge(xdt_ready, 4 * i + 4)
                for c in range(QT):
                    mm = pe.matmul(aux[1][:, c * P:(c + 1) * P], b_t[:, c * P:(c + 1) * P], c_t[:, c * P:(c + 1) * P],
                                   start=True, stop=True)
                mm.then_inc(cb_done, 1)
                pe.wait_ge(bn_ready, i + 1)
                pe.wait_ge(gcol_ready, 6 * i + 6)
                row(0)
                states(0)
                states(1)
                g(12)
                pe.wait_ge(cbm_ready, i + 1)
                row(1)
                states(2)
                third(0)
                third(1)
                pe.wait_ge(st_ready, 3 * i + 3)
                for hh in range(GH):
                    outputs(hh)
                    if hh + 2 < GH:
                        row(hh + 2)
                    if hh < 7:
                        third(hh + 2)

            ssm_group(0, True)
            with pe.Fori(1, GROUPS) as i:
                ssm_group(i, False)

            def gate_tile(j, thirds=(0, 1, 2)):
                blocks = [(2 * k + j % 2, k) for k in range(KC)]
                if 0 in thirds:
                    tile_high(0, P_GATE + j // 2, T_GATE + j, 0, 0, blocks, a_hi, a_lo, first=j % 2 == 0,
                              of=slice(0, KC // 2))
                if 1 in thirds:
                    high_products((T_GATE + j) % 4, (P_GATE + j // 2) % 2, blocks, a_hi, a_lo, of=slice(KC // 2, KC))
                if 2 in thirds:
                    tile_low(0, P_GATE + j // 2, T_GATE + j, 0, blocks, a_hi, first=j % 2 == 0)

            def token_sums(of, signal):
                for j in range(QT):
                    mm = pe.matmul(aux[0][:, j:j + 1], of[:, j * P:(j + 1) * P], ones[:, 0:1],
                                   start=(j == 0), stop=(j == QT - 1), skip_group_check=True)
                mm.then_inc(signal, 1)

            gate_tile(0, (0,))
            pe.wait_ge(u_sum_step, KC - 1)
            token_sums(u_sum, mean_done)
            gate_tile(0, (1,))
            pe.wait_ge(mean_ready, 1)
            for j in range(QT):
                mm = pe.matmul(aux[1][:, j * P:(j + 1) * P], neg_mean[:, j:j + 1].to_broadcast([P, P]), ident[:, :],
                               start=True, stop=True)
            mm.then_inc(mean_spread, 1)
            gate_tile(0, (2,))
            gate_tile(1)
            gate_tile(2, (0, 1))
            pe.wait_ge(ln_sum_step, KC - 1)
            token_sums(ln_sum, sum_done)
            gate_tile(2, (2,))
            spread(5)
            gate_tile(3)

            def full(p, t, hi, lo, hi_ready=None, lo_ready=None, low_weights_first=False):
                if hi_ready is not None:
                    tile_pair([(0, p, t + j, 0, 0, wide(j)) for j in range(2)], hi, lo, hi_ready, lo_ready,
                              low_weights_first)
                    return
                for j in range(2):
                    tile(0, p, t + j, 0, 0, wide(j), hi, lo, first=j == 0)

            for m in range(4):
                full(P_CONV + m, T_CONV + 2 * m, b_hi, b_lo,
                     *((b_hi_ready, B_USE_CONV + 1), (b_lo_ready, B_USE_CONV + 2), True) if m == 0 else ())
                pe.wait_ge(group_step, 3 * m + 3)
                if m == 0:
                    pe.wait_ge(root_ready, 6)
                for j in range(QT):
                    mm = pe.matmul(aux[0][:, 4 * m + j:4 * m + j + 1], y_sq[0][:, j * P:(j + 1) * P], ones[:, 0:1],
                                   start=(m == 0 and j == 0), stop=(m == 3 and j == QT - 1), skip_group_check=True)
                mm.then_inc(sq_read, 1)
            for m in range(2):
                full(P_GATE2 + m, T_GATE2 + 2 * m, a_hi, a_lo)
                if m == 0:
                    pe.wait_ge(ginv_ready, 1)
                    for q in (2, 3):
                        for j in range(QT):
                            mm = pe.matmul(aux[q][:, j * P:(j + 1) * P],
                                           group_inv[:, 4 * q + j:4 * q + j + 1].to_broadcast([P, P]), ident[:, :],
                                           start=True, stop=True)
                        mm.then_inc(gspread_done, 1)
            pe.wait_ge(centered, 8)
            pe.wait_ge(ln_raw, 8)
            for q in (0, 1):
                for j in range(QT):
                    mm = pe.matmul(aux[q][:, j * P:(j + 1) * P],
                                   group_inv[:, 4 * q + j:4 * q + j + 1].to_broadcast([P, P]), ident[:, :],
                                   start=True, stop=True)
                mm.then_inc(gspread_done, 1)
            for m in range(4):
                full(P_SSM + m, T_SSM + 2 * m, b_hi, b_lo,
                     *((b_hi_ready, B_USE_SSM + 1), (b_lo_ready, B_USE_SSM + 2), False) if m == 0 else ())
            for m in range(4):
                full(P_SSM + 4 + m, T_SSM + 8 + 2 * m, a_hi, a_lo,
                     *((a_hi_ready, A_USE_SSM + 1), (a_lo_ready, A_USE_SSM + 1), False) if m == 0 else ())
            for m in range(4):
                full(P_WOUT2 + m, T_WOUT2 + 2 * m, b_hi, b_lo,
                     *((b_hi_ready, B_USE_WOUT + 1), (b_lo_ready, B_USE_WOUT + 2), False) if m == 0 else ())
            sums_of_sum(25, 24)
            spread(6)

            for grp in range(FFN_GROUPS):
                p0, t0 = P_FFN + grp * (FC + 8), T_FFN + grp * (2 * FC + 8)

                def up(i, j):
                    tile(i, p0 + j // 2, t0 + j, 2, 4, wide(j), a_hi, a_lo, first=j % 2 == 0)

                with pe.Fori(0, FC // 2) as i:
                    tile_pair([(i, p0, t0 + j, 2, 4, wide(j)) for j in range(2)], a_hi, a_lo,
                              (a_hi_ready, A_USE_FFN + 1), (a_lo_ready, A_USE_FFN + 1), True)
                    up(i, 2), up(i, 3)
                up(0, 2 * FC - 2), up(0, 2 * FC - 1)
                with pe.Fori(0, 2) as i:
                    for j in range(4):
                        tile(i, p0 + FC + j, t0 + 2 * FC + j, 4, 4, [(k, k) for k in range(FC)], f_hi, f_lo,
                             ready=(f_lo_ready, FC * grp + 1) if j == 0 else None, first=True)
            sums_of_sum(33, 32)
            spread(7)

        @block.scalar
        def _(act):
            def round_weights(i, panel, p_it, tile_t, t_it):
                act.wait_ge(w_loaded[panel % 2], 16 * (panel // 2 + 1) + 16 * (p_it // 2) * i)
                if tile_t:
                    act.wait_ge(tile_done, tile_t + t_it * i)
                act.activation(whi[panel % 2][:, :], raw[panel % 2][:, :], ACT.Copy).then_inc(w_hi_ready, 1)

            def squares(q, gain=None, chunks=range(KC)):
                for k in chunks:
                    if q == 0:
                        act.wait_ge(x_loaded[k // 2], 16)
                    else:
                        act.wait_ge(h_ready, KC * (q - 1) + k + 1)
                    if gain is not None:
                        act.activation(a_hi[:, k, :], h[:, k, :], ACT.Identity, scale=col(gain, k)) \
                            .then_inc(a_hi_ready, 1)
                    if k >= 3:
                        act.wait_ge(added[q > 0], 6 * max(q - 1, 0) + k - 2)
                    act.activation(sq[:, k % 2, :] if k else sq_acc, h[:, k, :], ACT.Square).then_inc(sq_ready, 1)

            tables = 0

            def load_table(func):
                nonlocal tables
                act.activation(table_out[:, tables:tables + 1], eps[:, 0:1], func)
                tables += 1

            def roots(n, sem_, value, e=0):
                act.wait_ge(sem_, value)
                act.activation(root[:, :], aux[0][:, 0:QT], ACT.Sqrt, bias=eps[:, e:e + 1], scale=1.0 / D) \
                    .then_inc(root_ready, 1)

            def load_ada(piece, slot):
                act.dma_start(ada_w[slot], ada_in[bass.ds(piece, 1)].rearrange("a p n -> (a p) n")) \
                    .then_inc(ada_loaded[slot], 16)

            act.wait_ge(params_loaded, 16)
            act.activation(c_silu[:, :], cols[:, COLS["c"]:COLS["c"] + KC], ACT.Silu).then_inc(c_ready, 1)
            act.wait_ge(dve_consts, 2)
            load_table(ACT.Sqrt)
            round_weights(0, 0, 0, 0, 0)
            squares(0, "norm_mix_pre")
            round_weights(0, 1, 0, 0, 0)
            roots(0, sum_done, 1)

            with act.Fori(0, PAIRS) as i:
                def exps(head, qt):
                    u = 4 * head + qt
                    n = P * (qt + 1)
                    act.wait_ge(max_ready, 8 * i + u + 1)
                    act.activation(probs[:, qt, 0:n], probs[:, qt, 0:n], ACT.Exp, bias=neg_max[:, u:u + 1],
                                   accum_out=row_sum[:, u:u + 1]).then_inc(exp_ready, 1)

                def turned(head, j):
                    act.wait_ge(t_done, 9 * i + (1 if head < 0 else 2 + 4 * head + j))
                    if head < 0:
                        act.activation(v_n, aux[2][:, :], ACT.Copy).then_inc(t_read, 1)
                    else:
                        act.activation(probs_t[:, j, j * P:S], aux[2][:, j * P:S], ACT.Copy).then_inc(t_read, 1)

                round_weights(i, P_PAIR + 2, 4, 2, 8)
                exps(0, 0), exps(0, 1)
                round_weights(i, P_PAIR + 3, 4, 4, 8)
                exps(0, 2), exps(0, 3)
                turned(-1, 0)
                for j in range(QT):
                    turned(0, j)
                exps(1, 0), exps(1, 1)
                round_weights(i, P_PAIR + 4, 4, 6, 8)
                exps(1, 2), exps(1, 3)
                for j in range(QT):
                    turned(1, j)
                round_weights(i, P_PAIR + 5, 4, 8, 8)
                act.wait_ge(pv_done, 2 * i + 2)
                act.activation(chunk(b_hi, i), aux[3][:, :], ACT.Copy).then_inc(b_hi_ready, 1)

            for b in range(4):
                act.wait_ge(bank_free[b], 1 + 2 * PAIRS)
            for m in range(KC):
                for k in (8 + m, m):
                    act.activation(gates[:, k, :], gates[:, k, :], ACT.Sigmoid, bias=col("b_gate", k)) \
                        .then_inc(gate_ready, 1)
                act.wait_ge(tile_done, T_BRANCH + m + 1)
                act.activation(y_attn[:, m, :], gemm_bank[m % 4][:, :], ACT.Copy).then_inc(bank_free[m % 4], 1)
                if m % 4 == 3:
                    round_weights(0, P_BRANCH + 2 + m // 4, 0, T_BRANCH + m + 1, 0)
            for g4 in range(4):
                act.wait_ge(einsum_done, g4 + 1)
                act.activation(b_hi[:, 4 + g4, :], aux[g4][:, :], ACT.Identity, scale=col("pool_scale", g4)) \
                    .then_inc(b_hi_ready, 1)
            for m in range(KC):
                act.wait_ge(m_ready, m + 1)
                act.activation(a_hi[:, m, :], a_raw[:, m, :], ACT.Copy).then_inc(a_hi_ready, 1)
                if m % 4 == 3:
                    round_weights(0, P_WOUT + m // 4, 0, T_BRANCH + 8 + m + 1, 0)

            load_table(ACT.Sqrt)
            with act.Fori(0, 2) as i:
                for j in range(4):
                    act.wait_ge(tile_done, T_WOUT + 4 * i + j + 1)
                    act.wait_ge(sq_sum_step, 4 * i + max(j, 1))
                    act.activation(sq[:, j % 2, :], gemm_bank[(T_WOUT + j) % 4][:, :], ACT.Square).then_inc(ysq_ready, 1)
                    act.activation(chunk(y, 4 * i + j), gemm_bank[(T_WOUT + j) % 4][:, :], ACT.Copy) \
                        .then_inc(bank_free[(T_WOUT + j) % 4], 1)
                    if j % 2 == 1:
                        round_weights(i, P_WOUT + 2 + j // 2, 2, T_WOUT + j + 1, 4)
            roots(1, sum_done, 2)
            squares(1, "norm_mlp_pre")
            roots(2, sum_done, 3)

            load_ada(0, 0)
            load_ada(1, 1)

            def mlp(i, last):
                for j in range(8):
                    t = T_MLP + j
                    act.wait_ge(relu_ready, 8 * i + j + 1)
                    if j >= 1 and not (last and j == 7):
                        act.wait_ge(ada_used, ADA_PIECES * i + j)
                        load_ada(ADA_PIECES * i + j + 1, (j + 1) % 2)
                    act.activation(b_hi[:, j, :], relu[j % 2], ACT.Square).then_inc(b_hi_ready, 1)
                    if j % 2 == 1:
                        round_weights(i, P_MLP + 2 + j // 2, 8, t + 1, 16)
                if not last:
                    act.wait_ge(ada_used, ADA_PIECES * i + ADA_PIECES)
                    load_ada(ADA_PIECES * i + ADA_PIECES + 1, 1)
                for j in range(8):
                    t = T_MLP + 8 + j
                    if last:
                        act.wait_ge(y_step, 8 * i + j + 1)
                        act.wait_ge(sq_sum_step, 10 + max(j - 1, 0))
                        act.activation(sq[:, j % 2, :], y[:, j, :], ACT.Square).then_inc(ysq_ready, 1)
                    if j % 2 == 1:
                        round_weights(i, P_MLP + 6 + j // 2, 8, t + 1, 16)

            with act.Fori(0, MLP_GROUPS - 1) as i:
                mlp(i, False)
            mlp(MLP_GROUPS - 1, True)
            roots(3, sum_done, 4)
            squares(2)
            roots(4, sum_done, 5)

            def operand_shifted(n, shift):
                for k in range(KC):
                    act.wait_ge(pre_raw, KC * (n - 2) + k + 1)
                    act.activation(a_hi[:, k, :], a_raw[:, k, :], ACT.Identity, bias=mod[:, shift + k:shift + k + 1]) \
                        .then_inc(a_hi_ready, 1)

            act.wait_ge(mod_ready, MLP_GROUPS)
            operand_shifted(2, 0)

            act.wait_ge(tile_done, T_DT + 1)
            act.activation(dt_x, gemm_bank[T_DT % 4][0:SSM_HEADS, :], ACT.Identity,
                           bias=cols[0:SSM_HEADS, COLS["dt_bias"]:COLS["dt_bias"] + 1]).then_inc(bank_free[T_DT % 4], 1)
            act.wait_ge(bank_free[T_DT % 4], free_value(T_DT))
            act.activation(dt_e, dt_x, ACT.Abs).then_inc(dt_raw_ready, 1)
            act.wait_ge(dt_raw_ready, 1)
            act.activation(dt_e, dt_e, ACT.Exp, scale=-1.0).then_inc(exp_dt_ready, 1)
            act.activation(neg_exp_a[:, :], cols[0:SSM_HEADS, COLS["a_log"]:COLS["a_log"] + 1], ACT.Exp) \
                .then_inc(exp_dt_ready, 1)
            round_weights(0, P_DT + 2, 0, T_DT + 1, 0)

            def window_exps():
                act.wait_ge(last_ready, 1)
                act.activation(dec_t[:, :], aux[1][:, 0:P], ACT.Exp).then_inc(win_ready2, 1)
                act.activation(win_t[:, :], win_t[:, :], ACT.Exp).then_inc(win_ready2, 1)

            def ssm_group(i, first):
                def grp_round(j):
                    round_weights(i, P_GRP + j // 2 + 2, 8, T_GRP + j + 1, 16)

                def bank_of(j):
                    act.wait_ge(tile_done, T_GRP + 16 * i + j + 1)
                    return gemm_bank[(T_GRP + j) % 4][:, :]

                def freed(j):
                    return bank_free[(T_GRP + j) % 4]

                def conv_start(q):
                    act.wait_ge(u_ready, 2 * i + q + 1)
                    act.activation(acc31[:, q, :], u_buf[:, q, :], ACT.Identity, bias=gc(G_CONV_B + q),
                                   scale=gc(G_CONV_W + CONV_TAPS * q + CONV_TAPS - 1)).then_inc(conv_init, 1)

                for q in range(2):
                    src = bank_of(2 * q + 1)
                    act.activation(u_buf[:, q, :], src, ACT.Sigmoid).then_inc(freed(2 * q + 1), 1)
                    grp_round(2 * q + 1)
                    if q == 0:
                        if not first:
                            act.wait_ge(gcol_ready, 6 * i + 6)
                            conv_start(0)
                    elif first:
                        window_exps()
                        act.wait_ge(gcol_ready, 6 * i + 6)
                        conv_start(0)
                conv_start(1)

                def c4_start(n):
                    j = 4 + n
                    src = bank_of(j)
                    if n >= 2:
                        act.wait_ge(silu_ready, 6 * i + n - 1)
                    act.activation(sq[:, n % 2, :], src, ACT.Identity, bias=gc(G_SSM_B + n),
                                   scale=gc(G_SSM_W + SSM_TAPS * n + SSM_TAPS - 1)).then_inc(c4_init, 1)

                def c4_end(n):
                    j = 4 + n
                    act.wait_ge(freed(j), free_value(T_GRP + j) + 4 * i)
                    if n < 4:
                        if n >= 2:
                            act.wait_ge(xst_done, 4 * i + n - 1)
                            act.wait_ge(xcopy, 4 * i + n - 1)
                        act.activation(e_row[n % 2], sq[:, n % 2, :], ACT.Silu).then_inc(silu_ready, 1)
                        act.wait_ge(silu_ready, 6 * i + n + 1)
                        act.activation(chunk(y_ssm, 4 * i + n), e_row[n % 2], ACT.Copy).then_inc(xcopy, 1)
                    else:
                        act.activation([b_t, c_t][n - 4], sq[:, n % 2, :], ACT.Silu).then_inc(silu_ready, 1)

                for n in range(6):
                    c4_start(n)
                    if n % 2 == 1:
                        grp_round(4 + n)
                    if n >= 1:
                        c4_end(n - 1)
                c4_end(5)
                src = bank_of(10)
                act.activation(chunk(g_conv, 2 * i), src, ACT.Copy).then_inc(freed(10), 1)
                act.wait_ge(bt_done, i + 1)
                act.activation(b_n, aux[0][:, :], ACT.Copy).then_inc(bn_ready, 1)
                src = bank_of(11)
                act.activation(chunk(g_conv, 2 * i + 1), src, ACT.Copy).then_inc(freed(11), 1)
                grp_round(11)

                def exp_row(hh):
                    act.wait_ge(row_done, 8 * i + hh + 1)
                    if hh >= 2:
                        act.wait_ge(y_done, 8 * i + hh - 1)
                    else:
                        act.wait_ge(xcopy, 4 * i + 4)
                    act.activation(e_row[hh % 2], aux[hh % 2][:, :], ACT.Exp).then_inc(e_ready, 1)

                def exp_seg(hh):
                    act.wait_ge(seg_ready, 8 * i + hh + 1)
                    act.activation(seg[hh % 2], seg[hh % 2], ACT.Exp).then_inc(segx_ready, 1)

                zbuf = [tmp[:, 0, :], tmp[:, 1, :], sq[:, 0, :], sq[:, 1, :]]

                z_after = (1, 4, 5, 7)

                def z_copy(q):
                    src = bank_of(12 + q)
                    act.activation(zbuf[q], src, ACT.Copy).then_inc(freed(12 + q), 1)
                    if q % 2 == 1:
                        grp_round(12 + q)

                for hh in range(GH):
                    exp_row(hh)
                    exp_seg(hh)
                    if hh in z_after:
                        z_copy(z_after.index(hh))
                for q in range(2):
                    act.wait_ge(tap[q], (CONV_TAPS - 1) * (i + 1))
                    act.activation(chunk(conv_u, 2 * i + q), acc31[:, q, :], ACT.Copy).then_inc(uc_ready, 1)
                for q in range(4):
                    act.wait_ge(freed(12 + q), free_value(T_GRP + 12 + q) + 4 * i)
                    act.activation(zbuf[q], zbuf[q], ACT.Silu).then_inc(z_ready, 1)

            ssm_group(0, True)
            with act.Fori(1, GROUPS) as i:
                ssm_group(i, False)

            def after(p, t):
                round_weights(0, p + 2, 0, t + 2, 0)

            load_table(ACT.Sqrt)
            act.wait_ge(yz_ready, 4 * GROUPS)
            for k in range(KC):
                act.wait_ge(centered, k + 1)
                act.activation(ln_sq[:, k, :], conv_u[:, k, :], ACT.Square).then_inc(sq_ready, 1)
            after(P_GATE, T_GATE)
            roots(5, sum_done, 6, e=1)
            load_table(ACT.Silu)
            for q in range(2):
                act.wait_ge(tap[q], (CONV_TAPS - 1) * GROUPS)

            def store_gate(j):
                t = T_GATE + j
                act.wait_ge(tile_done, t + 1)
                act.activation(g_ssm[:, j, :], gemm_bank[t % 4][:, :], ACT.Copy).then_inc(bank_free[t % 4], 1)

            for k in range(KC):
                act.wait_ge(ln_raw, k + 1)
                value = b_raw[:, k, :]
                act.activation(value, value, ACT.Silu, bias=col("conv_ln_b", k)).then_inc(ln_silu, 1)
                act.wait_ge(ln_silu, k + 1)
                act.activation(b_hi[:, k, :], value, ACT.Copy).then_inc(b_hi_ready, 1)
                if k in (1, 2):
                    store_gate(k - 1)
            for j in range(2, 4):
                store_gate(j)
            after(P_GATE + 1, T_GATE + 2)

            def group_squares(m):
                for k in range(4 * m, 4 * m + 4):
                    if m and k == 4 * m:
                        act.wait_ge(sq_read, m)
                    act.activation(y_sq[k % 4], y_ssm[:, k, :], ACT.Square).then_inc(sq_ready, 1)

            group_squares(0)
            for j in range(4):
                t = T_GATE + j
                act.wait_ge(bank_free[t % 4], free_value(t))
                act.activation(g_ssm[:, j, :], g_ssm[:, j, :], ACT.Sigmoid).then_inc(gs_ready, 1)
            for k in range(KC):
                act.activation(g_conv[:, k, :], g_conv[:, k, :], ACT.Sigmoid).then_inc(gc_ready, 1)
            for m in range(4):
                after(P_CONV + m, T_CONV + 2 * m)
                if m < 3:
                    group_squares(m + 1)
            load_table(ACT.Sqrt)
            act.wait_ge(sq_read, GROUPS)
            act.activation(group_root[:, :], aux[0][:, 0:GROUPS * QT], ACT.Sqrt, bias=eps[:, 0:1],
                           scale=1.0 / (4 * P)).then_inc(groot_ready, 1)

            for m in range(2):
                for j in range(2):
                    t = T_GATE2 + 2 * m + j
                    act.wait_ge(tile_done, t + 1)
                    act.activation(g_ssm[:, 4 + 2 * m + j, :], gemm_bank[t % 4][:, :], ACT.Sigmoid) \
                        .then_inc(bank_free[t % 4], 1)
                after(P_GATE2 + m, T_GATE2 + 2 * m)
                for k in range(4 * m, 4 * m + 4):
                    act.wait_ge(yop_raw, k + 1)
                    act.activation(b_hi[:, k, :], b_raw[:, k, :], ACT.Copy).then_inc(b_hi_ready, 1)
            for k in range(KC):
                act.wait_ge(yop_raw, KC + k + 1)
                act.activation(a_hi[:, k, :], a_raw[:, k, :], ACT.Copy).then_inc(a_hi_ready, 1)
            for m in range(4):
                for j in range(2):
                    t = T_SSM + 2 * m + j
                    act.wait_ge(tile_done, t + 1)
                    act.activation(ssm_out[:, 2 * m + j, :], gemm_bank[t % 4][:, :], ACT.Copy).then_inc(bank_free[t % 4], 1)
                after(P_SSM + m, T_SSM + 2 * m)
            for m in range(4):
                for k in range(2 * m, 2 * m + 2):
                    act.wait_ge(merged, k + 1)
                    act.activation(b_hi[:, k, :], b_raw[:, k, :], ACT.Copy).then_inc(b_hi_ready, 1)
                after(P_SSM + 4 + m, T_SSM + 8 + 2 * m)
            load_table(ACT.Sqrt)
            for k in range(KC):
                act.wait_ge(h_ready, 2 * KC + k + 1)
                act.wait_ge(sq_sum_step, 18 + max(k - 1, 0))
                act.activation(sq[:, k % 2, :], h[:, k, :], ACT.Square).then_inc(ysq_ready, 1)
                if k % 2 == 1 and k < KC - 1:
                    after(P_WOUT2 + k // 2, T_WOUT2 + k - 1)
            roots(6, sum_done, 7)
            after(P_WOUT2 + 3, T_WOUT2 + 6)
            operand_shifted(3, 24)

            def ffn_up(grp, i, j, p_it, t_it, n_it):
                p, t = P_FFN + grp * (FC + 8) + j, T_FFN + grp * (2 * FC + 8) + 2 * j
                n = FC * grp + j + n_it * i
                act.wait_ge(tile_done, t + t_it * i + 1)
                if grp or j >= 2:
                    act.wait_ge(f_lo_ready, n - 1)
                act.activation(ffn_t[(FC * grp + j) % 2], gemm_bank[t % 4][:, :], ACT.Silu).then_inc(bank_free[t % 4], 1)
                act.wait_ge(f_raw, n + 1)
                kk = j + n_it * i
                act.activation(chunk(f_hi, kk), ffn_raw[(FC * grp + j) % 2], ACT.Copy).then_inc(f_hi_ready, 1)
                round_weights(i, p + 2, p_it, t + 2, t_it)

            for grp in range(FFN_GROUPS):
                ffn_up(grp, 0, 0, 0, 0, 0), ffn_up(grp, 0, 1, 0, 0, 0)
                with act.Fori(0, FC // 2 - 1) as i:
                    ffn_up(grp, i, 2, 2, 4, 2), ffn_up(grp, i, 3, 2, 4, 2)
                ffn_up(grp, 0, FC - 1, 0, 0, 0)
                p0, t0 = P_FFN + grp * (FC + 8) + FC, T_FFN + grp * (2 * FC + 8) + 2 * FC
                if grp == FFN_GROUPS - 1:
                    load_table(ACT.Sqrt)
                for k in range(KC):
                    if grp == FFN_GROUPS - 1:
                        act.wait_ge(h_ready, 4 * KC + k + 1)
                        act.wait_ge(sq_sum_step, 26 + max(k - 1, 0))
                        act.activation(sq[:, k % 2, :], h[:, k, :], ACT.Square).then_inc(ysq_ready, 1)
                    if p0 + k + 2 < P_END:
                        round_weights(0, p0 + k + 2, 0, t0 + k + 1, 0)
            roots(7, sum_done, 8)

        @block.vector
        def _(dve):
            def inverse(n):
                dve.wait_ge(root_ready, n + 1)
                if n:
                    dve.wait_ge(rinv_ready, n)
                dve.reciprocal(rinv[:, :], root[:, :]).then_inc(rinv_ready, 1)

            def normed_shifted(n, q, base, part):
                inverse(n)
                dve.wait_ge(r_ready, n + 1)
                for k in range(KC):
                    dve.scalar_tensor_tensor(a_raw[:, k, :], h[:, k, :],
                                             gain2[:, KC * part + k:KC * part + k + 1], aux[1][:, :],
                                             ALU.mult, ALU.mult).then_inc(pre_raw, 1)
                for k in range(KC):
                    dve.wait_ge(a_hi_ready, base + k + 1)
                    dve.scalar_tensor_tensor(a_lo[:, k, :], a_raw[:, k, :],
                                             mod[:, 24 * part + k:24 * part + k + 1], a_hi[:, k, :].bitcast(F32),
                                             ALU.add, ALU.subtract).then_inc(a_lo_ready, 1)

            def low_parts(use, gain, chunks=range(KC)):
                for k in chunks:
                    dve.wait_ge(a_hi_ready, use + k + 1)
                    dve.scalar_tensor_tensor(a_lo[:, k, :], h[:, k, :], col(gain, k), a_hi[:, k, :].bitcast(F32),
                                             ALU.mult, ALU.subtract).then_inc(a_lo_ready, 1)

            def root_row(n):
                inverse(n)
                dve.wait_ge(r_ready, n + 1)
                dve.tensor_copy(r_row, aux[1][:, :]).then_inc(r_row_ready, 1)
                dve.wait_ge(r_row_ready, n // 2 + 1)

            def residual(n, gain, base, a_used):
                inverse(n)
                dve.wait_ge(r_ready, n + 1)
                dve.wait_ge(a_lo_ready, a_used)
                for k in range(KC + 1):
                    if k < KC:
                        if k >= 2:
                            dve.wait_ge(h_ready, base + k - 1)
                        dve.scalar_tensor_tensor(tmp[:, k % 2, :], y[:, k, :], col(gain, k), aux[1][:, :],
                                                 ALU.mult, ALU.mult).then_inc(post_step, 1)
                    if k >= 1:
                        dve.wait_ge(post_step, base + k)
                        dve.tensor_tensor(h[:, k - 1, :], h[:, k - 1, :], tmp[:, (k - 1) % 2, :], ALU.add) \
                            .then_inc(h_ready, 1)

            for b in range(4):
                dve.sem_inc(bank_free[b], 1)
            dve.sem_inc(b_lo_ready, 1)
            dve.memset(eps[:, 0:1], EPS).then_inc(dve_consts, 1)
            dve.memset(eps[:, 1:2], LN_EPS).then_inc(dve_consts, 1)
            for k in range(HEADS):
                dve.memset(slopes[:, k:k + 1], -(2.0 ** (-8.0 * (k + 1) / HEADS))).then_inc(dve_consts, 1)
            dve.wait_ge(params_loaded, 16)
            for k in range(KC):
                low_parts(0, "norm_mix_pre", (k,))
                if 1 <= k < KC - 1:
                    add_squares(dve, 0, (k,))
            dve.wait_ge(consts, 3)
            dve.reciprocal(recip_count[:, :], recip_count[:, :]).then_inc(dve_consts, 1)
            dve.wait_ge(dve_consts, HEADS + 3)
            root_row(0)

            with dve.Fori(0, PAIRS) as i:
                def store(j, dst):
                    dve.wait_ge(tile_done, 8 * i + j + 1)
                    dve.tensor_tensor(dst, gemm_bank[j % 4][:, :], r_row, ALU.mult).then_inc(bank_free[j % 4], 1)

                dve.wait_ge(tile_done, 8 * i + 1)
                dve.scalar_tensor_tensor(q_s, gemm_bank[0][:, :], HEAD ** -0.5, r_row, ALU.mult, ALU.mult) \
                    .then_inc(bank_free[0], 1)
                store(1, k_s)
                store(2, v_s)
                for head in range(2):
                    for qt in range(QT + 1):
                        if qt < QT:
                            u = 4 * head + qt
                            n = P * (qt + 1)
                            dve.wait_ge(s_done, 8 * i + u + 1)
                            if head == 1:
                                dve.wait_ge(t_done, 9 * i + 5)
                            dve.scalar_tensor_tensor(probs[:, qt, 0:n], dist[:, S - n:S], slopes[:, bass.ds(2 * i + head, 1)],
                                                     aux[u % 2][:, 0:n], ALU.mult, ALU.add).then_inc(s_read, 1)
                            dve.wait_ge(s_read, 8 * i + u + 1)
                            dve.tensor_reduce(neg_max[:, u:u + 1], probs[:, qt, 0:n], AX.X, ALU.max, negate=True) \
                                .then_inc(max_ready, 1)
                        if qt >= 1:
                            u = 4 * head + qt - 1
                            n = P * qt
                            dve.wait_ge(exp_ready, 8 * i + u + 1)
                            dve.reciprocal(row_inv[:, u:u + 1], row_sum[:, u:u + 1]).then_inc(inv_step, 1)
                            dve.wait_ge(inv_step, 8 * i + u + 1)
                            dve.tensor_scalar(probs[:, qt - 1, 0:n], probs[:, qt - 1, 0:n], row_inv[:, u:u + 1], None,
                                              ALU.mult).then_inc(probs_ready, 1)
                        if head == 0 and qt == 1:
                            store(3, chunk(pool_x, i))
                    if head == 0:
                        store(4, chunk(gates, 4 * i))
                        store(5, chunk(gates, 4 * i + 1))
                store(6, chunk(gates, 4 * i + 2))
                store(7, chunk(gates, 4 * i + 3))
                dve.wait_ge(b_hi_ready, i + 1)
                dve.tensor_tensor(chunk(b_lo, i), aux[3][:, :], chunk(b_hi, i).bitcast(F32), ALU.subtract) \
                    .then_inc(b_lo_ready, 1)

            steps = 0
            dve.wait_ge(bank_free[3], 1 + 2 * PAIRS)
            for g in range(4):
                src = pool_x[:, g, :]
                if g:
                    dve.wait_ge(win_ready, g)
                for lvl in range(g + 1):
                    d = 1 << lvl
                    dst = win[lvl % 2]
                    dve.tensor_copy(dst[:, 0:d], src[:, 0:d]).then_inc(win_step, 1)
                    dve.tensor_tensor(dst[:, d:S], src[:, d:S], src[:, 0:S - d], ALU.add).then_inc(win_step, 1)
                    steps += 2
                    dve.wait_ge(win_step, steps)
                    src = dst
                w = 2 << g
                head_w = win[(g + 1) % 2]
                dve.tensor_tensor(head_w[:, 0:w - 1], src[:, 0:w - 1], recip_count[:, 0:w - 1], ALU.mult) \
                    .then_inc(win_step, 1)
                steps += 1
                dve.wait_ge(win_step, steps)
                dve.tensor_tensor(pool_x[:, g, 0:w - 1], head_w[:, 0:w - 1], pool_x[:, g, 0:w - 1], ALU.subtract) \
                    .then_inc(win_step, 1)
                steps += 1
                dve.wait_ge(win_step, steps)
                dve.scalar_tensor_tensor(pool_x[:, g, w - 1:S], src[:, w - 1:S], 1.0 / w, pool_x[:, g, w - 1:S],
                                         ALU.mult, ALU.subtract).then_inc(win_ready, 1)
            for g in range(4):
                dve.wait_ge(b_hi_ready, 4 + g + 1)
                dve.scalar_tensor_tensor(b_lo[:, 4 + g, :], aux[g][:, :], col("pool_scale", g),
                                         b_hi[:, 4 + g, :].bitcast(F32), ALU.mult, ALU.subtract).then_inc(b_lo_ready, 1)
            dve.wait_ge(gate_ready, 2 * KC)
            for m in range(KC):
                if m == 0:
                    for b in range(4):
                        dve.wait_ge(bank_free[b], 1 + (T_BRANCH + 8) // 4)
                dve.tensor_tensor(gates[:, 8 + m, :], gates[:, 8 + m, :], y_attn[:, m, :], ALU.mult).then_inc(m_step, 1)
                dve.wait_ge(tile_done, T_BRANCH + 8 + m + 1)
                dve.tensor_tensor(gates[:, m, :], gates[:, m, :], gemm_bank[m % 4][:, :], ALU.mult).then_inc(bank_free[m % 4], 1)
                dve.wait_ge(m_step, m + 1)
                dve.wait_ge(bank_free[m % 4], 1 + (T_BRANCH + 8 + m) // 4 + 1)
                dve.tensor_tensor(a_raw[:, m, :], gates[:, 8 + m, :], gates[:, m, :], ALU.add).then_inc(m_ready, 1)
                for k in range(max(m - 1, 0), m if m < KC - 1 else KC):
                    dve.wait_ge(a_hi_ready, KC + k + 1)
                    dve.tensor_tensor(a_lo[:, k, :], a_raw[:, k, :], a_hi[:, k, :].bitcast(F32), ALU.subtract) \
                        .then_inc(a_lo_ready, 1)

            dve.memset(sq_sum, 0.0).then_inc(sq_sum_step, 1)
            with dve.Fori(0, 2) as i:
                for j in range(4):
                    dve.wait_ge(ysq_ready, 4 * i + j + 1)
                    dve.wait_ge(sq_sum_step, 4 * i + j + 1)
                    dve.tensor_tensor(sq_sum, sq_sum, sq[:, j % 2, :], ALU.add).then_inc(sq_sum_step, 1)
            for b in range(4):
                dve.wait_ge(bank_free[b], 1 + (T_WOUT + 8) // 4)
            residual(1, "norm_mix_post", 0, 16)
            low_parts(2 * KC, "norm_mlp_pre")
            root_row(2)

            def mlp(i, first, last):
                for j in range(8):
                    t = T_MLP + j
                    dve.wait_ge(tile_done, t + 16 * i + 1)
                    if j >= 2:
                        dve.wait_ge(b_hi_ready, 8 + 8 * i + j - 1)
                    dve.scalar_tensor_tensor(relu[j % 2], gemm_bank[t % 4][:, :], 0.0, r_row, ALU.max, ALU.mult) \
                        .then_inc(relu_ready, 1)
                    dve.wait_ge(relu_ready, 8 * i + j + 1)
                    dve.sem_inc(bank_free[t % 4], 1)
                    dve.tensor_tensor(act_raw[j % 2], relu[j % 2], relu[j % 2], ALU.mult).then_inc(act_step, 1)
                    dve.wait_ge(act_step, 8 * i + j + 1)
                    dve.wait_ge(b_hi_ready, 8 + 8 * i + j + 1)
                    dve.tensor_tensor(b_lo[:, j, :], act_raw[j % 2], b_hi[:, j, :].bitcast(F32), ALU.subtract) \
                        .then_inc(b_lo_ready, 1)
                    dve.wait_ge(ada_loaded[j % 2], 16 * (4 * i + j // 2 + 1))
                    if j == 0:
                        dve.tensor_scalar(ada_acc, ada_w[0], c_silu[:, 0:1], None, ALU.mult).then_inc(ada_used, 1)
                    else:
                        dve.wait_ge(ada_used, ADA_PIECES * i + j)
                        dve.scalar_tensor_tensor(ada_acc, ada_w[j % 2], c_silu[:, j:j + 1], ada_acc,
                                                 ALU.mult, ALU.add).then_inc(ada_used, 1)
                for j in range(8):
                    t = T_MLP + 8 + j
                    bank = gemm_bank[t % 4][:, :]
                    dve.wait_ge(tile_done, t + 16 * i + 1)
                    if first:
                        dve.tensor_copy(y[:, j, :], bank).then_inc(y_step, 1)
                    else:
                        dve.tensor_tensor(y[:, j, :], y[:, j, :], bank, ALU.add).then_inc(y_step, 1)
                    dve.wait_ge(y_step, 8 * i + j + 1)
                    dve.sem_inc(bank_free[t % 4], 1)
                    if j == 5:
                        dve.wait_ge(mod_done, i + 1)
                        dve.tensor_tensor(mod[:, bass.ds(12 * i, 12)], aux[2][:, 0:12],
                                          cols[:, bass.ds(COLS["b_ada"] + 12 * i, 12)], ALU.add).then_inc(mod_ready, 1)
                    if last and j < 7:
                        dve.wait_ge(ysq_ready, 8 + j + 1)
                        dve.wait_ge(sq_sum_step, 10 + j)
                        dve.tensor_tensor(sq_sum, sq_sum, sq[:, j % 2, :], ALU.add).then_inc(sq_sum_step, 1)

            dve.wait_ge(c_ready, 1)
            mlp(0, True, False)
            with dve.Fori(1, MLP_GROUPS - 1) as i:
                mlp(i, False, False)
            dve.memset(sq_sum, 0.0).then_inc(sq_sum_step, 1)
            mlp(MLP_GROUPS - 1, False, True)
            residual(3, "norm_mlp_post", 8, 24)
            dve.wait_ge(mod_ready, MLP_GROUPS)
            for part, name in enumerate(("norm_mix_w", "norm_ffn_w")):
                dve.scalar_tensor_tensor(gain2[:, KC * part:KC * part + KC], mod[:, 24 * part + KC:24 * part + 2 * KC], 1.0,
                                         cols[:, COLS[name]:COLS[name] + KC], ALU.add, ALU.mult).then_inc(gain2_ready, 1)
            dve.wait_ge(gain2_ready, 2)
            dve.wait_ge(h_ready, 2 * KC)
            normed_shifted(4, 2, 3 * KC, 0)

            n = 0

            def step(ins):
                nonlocal n
                ins.then_inc(dt_step, 1)
                n += 1
                dve.wait_ge(dt_step, n)

            dve.wait_ge(exp_dt_ready, 2)
            step(dve.tensor_scalar(dt_s, dt_e, 2.0, None, ALU.add))
            step(dve.reciprocal(dt_s, dt_s))
            step(dve.tensor_tensor(dt_s, dt_s, dt_e, ALU.mult))
            step(dve.tensor_tensor(dt_q, dt_s, dt_s, ALU.mult))
            step(dve.tensor_scalar(dt_p, dt_q, 1.0 / 17, None, ALU.mult))
            for odd in range(15, 1, -2):
                step(dve.scalar_tensor_tensor(dt_p, dt_p, 1.0 / odd, dt_q, ALU.add, ALU.mult))
            step(dve.scalar_tensor_tensor(dt_p, dt_p, 1.0, dt_s, ALU.add, ALU.mult))
            step(dve.tensor_scalar(dt_x, dt_x, 0.0, None, ALU.max))
            step(dve.scalar_tensor_tensor(dt_row, dt_p, 2.0, dt_x, ALU.mult, ALU.add))
            step(dve.tensor_scalar(dt_p, dt_row, neg_exp_a[:, 0:1], -1.0, ALU.mult, ALU.mult))
            for c in range(QT):
                dve.tensor_tensor_scan(cum[:, c * P:(c + 1) * P], ones[0:SSM_HEADS, :], dt_p[:, c * P:(c + 1) * P],
                                       0.0, ALU.mult, ALU.add).then_inc(cum_step, 1)
            dve.wait_ge(cum_step, QT)
            dve.tensor_copy(cum_hi[:, :], cum[:, :]).then_inc(cum_split, 1)
            dve.wait_ge(cum_split, 1)
            dve.tensor_tensor(cum_lo[:, :], cum[:, :], cum_hi[:, :].bitcast(F32), ALU.subtract).then_inc(cum_split, 1)
            dve.wait_ge(dtt_done, 1)
            dve.tensor_copy(cum_t[:, :], aux[0][:, 0:P]).then_inc(dtt_ready, 1)
            dve.tensor_copy(dt_t[:, :], aux[0][:, P:2 * P]).then_inc(dtt_ready, 1)
            dve.wait_ge(dtt_ready, 2)
            dve.wait_ge(last_done, 1)
            dve.tensor_tensor(win_t[:, :], aux[1][:, 0:P], cum_t[:, :], ALU.subtract).then_inc(last_ready, 1)
            dve.wait_ge(win_ready2, 2)

            def ssm_group(i, first):
                def done(j):
                    dve.wait_ge(tile_done, T_GRP + 16 * i + j + 1)
                    return gemm_bank[(T_GRP + j) % 4][:, :]

                def freed(j):
                    return bank_free[(T_GRP + j) % 4]

                next_tap = [1, 1]

                def taps(count, chunks=(0, 1)):
                    for _ in range(count):
                        q = min(chunks, key=lambda c: next_tap[c])
                        d = next_tap[q]
                        next_tap[q] += 1
                        if d == 1:
                            dve.wait_ge(conv_init, 2 * i + q + 1)
                        else:
                            dve.wait_ge(tap[q], (CONV_TAPS - 1) * i + d - 1)
                        dve.scalar_tensor_tensor(acc31[:, q, d:S], u_buf[:, q, 0:S - d],
                                                 gc(G_CONV_W + CONV_TAPS * q + CONV_TAPS - 1 - d), acc31[:, q, d:S],
                                                 ALU.mult, ALU.add).then_inc(tap[q], 1)

                dve.tensor_copy(gcol[:, :], cols[:, bass.ds(COLS["group"] + GCOLS * i, GCOLS)]).then_inc(gcol_ready, 1)
                for dst, src in ((cum_g, cum_t), (dt_g, dt_t), (win_g, win_t), (dec_g, dec_t)):
                    dve.tensor_copy(dst[:, :, :], src[:, :].rearrange("p (c h) -> p c h", c=QT)[:, :, bass.ds(GH * i, GH)]) \
                        .then_inc(gcol_ready, 1)
                dve.tensor_copy(sel_g[:, :], ident[0:SSM_HEADS, bass.ds(GH * i, GH)]).then_inc(gcol_ready, 1)
                dve.wait_ge(gcol_ready, 6 * i + 6)
                for q in range(2):
                    src = done(2 * q + 1)
                    dve.wait_ge(freed(2 * q + 1), free_value(T_GRP + 2 * q + 1) + 4 * i)
                    src = done(2 * q)
                    dve.tensor_tensor(u_buf[:, q, :], u_buf[:, q, :], src, ALU.mult).then_inc(u_ready, 1)
                    dve.wait_ge(u_ready, 2 * i + q + 1)
                    dve.sem_inc(freed(2 * q), 1)
                    taps((11, 8)[q], (q,))

                def conv4(n):
                    j = 4 + n
                    acc = sq[:, n % 2, :]
                    bank = gemm_bank[(T_GRP + j) % 4][:, :]
                    dve.wait_ge(c4_init, 6 * i + n + 1)
                    for d in range(1, SSM_TAPS):
                        ins = dve.scalar_tensor_tensor(acc[:, d:S], bank[:, 0:S - d],
                                                       gc(G_SSM_W + SSM_TAPS * n + SSM_TAPS - 1 - d), acc[:, d:S],
                                                       ALU.mult, ALU.add)
                        if d < SSM_TAPS - 1:
                            ins.then_inc(c4_step, 1)
                            dve.wait_ge(c4_step, 12 * i + 2 * n + d)
                        else:
                            ins.then_inc(freed(j), 1)

                def x_times_dt(k):
                    dve.wait_ge(xst_done, 4 * i + k + 1)
                    heads = lambda ap: ap.rearrange("p c (h f) -> p c h f", h=2)
                    dve.tensor_tensor(heads(x_dt[:, :, k * P:(k + 1) * P]),
                                      heads(aux[k % 2][:, :].rearrange("p (c f) -> p c f", c=QT)),
                                      dt_g[:, :, 2 * k:2 * k + 2].unsqueeze(3).to_broadcast([P, QT, 2, HEAD]),
                                      ALU.mult).then_inc(xdt_ready, 1)

                def per_head(ap, vals):
                    return ap.rearrange("p (h f) -> p h f", h=GH), vals.unsqueeze(2).to_broadcast([P, GH, HEAD])

                def x_window(c):
                    a, b = per_head(x_dt[:, c, :], win_g[:, c, :])
                    dst = x_win[c]
                    if c == 0:
                        dve.wait_ge(xdt_ready, 4 * i + 4)
                    dve.tensor_tensor(dst.rearrange("p (h f) -> p h f", h=GH), a, b, ALU.mult).then_inc(xw_ready, 1)

                def next_state(c):
                    dve.wait_ge(st_done, 3 * i + c + 1)
                    bank = aux[2 + c % 2][:, :]
                    if c == 0:
                        dve.tensor_copy(state[:, 0, :], bank).then_inc(st_ready, 1)
                        return
                    dve.wait_ge(st_ready, 3 * i + c)
                    a, b = per_head(state[:, c - 1, :], dec_g[:, c, :])
                    dve.tensor_tensor(state[:, c, :].rearrange("p (h f) -> p h f", h=GH), a, b, ALU.mult) \
                        .then_inc(st_step, 1)
                    dve.wait_ge(st_step, 2 * i + c)
                    dve.tensor_tensor(state[:, c, :], state[:, c, :], bank, ALU.add).then_inc(st_ready, 1)

                def segments(hh):
                    dve.wait_ge(e_ready, 8 * i + hh + 1)
                    if hh >= 2:
                        dve.wait_ge(y_done, 8 * i + hh - 1)
                    if hh < 2:
                        dve.wait_ge(st_done, 3 * i + hh + 1)
                    for c in range(QT):
                        t_ = slice(c * P, (c + 1) * P)
                        ins = dve.tensor_scalar(seg[hh % 2][:, t_], aux[hh % 2][:, t_], cum_g[:, c, hh:hh + 1], 0.0,
                                                ALU.subtract, ALU.min)
                        if c < QT - 1:
                            ins.then_inc(seg_step, 1)
                        else:
                            ins.then_inc(seg_ready, 1)

                def weigh(hh):
                    dve.wait_ge(segx_ready, 8 * i + hh + 1)
                    dve.tensor_tensor(seg[hh % 2], seg[hh % 2], cb, ALU.mult).then_inc(mt_ready, 1)
                    dve.tensor_tensor(e_row[hh % 2], e_row[hh % 2], c_t, ALU.mult).then_inc(ce_ready, 1)

                def skip(k):
                    dve.wait_ge(y_done, 8 * i + 2 * k + 2)
                    dve.wait_ge(xcopy, 4 * i + k + 1)
                    yk = chunk(y_ssm, 4 * i + k)
                    dve.scalar_tensor_tensor(yk, yk, gc(G_D + k), aux[2 + k % 2][:, :], ALU.mult, ALU.add) \
                        .then_inc(yskip, 1)

                for n in range(6):
                    conv4(n)
                    taps(4)
                    if n >= 2:
                        x_times_dt(n - 2)
                for c in range(3):
                    x_window(c)
                taps(6)
                dve.wait_ge(cb_done, i + 1)
                dve.tensor_tensor(cb.rearrange("p (c l) -> p c l", c=QT), aux[1][:, :].rearrange("p (c l) -> p c l", c=QT),
                                  causal[:, :].unsqueeze(1).to_broadcast([P, QT, P]), ALU.mult).then_inc(cbm_ready, 1)
                dve.wait_ge(cbm_ready, i + 1)
                segments(0)
                next_state(0)
                next_state(1)
                weigh(0)
                segments(1)
                next_state(2)
                weigh(1)
                taps(4)
                for hh in range(2, GH):
                    segments(hh)
                    taps((2, 1, 1, 1, 1, 1)[hh - 2])
                    weigh(hh)
                    if hh % 2 == 1:
                        skip((hh - 3) // 2)
                assert next_tap == [CONV_TAPS, CONV_TAPS]
                for q in range(2):
                    dve.wait_ge(tap[q], (CONV_TAPS - 1) * (i + 1))
                if first:
                    dve.tensor_tensor(u_sum, acc31[:, 0, :], acc31[:, 1, :], ALU.add).then_inc(u_sum_step, 1)
                else:
                    for q in range(2):
                        dve.wait_ge(u_sum_step, 2 * i - 1 + q)
                        dve.tensor_tensor(u_sum, u_sum, acc31[:, q, :], ALU.add).then_inc(u_sum_step, 1)
                skip(3)
                for q in range(4):
                    dve.wait_ge(z_ready, 4 * i + q + 1)
                    dve.wait_ge(yskip, 4 * i + q + 1)
                    yk = chunk(y_ssm, 4 * i + q)
                    dve.tensor_tensor(yk, yk, [tmp[:, 0, :], tmp[:, 1, :], sq[:, 0, :], sq[:, 1, :]][q], ALU.mult) \
                        .then_inc(yz_ready, 1)

            ssm_group(0, True)
            with dve.Fori(1, GROUPS) as i:
                ssm_group(i, False)

            dve.wait_ge(mean_done, 1)
            dve.tensor_scalar(neg_mean[:, :], aux[0][:, 0:QT], -1.0 / D, None, ALU.mult).then_inc(mean_ready, 1)
            dve.wait_ge(mean_spread, 1)
            for k in range(KC + 2):
                if k < KC:
                    dve.tensor_tensor(conv_u[:, k, :], conv_u[:, k, :], aux[1][:, :], ALU.add).then_inc(centered, 1)
                if k >= 2:
                    dve.wait_ge(sq_ready, 3 * KC + k - 1)
                    if k == 3:
                        dve.tensor_tensor(ln_sum, ln_sq[:, 0, :], ln_sq[:, 1, :], ALU.add).then_inc(ln_sum_step, 1)
                    elif k > 3:
                        dve.wait_ge(ln_sum_step, k - 3)
                        dve.tensor_tensor(ln_sum, ln_sum, ln_sq[:, k - 2, :], ALU.add).then_inc(ln_sum_step, 1)
            inverse(5)
            dve.wait_ge(r_ready, 6)
            dve.wait_ge(centered, KC)
            dve.wait_ge(yz_ready, 4 * GROUPS)
            for k in range(KC):
                dve.scalar_tensor_tensor(b_raw[:, k, :], conv_u[:, k, :], col("conv_ln_w", k), aux[1][:, :],
                                         ALU.mult, ALU.mult).then_inc(ln_raw, 1)
            for k in range(KC):
                dve.wait_ge(b_hi_ready, B_USE_CONV + k + 1)
                dve.tensor_tensor(b_lo[:, k, :], b_raw[:, k, :], b_hi[:, k, :].bitcast(F32),
                                  ALU.subtract).then_inc(b_lo_ready, 1)
            for k in range(KC):
                t = T_CONV + k
                if k % 2 == 0:
                    for n in range(1, 4):
                        dve.wait_ge(sq_ready, 4 * KC + 2 * k + n + 1)
                        if n > 1:
                            dve.wait_ge(group_step, 3 * (k // 2) + n - 1)
                        dve.tensor_tensor(y_sq[0], y_sq[0], y_sq[n], ALU.add).then_inc(group_step, 1)
                dve.wait_ge(gc_ready, k + 1)
                dve.wait_ge(tile_done, t + 1)
                dve.tensor_tensor(g_conv[:, k, :], g_conv[:, k, :], gemm_bank[t % 4][:, :], ALU.mult) \
                    .then_inc(bank_free[t % 4], 1)
            dve.wait_ge(groot_ready, 1)
            dve.reciprocal(group_inv[:, :], group_root[:, :]).then_inc(ginv_ready, 1)

            def y_operand(first, value, hi, hi_sem, hi_base, lo, lo_sem, spreads):
                dve.wait_ge(gspread_done, spreads)
                for k in range(KC):
                    f = first + k
                    dve.scalar_tensor_tensor(value[:, k, :], y_ssm[:, f, :], col("ssm_norm_w", f),
                                             aux[f // 4][:, :], ALU.mult, ALU.mult).then_inc(yop_raw, 1)
                for k in range(KC):
                    dve.wait_ge(hi_sem, hi_base + k + 1)
                    dve.tensor_tensor(lo[:, k, :], value[:, k, :], hi[:, k, :].bitcast(F32),
                                      ALU.subtract).then_inc(lo_sem, 1)

            dve.wait_ge(ln_silu, KC)
            dve.wait_ge(tile_done, T_GATE2)
            y_operand(8, b_raw, b_hi, b_hi_ready, B_USE_SSM, b_lo, b_lo_ready, 2)
            dve.wait_ge(tile_done, T_SSM)
            dve.wait_ge(b_lo_ready, B_USE_SSM + 1 + KC)
            y_operand(0, a_raw, a_hi, a_hi_ready, A_USE_SSM, a_lo, a_lo_ready, 4)
            for k in range(KC + 1):
                if k < KC:
                    t = T_SSM + 8 + k
                    t1 = T_SSM + k
                    dve.wait_ge(tile_done, t + 1)
                    dve.wait_ge(bank_free[t1 % 4], free_value(t1))
                    dve.tensor_tensor(ssm_out[:, k, :], ssm_out[:, k, :], gemm_bank[t % 4][:, :], ALU.add) \
                        .then_inc(bank_free[t % 4], 1)
                    dve.wait_ge(bank_free[t % 4], free_value(t))
                    dve.tensor_tensor(ssm_out[:, k, :], ssm_out[:, k, :], g_ssm[:, k, :], ALU.mult).then_inc(ssm_step, 1)
                    dve.wait_ge(ssm_step, k + 1)
                    dve.tensor_tensor(b_raw[:, k, :], ssm_out[:, k, :], g_conv[:, k, :], ALU.add).then_inc(merged, 1)
                if k >= 1:
                    dve.wait_ge(b_hi_ready, B_USE_WOUT + k)
                    dve.tensor_tensor(b_lo[:, k - 1, :], b_raw[:, k - 1, :], b_hi[:, k - 1, :].bitcast(F32),
                                      ALU.subtract).then_inc(b_lo_ready, 1)

            def add_gated(k, t, part, n, done_count):
                dve.wait_ge(tile_done, done_count)
                dve.wait_ge(h_ready, n - KC + 1)
                hk = chunk(h, k)
                c = 24 * part + 16 + k
                g_ = mod[:, c:c + 1] if isinstance(c, int) else mod[:, bass.ds(c, 1)]
                dve.scalar_tensor_tensor(hk, gemm_bank[t % 4][:, :], g_, hk, ALU.mult, ALU.add).then_inc(h_ready, 1)
                dve.wait_ge(h_ready, n + 1)
                dve.sem_inc(bank_free[t % 4], 1)

            def add_square(k, first, n):
                dve.wait_ge(ysq_ready, n + k + 1)
                dve.wait_ge(sq_sum_step, first + k)
                dve.tensor_tensor(sq_sum, sq_sum, sq[:, k % 2, :], ALU.add).then_inc(sq_sum_step, 1)

            dve.memset(sq_sum, 0.0).then_inc(sq_sum_step, 1)
            for k in range(KC):
                add_gated(k, T_WOUT2 + k, 0, 2 * KC + k, T_WOUT2 + k + 1)
                if k >= 1:
                    add_square(k - 1, 18, 16)
            dve.wait_ge(b_lo_ready, B_USE_WOUT + 1 + KC)
            dve.wait_ge(h_ready, 3 * KC)
            normed_shifted(6, 3, A_USE_FFN, 1)

            def ffn_up(grp, i, j, t_it, n_it):
                t = T_FFN + grp * (2 * FC + 8) + 2 * j
                n = FC * grp + j + n_it * i
                s = (FC * grp + j) % 2
                dve.wait_ge(tile_done, t + t_it * i + 2)
                dve.wait_ge(bank_free[t % 4], free_value(t) + (t_it // 4) * i)
                if grp or j >= 2:
                    dve.wait_ge(f_lo_ready, n - 1)
                dve.tensor_tensor(ffn_raw[s], ffn_t[s], gemm_bank[(t + 1) % 4][:, :], ALU.mult).then_inc(f_raw, 1)
                dve.wait_ge(f_raw, n + 1)
                dve.sem_inc(bank_free[(t + 1) % 4], 1)
                dve.wait_ge(f_hi_ready, n + 1)
                kk = j + n_it * i
                dve.tensor_tensor(chunk(f_lo, kk), ffn_raw[s], chunk(f_hi, kk).bitcast(F32), ALU.subtract) \
                    .then_inc(f_lo_ready, 1)

            for grp in range(FFN_GROUPS):
                ffn_up(grp, 0, 0, 0, 0), ffn_up(grp, 0, 1, 0, 0)
                with dve.Fori(0, FC // 2 - 1) as i:
                    ffn_up(grp, i, 2, 4, 2), ffn_up(grp, i, 3, 4, 2)
                ffn_up(grp, 0, FC - 1, 0, 0)
                if grp == FFN_GROUPS - 1:
                    dve.memset(sq_sum, 0.0).then_inc(sq_sum_step, 1)
                t0 = T_FFN + grp * (2 * FC + 8) + 2 * FC
                for k in range(KC):
                    add_gated(k, t0 + k, 1, (3 + grp) * KC + k, t0 + k + 1)
                    if grp == FFN_GROUPS - 1 and k >= 1:
                        add_square(k - 1, 26, 24)
            inverse(7)
            dve.wait_ge(r_ready, 8)
            dve.wait_ge(h_ready, 5 * KC)
            dve.wait_ge(f_lo_ready, FFN_GROUPS * FC)
            for k in range(KC):
                dve.scalar_tensor_tensor(arena[:, k, :], h[:, k, :], col("final_norm_w", k), aux[1][:, :],
                                         ALU.mult, ALU.mult).then_inc(out_raw, 1)


def panels(w, kc, mc):
    n = w.shape[1] // (mc * P)
    return w.reshape(kc, P, n, mc * P).transpose(2, 1, 0, 3).reshape(n, P, kc * mc * P)


INPUTS = """x norm_mix_pre w_in b_gate pool_w pool_scale w_branch_pool w_branch_attn w_out norm_mix_post
norm_mlp_pre w_up w_down norm_mlp_post c_2 w_ada_mix_2 b_ada_mix_2 norm_mix_w_2 w_in_2 conv_dw_w_2 conv_dw_b_2
conv_ln_w_2 conv_ln_b_2 w_conv_out_2 ssm_conv_w_2 ssm_conv_b_2 dt_bias_2 a_log_2 d_skip_2 ssm_norm_w_2 w_ssm_out_2
w_out_2 w_ada_ffn_2 b_ada_ffn_2 norm_ffn_w_2 w_ffn_in_2 w_ffn_down_2 final_norm_w_2""".split()


def weight_stream(v):
    def pick(w, chunks):
        return np.concatenate([w[:, c * P:(c + 1) * P] for c in chunks], axis=1)

    w_in, up, down = v["w_in"], v["w_up"], v["w_down"]
    stream = [panels(pick(w_in, [4 + i, 8 + i, 12 + i, i] + [16 + 4 * i + j for j in range(4)]), KC, 2)
              for i in range(PAIRS)]
    stream += [panels(v["w_branch_attn"], 4, 4), panels(v["w_branch_pool"], 4, 4), panels(v["w_out"], KC, 2)]
    for g in range(MLP_GROUPS):
        stream += [panels(up[:, g * D:(g + 1) * D], KC, 2), panels(down[g * D:(g + 1) * D, :], KC, 2)]
    w = v["w_in_2"]
    z0, x0 = 16, 32
    dt0 = (x0 + 24) * P
    dt = np.zeros((D, 2 * P), np.float32)
    dt[:, 0:SSM_HEADS] = w[:, dt0:dt0 + SSM_HEADS]
    stream.append(panels(dt, KC, 2))
    gates = w[:, dt0 + SSM_HEADS:]
    for g in range(GROUPS):
        stream.append(panels(pick(w, [2 * g, 8 + 2 * g, 2 * g + 1, 8 + 2 * g + 1]
                                  + [x0 + 4 * g + j for j in range(4)] + [x0 + 16 + g, x0 + 20 + g]), KC, 2))
        stream.append(panels(pick(gates, [2 * g, 2 * g + 1]), KC, 2))
        stream.append(panels(pick(w, [z0 + 4 * g + j for j in range(4)]), KC, 2))
    stream += [panels(pick(gates, range(8, 12)), KC, 2), panels(v["w_conv_out_2"], KC, 2),
               panels(pick(gates, range(12, 16)), KC, 2),
               panels(v["w_ssm_out_2"][D:], KC, 2), panels(v["w_ssm_out_2"][:D], KC, 2), panels(v["w_out_2"], KC, 2)]
    ffn, ffn_down = v["w_ffn_in_2"], v["w_ffn_down_2"]
    for g in range(FFN_GROUPS):
        chunks = range(FC * g, FC * g + FC)
        stream.append(panels(pick(ffn, [c + half for c in chunks for half in (0, FFN_GROUPS * FC)]), KC, 2))
        rows = np.zeros((16 * P, D), np.float32)
        rows[:FC * P] = ffn_down[FC * P * g:FC * P * (g + 1)]
        stream.append(panels(rows, 16, 1))
    return np.ascontiguousarray(np.concatenate(stream, axis=0))


def columns(v):
    def cols(a):
        return a.reshape(-1, P).T

    def heads(a):
        out = np.zeros((P, 1), np.float32)
        out[:SSM_HEADS, 0] = a
        return out

    parts = [cols(v[n]) for n in ("norm_mix_pre", "b_gate", "pool_scale", "norm_mix_post", "norm_mlp_pre",
                                  "norm_mlp_post", "b_ada_mix_2", "b_ada_ffn_2", "norm_mix_w_2", "norm_ffn_w_2",
                                  "final_norm_w_2", "conv_ln_w_2", "conv_ln_b_2", "ssm_norm_w_2", "c_2")]
    parts += [heads(v["dt_bias_2"]), heads(v["a_log_2"])]
    wide = v["conv_dw_w_2"].reshape(CONV_TAPS, KC, P).transpose(2, 1, 0)
    short = v["ssm_conv_w_2"].reshape(SSM_TAPS, 24, P).transpose(2, 1, 0)
    wide_b, short_b = cols(v["conv_dw_b_2"]), cols(v["ssm_conv_b_2"])
    d = cols(np.repeat(v["d_skip_2"], HEAD))
    for g in range(GROUPS):
        own = [4 * g + j for j in range(4)] + [16 + g, 20 + g]
        parts += [wide[:, 2 * g:2 * g + 2].reshape(P, -1), wide_b[:, 2 * g:2 * g + 2], short[:, own].reshape(P, -1),
                  short_b[:, own], d[:, 4 * g:4 * g + 4]]
    return np.ascontiguousarray(np.concatenate(parts, axis=1))


def kernel(**inputs):
    import concourse.bacc as bacc
    from concourse.bass_utils import run_bass_kernel_spmd

    v = {n: np.asarray(inputs[n]) for n in INPUTS}
    v = {n: a if n == "final_norm_w_2" else a[0] for n, a in v.items()}
    ada = [v[n].reshape(KC, P, 2, ADA_COLS).transpose(2, 0, 1, 3) for n in ("w_ada_mix_2", "w_ada_ffn_2")]
    arrays = {
        "x_t": np.ascontiguousarray(v["x"].T.reshape(KC, P, S).transpose(1, 0, 2)),
        "weights": weight_stream(v),
        "cols": columns(v),
        "pool_w": np.ascontiguousarray(v["pool_w"].transpose(1, 0, 2)),
        "ada": np.ascontiguousarray(np.concatenate(ada).reshape(4 * ADA_PIECES, P, ADA_COLS)),
    }
    assert arrays["weights"].shape == (P_END, P, PANEL) and arrays["cols"].shape == (P, NCOL)
    nc = bacc.Bacc("TRN2", target_bir_lowering=False, num_devices=1, dynamic_dma_scratch_size=2048)
    aps = [nc.dram_tensor(n + "_dram", a.shape, F32, kind="ExternalInput").ap() for n, a in arrays.items()]
    out = nc.dram_tensor("out_t_dram", (P, KC, S), F32, kind="ExternalOutput").ap()
    build(nc, *aps, out)
    r = run_bass_kernel_spmd(nc, [{n + "_dram": a for n, a in arrays.items()}], core_ids=[0])
    return r.results[0]["out_t_dram"].transpose(1, 0, 2).reshape(D, S).T[None]
```
